# Optimizing a Trainium2 kernel written in Bass

```python
import math
import jax, jax.numpy as jnp
from jax import lax
import numpy as np

D_MODEL = 2048
BATCH = 1
SEQ = 256
DEPTH = 1

GLA_HEADS = 4
GLA_HEAD_K = D_MODEL // (2 * GLA_HEADS)
GLA_HEAD_V = D_MODEL // GLA_HEADS
GLA_GATE_RANK = 16
GLA_GATE_NORMALIZER = 16.0
GLA_CHUNK = 64
GLA_QK_W = GLA_HEADS * GLA_HEAD_K
GLA_V_W = GLA_HEADS * GLA_HEAD_V

DSA_HEADS = 16
DSA_HEAD_DIM = D_MODEL // DSA_HEADS
DSA_LATENT = 256
DSA_TOPK = 256
DSA_Q_BLOCK = 128
IDX_HEADS = 16
IDX_DIM = 64
DSA_Q_W = DSA_HEADS * DSA_LATENT

REL_BUCKETS = 32
REL_MAX_DIST = 128

D_FF = 4 * D_MODEL
N_MOD = 6
EPS = 1e-6

IN_SIZES = (GLA_QK_W, GLA_QK_W, GLA_V_W, GLA_GATE_RANK, GLA_V_W,
            DSA_Q_W, DSA_LATENT, IDX_HEADS * IDX_DIM, IDX_DIM, IDX_HEADS,
            D_MODEL, D_MODEL)
N_IN = sum(IN_SIZES)

kernel_name = "hybrid_gla_dsa_gated_parallel"

def rms_norm(x, g):
    xf = x.astype(jnp.float32)
    y = xf * lax.rsqrt(jnp.mean(xf * xf, axis=-1, keepdims=True) + EPS)
    return (y * g.astype(jnp.float32)).astype(x.dtype)

def split_cols(z):
    parts, off = [], 0
    for s in IN_SIZES:
        parts.append(z[..., off:off + s])
        off += s
    return parts

def rel_bucket(dist):
    max_exact = REL_BUCKETS // 2
    d = jnp.maximum(dist, 0)
    df = jnp.maximum(d, 1).astype(jnp.float32)
    large = max_exact + (jnp.log(df / max_exact) / math.log(REL_MAX_DIST / max_exact)
                         * (REL_BUCKETS - max_exact)).astype(jnp.int32)
    large = jnp.minimum(large, REL_BUCKETS - 1)
    return jnp.where(d < max_exact, d, large)

def gla_branch(q, k, v, a_low, r, w_a2, b_a, g_norm):
    B, S, _ = q.shape
    H, dk, dv, C = GLA_HEADS, GLA_HEAD_K, GLA_HEAD_V, GLA_CHUNK
    n = S // C
    f32 = jnp.float32
    qf = q.reshape(B, S, H, dk).astype(f32) * (dk ** -0.5)
    kf = k.reshape(B, S, H, dk).astype(f32)
    vf = v.reshape(B, S, H, dv).astype(f32)
    g = jax.nn.log_sigmoid((a_low @ w_a2 + b_a).astype(f32)) / GLA_GATE_NORMALIZER
    g = g.reshape(B, S, H, dk)

    def to_chunks(t):
        return t.reshape(B, n, C, H, t.shape[-1]).transpose(1, 0, 3, 2, 4)

    tril = jnp.tril(jnp.ones((C, C), dtype=bool))

    def step(state, inp):
        qc, kc, vc, gc = inp
        b = jnp.cumsum(gc, axis=2)
        o_inter = jnp.einsum('bhcd,bhde->bhce', qc * jnp.exp(b), state)
        diff = b[:, :, :, None, :] - b[:, :, None, :, :]
        decay = jnp.exp(jnp.where(tril[:, :, None], diff, -jnp.inf))
        attn = jnp.sum(qc[:, :, :, None, :] * kc[:, :, None, :, :] * decay, axis=-1)
        o = o_inter + jnp.einsum('bhij,bhje->bhie', attn, vc)
        b_last = b[:, :, -1:, :]
        state = (jnp.exp(b_last[:, :, 0, :])[..., None] * state
                 + jnp.einsum('bhcd,bhce->bhde', kc * jnp.exp(b_last - b), vc))
        return state, o

    state0 = jnp.zeros((B, H, dk, dv), f32)
    _, o = lax.scan(step, state0, (to_chunks(qf), to_chunks(kf), to_chunks(vf), to_chunks(g)))
    o = o.transpose(1, 0, 3, 2, 4).reshape(B, S, H, dv)
    o = o * lax.rsqrt(jnp.mean(o * o, axis=-1, keepdims=True) + EPS) * g_norm.astype(f32)
    o = o.reshape(B, S, GLA_V_W) * jax.nn.silu(r.astype(f32))
    return o.astype(q.dtype)

def dsa_branch(q_lat, kv_lat, iq, ik, iw, kv_g, w_uv, rel_bias):
    B, S, _ = q_lat.shape
    k_sel = min(DSA_TOPK, S // 4)
    nb = S // DSA_Q_BLOCK
    f32 = jnp.float32
    kv = rms_norm(kv_lat, kv_g)
    q4 = q_lat.reshape(B, S, DSA_HEADS, DSA_LATENT)
    iq4 = iq.reshape(B, S, IDX_HEADS, IDX_DIM)
    kpos = jnp.arange(S, dtype=jnp.int32)

    def blocks(t):
        return t.reshape(B, nb, DSA_Q_BLOCK, *t.shape[2:]).swapaxes(0, 1)

    def one_block(inp):
        qb, iqb, iwb, start = inp
        qpos = start + jnp.arange(DSA_Q_BLOCK, dtype=jnp.int32)
        idx_logits = jax.nn.relu(jnp.einsum('bqhd,bkd->bqhk', iqb, ik).astype(f32) * (IDX_DIM ** -0.5))
        score = jnp.einsum('bqh,bqhk->bqk', iwb.astype(f32) * (IDX_HEADS ** -0.5), idx_logits)
        score = jnp.where(kpos[None, None, :] <= qpos[None, :, None], score, -jnp.inf)
        _, idx = lax.top_k(score, k_sel)
        sel = jax.vmap(lambda kvb, ib: kvb[ib])(kv, idx)
        rel = qpos[None, :, None] - idx
        bias = jnp.moveaxis(rel_bias[rel_bucket(rel)], -1, 2)
        logits = (jnp.einsum('bqhl,bqkl->bqhk', qb, sel).astype(f32) * (DSA_LATENT ** -0.5)
                  + bias.astype(f32))
        valid = (rel >= 0)[:, :, None, :]
        probs = jax.nn.softmax(jnp.where(valid, logits, -jnp.inf), axis=-1).astype(sel.dtype)
        o_lat = jnp.einsum('bqhk,bqkl->bqhl', probs, sel)
        o = jnp.einsum('bqhl,hld->bqhd', o_lat, w_uv)
        return o.reshape(B, DSA_Q_BLOCK, DSA_HEADS * DSA_HEAD_DIM)

    starts = jnp.arange(nb, dtype=jnp.int32) * DSA_Q_BLOCK
    out = lax.map(one_block, (blocks(q4), blocks(iq4), blocks(iw), starts))
    return out.swapaxes(0, 1).reshape(B, S, DSA_HEADS * DSA_HEAD_DIM)

def setup_inputs(seed: int = 0) -> dict:
    key = jax.random.key(seed)
    ks = jax.random.split(key, 17)
    f32 = jnp.float32
    D = D_MODEL
    nrm = lambda k, shape, s: jax.random.normal(k, shape, f32) * s
    return {
        "x": nrm(ks[0], (BATCH, SEQ, D), 1.0),
        "c": nrm(ks[1], (BATCH, D), 1.0),
        "w_mod": nrm(ks[2], (DEPTH, D, N_MOD * D), 0.5 * D ** -0.5),
        "b_mod": nrm(ks[3], (DEPTH, N_MOD * D), 0.02),
        "norm1_g": 1.0 + nrm(ks[4], (DEPTH, D), 0.02),
        "w_in": nrm(ks[5], (DEPTH, D, N_IN), D ** -0.5),
        "w_gate_up": nrm(ks[6], (DEPTH, GLA_GATE_RANK, GLA_QK_W), GLA_GATE_RANK ** -0.5),
        "b_gate": nrm(ks[7], (DEPTH, GLA_QK_W), 0.1),
        "gla_norm_g": 1.0 + nrm(ks[8], (DEPTH, GLA_HEAD_V), 0.02),
        "kv_norm_g": 1.0 + nrm(ks[9], (DEPTH, DSA_LATENT), 0.02),
        "w_uv": nrm(ks[10], (DEPTH, DSA_HEADS, DSA_LATENT, DSA_HEAD_DIM), DSA_LATENT ** -0.5),
        "w_out": nrm(ks[11], (DEPTH, D, D), D ** -0.5),
        "norm2_g": 1.0 + nrm(ks[12], (DEPTH, D), 0.02),
        "w_ff1": nrm(ks[13], (DEPTH, D, D_FF), D ** -0.5),
        "w_ff2": nrm(ks[14], (DEPTH, D_FF, D), D_FF ** -0.5),
        "rel_bias": nrm(ks[15], (REL_BUCKETS, DSA_HEADS), 0.5),
        "final_g": 1.0 + nrm(ks[16], (D,), 0.02),
    }

def reference(x, c, w_mod, b_mod, norm1_g, w_in, w_gate_up, b_gate, gla_norm_g, kv_norm_g,
              w_uv, w_out, norm2_g, w_ff1, w_ff2, rel_bias, final_g):
    c_act = jax.nn.silu(c)
    for l in range(DEPTH):
        mod = c_act @ w_mod[l] + b_mod[l]
        sh1, sc1, gt1, sh2, sc2, gt2 = [m[:, None, :] for m in jnp.split(mod, N_MOD, axis=-1)]

        h = rms_norm(x, norm1_g[l]) * (1.0 + sc1) + sh1
        (q_g, k_g, v_g, a_low, r_g, q_lat, kv_lat, iq, ik, iw,
         g_gla, g_dsa) = split_cols(h @ w_in[l])
        y_gla = gla_branch(q_g, k_g, v_g, a_low, r_g, w_gate_up[l], b_gate[l], gla_norm_g[l])
        y_dsa = dsa_branch(q_lat, kv_lat, iq, ik, iw, kv_norm_g[l], w_uv[l], rel_bias)
        merged = jax.nn.sigmoid(g_gla) * y_gla + jax.nn.sigmoid(g_dsa) * y_dsa
        x = x + gt1 * (merged @ w_out[l])

        h = rms_norm(x, norm2_g[l]) * (1.0 + sc2) + sh2
        u = jnp.square(jax.nn.relu(h @ w_ff1[l]))
        x = x + gt2 * (u @ w_ff2[l])
    return rms_norm(x, final_g)


_drawn_inputs = setup_inputs


def setup_inputs(seed=0):
    import zlib

    import numpy as np

    out = dict(_drawn_inputs(seed))
    spreads = {}
    factors = {'norm1_g': 8.0,
     'b_gate': 8.0,
     'gla_norm_g': 21.529,
     'kv_norm_g': 46.727,
     'norm2_g': 18.574,
     'rel_bias': 18.617,
     'final_g': 24.891}
    for name, (base, spread) in spreads.items():
        noise = np.random.default_rng([zlib.crc32(name.encode()), seed]).standard_normal(out[name].shape)
        drawn = base * np.exp(spread * noise) if base else spread * noise
        out[name] = __import__('jax').numpy.asarray(drawn.astype(out[name].dtype))
    for name, factor in factors.items():
        out[name] = (out[name] * factor).astype(out[name].dtype)
    return out
```

```python
from contextlib import ExitStack

import numpy as np

import concourse.bass as bass
from concourse import mybir

F32 = mybir.dt.float32
F32R = mybir.dt.float32r
U8 = mybir.dt.uint8
ACT = mybir.ActivationFunctionType
ALU = mybir.AluOpType
AX_X = mybir.AxisListType.X

P = 128
D = 2048
S = 256
T = S // P
KT = D // P
W = 512
PIECES = 8
PK = KT // PIECES
RING = 4
AHEAD = RING - 1
H_GLA, DK, DV = 4, 256, 512
RANK = 16
H_DSA, LAT, HD = 16, 256, 128
H_IDX, D_IDX = 16, 64
TOPK = min(256, S // 4)
BUCKETS, MAX_DIST = 32, 128
N_MOD = 6
FF = 4 * D
EPS = 1e-6
MW = 1024
MODS = N_MOD * D // MW
MOD_FIRST = 2 * D // MW
MB = MW // P
KEYS = P + S

SIZES = (H_GLA * DK, H_GLA * DK, H_GLA * DV, RANK, H_GLA * DV, H_DSA * LAT, LAT,
         H_IDX * D_IDX, D_IDX, H_IDX, D, D)
OFF = [sum(SIZES[:n]) for n in range(len(SIZES) + 1)]
(O_Q, O_K, O_V, O_A, O_R, O_QLAT, O_KV, O_IQ, O_IK, O_IW, O_GG, O_GD, N_IN) = OFF
MISC = LAT + D_IDX + H_IDX + RANK

FILL = -3.0e38
TAKEN = -3.4e38
BETWEEN = -3.2e38
NEG = -1.0e30

C_IQ, C_Q, C_K, C_V, C_QL, C_RG, C_GD, C_WO, C_FF = 1, 3, 5, 7, 11, 19, 27, 31, 35
CHUNKS = C_FF + 32
LEVELS = [1, 2, 4, 8, 16, 32, 64]

PLAN = [(0, 16, 1), (16, 2, 2), (20, 2, 4), (28, 8, 1), (36, 8, 3), (60, 7, 1)]


def group_slot(c):
    return (c - C_FF) % 8


def pa_uses(c):
    if c in (0, C_FF):
        return 4
    if c == 1:
        return 2
    if 2 <= c <= 11:
        return 1 + (c == 6)
    if 12 <= c <= 15:
        return 3
    if 16 <= c <= 19:
        return 2 + c % 2
    if 20 <= c <= 27:
        return c % 2
    if 28 <= c <= 31:
        return 1 + (c == 29)
    if c > C_FF:
        return 1 if 1 <= group_slot(c) <= 4 else 0
    return 0


def pb_uses(c):
    if c in (0, C_FF):
        return 4
    if c == 1:
        return 1
    if c in (2, 3):
        return 4
    if c in (5, 6):
        return 2
    if c == 8:
        return 2
    if 9 <= c <= 11:
        return 1
    if 12 <= c <= 19:
        return 2
    if c in (29, 31):
        return 4
    return 0


def mod_ops(c):
    return (9 if first_of_mod(c) else 7) if c in (5, 6) or 16 <= c <= 29 else 0


def first_of_mod(c):
    return c == 5 or (c != 6 and c % 2 == 0)


def mod_ends(c):
    return mod_ops(c) == 7


def prefix(f, start=0):
    out = [start]
    for c in range(CHUNKS + 8):
        out.append(out[-1] + f(c))
    return out


SETUP_PA = 1
SETUP_PB = 1 + MOD_FIRST
PA_AT, PB_AT = prefix(pa_uses, SETUP_PA), prefix(pb_uses, SETUP_PB)
MOD_AT = prefix(mod_ops, MOD_FIRST * KT)
FF1_AT = prefix(lambda c: int(c > C_FF and 1 <= group_slot(c) <= 4))


class Pos:

    def __init__(self, first, i=0, stride=0):
        self.first, self.i, self.stride = first, i, stride
        self.n = self.at(range(CHUNKS + 16))

    def at(self, table):
        per = table[self.first + self.stride] - table[self.first]
        return table[self.first] + self.i * per if per else table[self.first]


def run_plan(eng, chunk):
    for first, body, times in PLAN:
        if times == 1:
            for j in range(body):
                chunk(Pos(first + j))
        else:
            with eng.Fori(0, times) as i:
                for j in range(body):
                    chunk(Pos(first + j, i, body))


def buckets_of_distance():
    exact = BUCKETS // 2
    d = np.arange(S)
    far = np.log(np.maximum(d, 1) / exact) / np.log(MAX_DIST / exact) * (BUCKETS - exact)
    large = np.minimum(exact + np.floor(far + 1e-9).astype(int), BUCKETS - 1)
    return np.where(d < exact, d, large)


def shape_constants():
    ident = np.eye(P, dtype=np.float32)
    onehot = np.zeros((BUCKETS, KEYS), np.float32)
    bucket = buckets_of_distance()
    for j in range(KEYS):
        onehot[bucket[max(S - 1 - j, 0)], j] = 1
    j, i = np.arange(P)[:, None], np.arange(P)[None, :]
    masks = [i == j]
    for s in LEVELS:
        masks.append((j // (2 * s) == i // (2 * s)) & (j % (2 * s) < s) & (i % (2 * s) >= s))
    return ident, onehot, np.stack(masks, 1).astype(np.uint8)


def build_layer(nc, x, c, w_mod, b_mod, norm1_g, w_in, w_gate_up, b_gate, gla_norm_g, kv_norm_g,
                w_uv, w_out, norm2_g, w_ff1, w_ff2, rel_bias, final_g, out):
    ident_c, onehot_c, masks_c = shape_constants()
    ident_d = nc.inline_tensor(ident_c, "identity").ap()
    onehot_d = nc.inline_tensor(onehot_c, "bucket_onehot").ap()
    masks_d = nc.inline_tensor(masks_c.reshape(P, -1), "level_masks").ap()
    bias_rows_h = nc.dram_tensor("bias_rows", (H_DSA, P, KEYS), F32)
    bias_rows = bias_rows_h.ap()

    x_v = x.rearrange("b (t p) d -> p (b t) d", p=P)
    out_v = out.rearrange("b (t p) d -> p (b t) d", p=P)
    w_in_v = w_in.rearrange("l (k p) n -> p (l k) n", p=P)
    w_out_v = w_out.rearrange("l (k p) n -> p (l k) n", p=P)
    w_ff1_v = w_ff1.rearrange("l (k p) n -> p (l k) n", p=P)
    w_ff2_v = w_ff2.rearrange("l (k p) n -> p (l k) n", p=P)
    w_mod_v = w_mod.rearrange("l (p k) n -> p (l k) n", p=P)
    c_v = c.rearrange("b (p k) -> p (b k)", p=P)
    w_uv_v = w_uv.rearrange("l h (a p) d -> p a (l h) d", p=P)

    with ExitStack() as ctx:
        def sem(name):
            return ctx.enter_context(nc.semaphore(name))

        base = (nc.sbuf_base + 63) // 64 * 64
        KIB = 1024
        at = [base]
        used = []

        def place(name, shape, dt=F32, offset=None):
            size = mybir.dt.size(dt)
            for n in shape[1:]:
                size *= n
            if offset is None:
                offset = at[0]
                at[0] += (size + 31) // 32 * 32
            used.append(offset + size)
            return nc.alloc_sbuf_tensor_at(name, shape, dt, offset=offset)

        def region(kib):
            start = at[0]
            at[0] += kib * KIB
            return start

        h_hi = place("h_hi", [P, KT, S], F32R)
        h_lo = place("h_lo", [P, KT, S], F32R)
        w_raw = place("w_raw", [P, RING, PK, W])
        w_hi = place("w_hi", [P, RING, PK, W], F32R)
        w_lo = place("w_lo", [P, RING, PK, W], F32R)
        m_raw = place("m_raw", [P, RING, MW])
        z = place("z", [P, T, W])
        full = place("full", [P, 2, 2 * S], F32, offset=at[0] - 4 * KIB)

        r_sum = region(8)
        m_sum = place("m_sum", [P, 2, MW], F32, r_sum)
        att = place("att", [P, H_GLA, T, P], F32, r_sum)
        att_far = place("att_far", [P, H_GLA, P], F32, r_sum + 4 * KIB)

        r_act = region(32)
        m_hi = place("m_hi", [P, KT, S], F32R, r_act)
        m_lo = place("m_lo", [P, KT, S], F32R, r_act + 16 * KIB)
        u_hi = place("u_hi", [P, KT, S], F32R, r_act)
        u_lo = place("u_lo", [P, KT, S], F32R, r_act + 16 * KIB)
        vals = place("vals", [P, T, H_DSA * HD], F32, r_act)
        gate_up = place("gate_up", [RANK, H_GLA * DK], F32, r_act)
        onehot = place("onehot", [BUCKETS, KEYS], F32, r_act + 4 * KIB)
        table = place("table", [BUCKETS, H_DSA], F32, r_act + 6 * KIB)
        rows = place("rows", [H_DSA, KEYS], F32, r_act + 7 * KIB)
        kv_g = place("kv_g", [P, LAT], F32, r_act + 9 * KIB)
        vec_rows = place("vec_rows", [P, P], F32, r_act + 10 * KIB)
        gate_rows = place("gate_rows", [H_GLA * DK // P, P], F32, r_act + 11 * KIB)
        bias = place("bias", [P, H_DSA, S], F32, r_act + 16 * KIB)
        gate_x = place("gate_x", [P, 8, S], F32, r_act + 16 * KIB)
        gate_e = place("gate_e", [P, 8, S], F32, r_act + 24 * KIB)
        level = [place(f"level{n}", [P, 8, S], F32, r_act + (16 + 8 * n) * KIB) for n in (0, 1)]

        r_x = region(16)
        xs = place("xs", [P, T, D], F32, r_x)
        y_dsa = place("y_dsa", [P, T, D], F32, r_x)
        score = place("score", [P, KEYS], F32, r_x)
        left = [place(f"left{n}", [P, KEYS], F32, r_x + 1536 * (n + 1)) for n in (0, 1)]
        relu = place("relu", [P, 2, KEYS], F32, r_x + 1536 * 3)
        ik2 = place("ik2", [P, T, 2 * D_IDX], F32, r_x + 1536 * 5)
        kvn = place("kvn", [P, T, LAT], F32, r_x + 1536 * 5 + KIB)
        top8 = place("top8", [P, T, 8], F32, r_x + 1536 * 5 + 3 * KIB)

        r_v = region(16)
        normed = place("normed", [P, T, D], F32, r_v)
        wuv = place("wuv", [P, 2, H_DSA, HD], F32, r_v)
        v = place("v", [P, T, D], F32, r_v)

        r_g = region(24)
        qt = place("qt", [P, 8, S], F32, r_g)
        kt = place("kt", [P, 8, S], F32, r_g + 8 * KIB)
        cum = place("cum", [P, 8, S], F32, r_g + 16 * KIB)
        iqt = place("iqt", [P, 8, S], F32, r_g + 8 * KIB)
        q_lat = place("q_lat", [P, 4, S], F32, r_g)
        logit = place("logit", [P, 2, KEYS], F32, r_g + 4 * KIB)
        prob_t = place("prob_t", [P, 2, KEYS], F32, r_g + 7 * KIB)
        junk = place("junk", [P, T, W], F32, r_g + 10 * KIB)
        gate1_row = place("gate1_row", [P, D], F32, r_g)
        gate2_row = place("gate2_row", [P, D], F32, r_g + 8 * KIB)
        diag = place("diag", [P, 4, P], F32, r_g + 16 * KIB)
        final_row = place("final_row", [P, D], F32, r_g + 16 * KIB)

        ident = place("ident", [P, P])
        ones = place("ones", [P, P])
        masks = place("masks", [P, 1 + len(LEVELS), P], U8)
        gla_g = place("gla_g", [P, DV])
        kvt = place("kvt", [P, 2, S])
        ikt = place("ikt", [P, S])
        a_t = place("a_t", [RANK, S])
        mask = place("mask", [P, KEYS])
        vec_cols = place("vec_cols", [P, P])
        gate_cols = place("gate_cols", [P, 8])
        mod_cols = place("mod_cols", [P, N_MOD * KT])
        h_scale = place("h_scale", [P, KT])
        c_act = place("c_act", [P, KT])
        c_tmp = place("c_tmp", [P, 3, KT])
        iw = place("iw", [P, T, H_IDX])
        st = place("st", [P, 64])
        assert max(used + at) <= nc.sbuf_usable_end, (max(used + at), nc.sbuf_usable_end)
        ssq_x, rin_x = st[:, 0:T], st[:, 2:2 + T]
        ssq_kv, rin_kv = st[:, 4:4 + T], st[:, 6:6 + T]
        neg_top = st[:, 12:16]
        total, inv_total = st[:, 16:20], st[:, 20:24]
        ssq_o, rin_o = st[:, 24:24 + T], st[:, 26:26 + T]
        root, eps = st[:, 28:28 + T], st[:, 36:37]

        acc = ctx.enter_context(nc.psum_tensor("acc", [P, 2, T, W], F32))
        pa = ctx.enter_context(nc.psum_tensor("pa", [P, 2, W], F32))
        pb = ctx.enter_context(nc.psum_tensor("pb", [P, 2, W], F32))

        raw_landed = [sem(f"raw_landed{n}") for n in range(RING)]
        hi_ready = sem("hi_ready")
        lo_ready = sem("lo_ready")
        pe_used = sem("pe_used")
        pa_full, pa_read = sem("pa_full"), sem("pa_read")
        pb_full, pb_read = sem("pb_full"), sem("pb_read")
        z_full = sem("z_full")
        mod_landed = [sem(f"mod_landed{n}") for n in range(RING)]
        mod_late = [sem(f"mod_late{n}") for n in range(RING)]
        mod_done = sem("mod_done")
        x_landed, c_landed, consts_landed = sem("x_landed"), sem("c_landed"), sem("consts_landed")
        ones_ready = sem("ones_ready")
        act_setup, dve_setup = sem("act_setup"), sem("dve_setup")
        normed_ready = sem("normed_ready")
        x_ssq, root_ready = sem("x_ssq"), sem("root_ready")
        scale_ready = sem("scale_ready")
        h_hi_ready, h_lo_ready = sem("h_hi_ready"), sem("h_lo_ready")
        rows_stored, bias_landed = sem("rows_stored"), sem("bias_landed")
        kv_ssq, misc_ready, kv_chain = sem("kv_ssq"), sem("misc_ready"), sem("kv_chain")
        gate_chain, gate_l_ready = sem("gate_chain"), sem("gate_l_ready")
        decay_ready = sem("decay_ready")
        score_zero, score_steps = sem("score_zero"), sem("score_steps")
        score_masked, topk_steps, mask_ready = sem("score_masked"), sem("topk_steps"), sem("mask_ready")
        wuv_landed = sem("wuv_landed")
        v_ready = sem("v_ready")
        level_diff, level_exp, level_ready = sem("level_diff"), sem("level_exp"), sem("level_ready")
        att_zero = sem("att_zero")
        dsa_steps, prob_ready, inv_ready = sem("dsa_steps"), sem("prob_ready"), sem("inv_ready")
        o_ssq, o_steps = sem("o_ssq"), sem("o_steps")
        gate_steps, merge_steps = sem("gate_steps"), sem("merge_steps")
        split_hi = sem("split_hi")
        diag_ready = sem("diag_ready")
        final_row_landed = sem("final_row_landed")
        x_again = sem("x_again")
        res_steps = sem("res_steps")
        norm_steps = sem("norm_steps")
        square_ready = sem("square_ready")
        out_ready, out_stored = sem("out_ready"), sem("out_stored")

        def raw_count(pos, p):
            if isinstance(pos.n, int) and pos.n == 0:
                return 48 * (p // RING + 1)
            return 96 + 16 * (2 * (pos.n - 1) + p // RING + 1)

        def later(pos, p):
            if p + AHEAD < PIECES:
                return pos, p + AHEAD
            return Pos(pos.first + 1, pos.i, pos.stride), p + AHEAD - PIECES

        def width(pos):
            return MISC if pos.first == 0 else W

        def is_gt_stage(c):
            return C_GD + 1 <= c <= C_WO

        block = ctx.enter_context(nc.Block())

        @block.sync
        def _(sp):
            sp.dma_start(c_act[:, :], c_v).then_inc(c_landed, 16)
            for t in range(T):
                sp.dma_start(xs[:, t, :], x_v[:, t, :]).then_inc(x_landed, 16)
            for m in range(MOD_FIRST):
                for k in range(KT):
                    n = m * KT + k
                    if n >= RING:
                        sp.wait_ge(mod_done, n - RING + 1)
                    sp.dma_start(m_raw[:, n % RING, :], w_mod_v[:, k, m * MW:(m + 1) * MW]).then_inc(
                        mod_landed[n % RING], 16)

            def load(n, p, view, col, row=0):
                if not (isinstance(n, int) and n == 0 and p < RING):
                    sp.wait_ge(lo_ready, PIECES * n + p - RING + 1)
                k = row + p * PK
                sp.dma_start(w_raw[:, p % RING, :, :], view[:, bass.ds(k, PK), bass.ds(col, W)]).then_inc(
                    raw_landed[p % RING], 16)

            for p in range(PIECES):
                if p >= RING:
                    sp.wait_ge(lo_ready, p - RING + 1)
                for to, col, n in ((0, O_KV, LAT), (LAT, O_IK, D_IDX + H_IDX), (LAT + D_IDX + H_IDX, O_A, RANK)):
                    sp.dma_start(w_raw[:, p % RING, :, to:to + n],
                                 w_in_v[:, p * PK:(p + 1) * PK, col:col + n]).then_inc(raw_landed[p % RING], 16)
            for first, count, col in ((C_IQ, 2, O_IQ), (C_Q, 4, O_Q), (C_V, 4, O_V), (C_QL, 8, O_QLAT)):
                with sp.Fori(0, count) as i:
                    for p in range(PIECES):
                        load(i + first, p, w_in_v, i * W + col)
            with sp.Fori(0, H_GLA) as i:
                for p in range(PIECES):
                    load(i * 2 + C_RG, p, w_in_v, i * W + O_R)
                for p in range(PIECES):
                    load(i * 2 + (C_RG + 1), p, w_in_v, i * W + O_GG)
            with sp.Fori(0, D // W) as i:
                for p in range(PIECES):
                    load(i + C_GD, p, w_in_v, i * W + O_GD)
            with sp.Fori(0, D // W) as i:
                for p in range(PIECES):
                    load(i + C_WO, p, w_out_v, i * W)
            with sp.Fori(0, FF // D) as g:
                for j in range(D // W):
                    for p in range(PIECES):
                        load(g * 8 + (C_FF + j), p, w_ff1_v, g * D + j * W)
                for j in range(D // W):
                    for p in range(PIECES):
                        load(g * 8 + (C_FF + 4 + j), p, w_ff2_v, j * W, g * KT)
            for t in range(T):
                sp.wait_ge(out_ready, t + 1)
                sp.dma_start(out_v[:, t, :], normed[:, t, :]).then_inc(out_stored, 16)
            sp.wait_ge(out_stored, 16 * T)
            sp.wait_ge(rows_stored, 16)

        @block.gpsimd
        def _(pool):
            pool.wait_ge(pa_full, PA_AT[0] + 4)
            pool.wait_ge(pb_full, PB_AT[0] + 4)
            for a in range(2):
                pool.dma_start(wuv[:, a, :, :], w_uv_v[:, a, :, :]).then_inc(wuv_landed, 16)

            pool.dma_start(bias_rows, rows[:, :].rearrange("h (a j) -> h a j", a=1).to_broadcast(
                [H_DSA, P, KEYS])).then_inc(rows_stored, 16)

            def load_mod(n, k, col):
                pool.wait_ge(mod_done, n - RING + 1)
                pool.dma_start(m_raw[:, k % RING, :], w_mod_v[:, k, bass.ds(col, MW)]).then_inc(
                    mod_late[k % RING], 16)

            for k in range(RING):
                load_mod(MOD_FIRST * KT + k, k, MOD_FIRST * MW)
            pool.wait_ge(score_steps, 4 * H_IDX // 2)
            for t, (a, b) in enumerate(((0, P), (P, KEYS))):
                nc.gpsimd.affine_select(out=score[:, a:b], in_=score[:, a:b], compare_op=ALU.is_ge, fill=FILL,
                                        base=t * P, pattern=[[-1, b - a]], channel_multiplier=1).then_inc(
                                            score_masked, 1)
            for k in range(RING, KT):
                load_mod(MOD_FIRST * KT + k, k, MOD_FIRST * MW)
            pool.wait_ge(topk_steps, 4 * (TOPK // 8) + 1)
            for t, (a, b) in enumerate(((0, P), (P, KEYS))):
                nc.gpsimd.affine_select(out=mask[:, a:b], in_=mask[:, a:b], compare_op=ALU.is_ge, fill=NEG,
                                        base=t * P, pattern=[[-1, b - a]], channel_multiplier=1).then_inc(
                                            mask_ready, 1)
            pool.wait_ge(rows_stored, 16)
            pool.wait_ge(pa_full, PA_AT[12])
            pool.wait_ge(pb_full, PB_AT[12])
            for half in range(2):
                src = bass.AP(tensor=bias_rows_h, offset=P - 1 + half * 8 * P * KEYS,
                              ap=[[KEYS - 1, P], [P * KEYS, 8], [1, S]])
                pool.dma_start(bias[:, 8 * half:8 * half + 8, :], src).then_inc(bias_landed, 16)
            with pool.Fori(0, MODS - MOD_FIRST - 1) as i:
                for k in range(KT):
                    load_mod(i * KT + ((MOD_FIRST + 1) * KT + k), k, i * MW + (MOD_FIRST + 1) * MW)
            pool.wait_ge(merge_steps, 2 * (D // W))
            for t in range(T):
                pool.dma_start(xs[:, t, :], x_v[:, t, :]).then_inc(x_again, 16)
            pool.wait_ge(pb_full, PB_AT[32])
            pool.dma_start(final_row[:, :], final_g.rearrange("(a n) -> a n", a=1).to_broadcast([P, D])).then_inc(
                final_row_landed, 16)

        @block.scalar
        def _(act):
            def high(pos, p):
                s = p % RING
                act.wait_ge(raw_landed[s], raw_count(pos, p))
                if not (isinstance(pos.n, int) and pos.n * PIECES + p < RING):
                    act.wait_ge(pe_used, PIECES * pos.n + (p - RING + 1))
                n = width(pos)
                nc.scalar.activation(w_hi[:, s, :, 0:n], w_raw[:, s, :, 0:n], ACT.Copy).then_inc(hi_ready, 1)

            mod_rows, g_rows = N_MOD * KT, KT
            for to, of in (
                (ident[:, :], ident_d), (masks[:, :, :].rearrange("p a b -> p (a b)"), masks_d),
                (onehot[:, :], onehot_d), (table[:, :], rel_bias),
                (vec_rows[0:mod_rows, :], b_mod.rearrange("l (a p) -> (l a) p", p=P)),
                (vec_rows[mod_rows:mod_rows + g_rows, :], norm1_g.rearrange("l (a p) -> (l a) p", p=P)),
                (vec_rows[mod_rows + g_rows:P, :], norm2_g.rearrange("l (a p) -> (l a) p", p=P)),
                (gate_rows[:, :], b_gate.rearrange("l (a p) -> (l a) p", p=P)),
                (gate_up[:, :], w_gate_up.rearrange("l r n -> (l r) n")),
                (kv_g[:, :], kv_norm_g.to_broadcast([P, LAT])),
                (gla_g[:, :], gla_norm_g.to_broadcast([P, DV])),
            ):
                act.dma_start(to, of).then_inc(consts_landed, 16)
            act.wait_ge(c_landed, 16)
            nc.scalar.activation(c_tmp[:, 0, :], c_act[:, :], ACT.Exp, scale=-1.0).then_inc(act_setup, 1)

            def take_root(of, n, ready, count):
                act.wait_ge(ready, count)
                nc.scalar.activation(root, of, ACT.Sqrt, bias=eps, scale=1.0 / n).then_inc(root_ready, 1)

            def sum_squares(k):
                for t in range(T):
                    nc.scalar.activation(normed[:, t, :], xs[:, t, :], ACT.Square,
                                         accum_out=ssq_x[:, t:t + 1]).then_inc(x_ssq, 1)
                take_root(ssq_x, D, x_ssq, T * (k + 1))

            def normalise(k):
                act.wait_ge(norm_steps, ROOT_STEPS * (k + 1))
                nc.scalar.activation(normed[:, 1, :], xs[:, 1, :], ACT.Copy,
                                     scale=rin_x[:, 1:2]).then_inc(normed_ready, 1)

            def h_high(k, q):
                reads, at_ = (pa_read, PA_AT) if q % 2 == 0 else (pb_read, PB_AT)
                act.wait_ge(reads, at_[(0, C_FF)[k]] + q // 2 + 1)
                nc.scalar.activation(h_hi[:, 2 * q:2 * q + 2, :].rearrange("p a s -> p (a s)"),
                                     full[:, q % 2, :], ACT.Copy).then_inc(h_hi_ready, 1)

            def take(pos, func, to=None):
                prev = pos.n - 1
                act.wait_ge(pe_used, PIECES * prev + PIECES)
                if pos.first in (1, C_FF + 1):
                    act.wait_ge(h_lo_ready, 8 * (1 + int(pos.first > 1)))
                n = width(Pos(pos.first - 1))
                if to is None:
                    to, done = z[:, :, 0:n], z_full
                    if 20 <= pos.first <= 28:
                        act.wait_ge(gate_steps, pos.at(GATE_AT))
                    if pos.first > C_FF:
                        act.wait_ge(res_steps, pos.at(RES_AT) * 2)
                else:
                    done = v_ready
                a = acc[:, (pos.first - 1) % 2, :, 0:n]
                return nc.scalar.activation(to, a, func), done

            def copy_pa(to, scale=1.0):
                return nc.scalar.activation(to.rearrange("p a s -> p (a s)"),
                                            pa[:, :, :].rearrange("p a w -> p (a w)"), ACT.Copy, scale=scale)

            def chunk(pos):
                c = pos.first
                for p in range(PIECES):
                    if p == 0 and (1 <= c <= 7 or 12 <= c <= 19 or is_gt_stage(c)
                                   or 20 <= c <= 27 or (c > C_FF and 1 <= group_slot(c) <= 4)):
                        func = (ACT.Sigmoid if 20 <= c <= 31 else ACT.Relu if c > C_FF else ACT.Copy)
                        ins, done = take(pos, func)
                        ins.then_inc(done, 1)
                    if p == 0 and 8 <= c <= 11:
                        ins, done = take(pos, ACT.Copy, v[:, :, (c - 8) * W:(c - 7) * W])
                        ins.then_inc(done, 1)
                    if p == 0 and c == C_FF:
                        act.wait_ge(res_steps, 2 * 4)
                        sum_squares(1)
                        normalise(1)
                        h_high(1, 0)
                        h_high(1, 1)
                    at_, q = later(pos, p)
                    if at_.first < CHUNKS:
                        high(at_, q)
                    if c in (0, C_FF) and p + 2 < 8:
                        h_high(int(c > 0), p + 2)
                    if c == 1:
                        if p == 1:
                            act.wait_ge(z_full, 1)
                            for t in range(T):
                                nc.scalar.activation(junk[:, t, 0:LAT], z[:, t, 0:LAT], ACT.Square,
                                                     accum_out=ssq_kv[:, t:t + 1]).then_inc(kv_ssq, 1)
                            take_root(ssq_kv, LAT, kv_ssq, T)
                        if p == 3:
                            act.wait_ge(pa_full, PA_AT[1] + 1)
                            nc.scalar.activation(kvt[:, :, :].rearrange("p a s -> p (a s)"), pa[:, 0, :], ACT.Copy)
                            nc.scalar.activation(ikt[:, :], pa[:, 1, 0:S], ACT.Copy)
                            nc.scalar.activation(a_t[:, :], pa[0:RANK, 1, S:2 * S], ACT.Copy).then_inc(pa_read, 1)
                    if c == 2 and p in (1, 2, 3):
                        if p == 1:
                            act.wait_ge(pb_read, PB_AT[1] + 1)
                            nc.scalar.activation(gate_e[:, :, :], gate_x[:, :, :], ACT.Abs).then_inc(gate_chain, 1)
                        if p == 2:
                            act.wait_ge(gate_chain, 1)
                            nc.scalar.activation(gate_e[:, :, :], gate_e[:, :, :], ACT.Exp,
                                                 scale=-1.0).then_inc(gate_chain, 1)
                        if p == 3:
                            act.wait_ge(gate_chain, 2)
                            nc.scalar.activation(gate_e[:, :, :], gate_e[:, :, :], ACT.Ln,
                                                 bias=1.0).then_inc(gate_l_ready, 1)
                    if 2 <= c <= 7 and p == 2:
                        act.wait_ge(pa_full, pos.at(PA_AT) + 1)
                        half = 4 * (c % 2)
                        to = (iqt, qt, kt)[(c - 2) // 2][:, half:half + 4, :]
                        if c == 6:
                            act.wait_ge(score_steps, 4 * H_IDX // 2)
                        ins = copy_pa(to, DK ** -0.5 if c in (4, 5) else 1.0)
                        ins.then_inc(pa_read, 1)
                    if c in (2, 3) and 3 <= p <= 6:
                        k = 4 * (c - 2) + p - 3
                        act.wait_ge(pb_full, PB_AT[2] + k + 1)
                        if k:
                            act.wait_ge(score_steps, 4 * k)
                        ins = nc.scalar.activation(relu[:, :, :], pb[:, :, 0:KEYS], ACT.Relu)
                        ins.then_inc(pb_read, 1)
                    if c in (5, 6) and p in (3, 5):
                        k = 2 * (c - 5) + (p - 3) // 2
                        act.wait_ge(pb_full, PB_AT[5] + k + 1)
                        act.wait_ge(rows_stored, 16)
                        ins = nc.scalar.activation(vals[:, :, k * W:(k + 1) * W], pb[:, :, :], ACT.Copy)
                        ins.then_inc(pb_read, 1)
                    if 8 <= c <= 11 and p in (1, 2):
                        k = 2 * (c - 8) + p - 1
                        act.wait_ge(level_diff, k + 1)
                        nc.scalar.activation(level[k % 2][:, :, :], level[k % 2][:, :, :], ACT.Exp,
                                             scale=1.0 / 16.0).then_inc(level_exp, 1)
                    if 12 <= c <= 19:
                        u = pos.n - 12
                        if p == 1:
                            act.wait_ge(pa_full, pos.at(PA_AT) + 1)
                            ins = copy_pa(q_lat[:, :, :])
                            ins.then_inc(pa_read, 1)
                        if p == 3 and c <= 15:
                            act.wait_ge(pa_full, pos.at(PA_AT) + 2)
                            for t in range(T):
                                nc.scalar.activation(junk[:, t, :], pa[:, t, :], ACT.Square,
                                                     accum_out=ssq_o[:, t:t + 1]).then_inc(o_ssq, 1)
                            take_root(ssq_o, DV, o_ssq, T * (c - 11))
                        if p == 4:
                            act.wait_ge(dsa_steps, u * DSA_STEPS + DSA_STEPS)
                            for e in range(2):
                                for t, (a, b) in enumerate(((0, P), (P, KEYS))):
                                    n = 2 * e + t
                                    nc.scalar.activation(logit[:, e, a:b], logit[:, e, a:b], ACT.Exp,
                                                         bias=neg_top[:, 2 * t + e:2 * t + e + 1],
                                                         accum_out=total[:, n:n + 1]).then_inc(prob_ready, 1)
                        last = 2 if c > 15 else 3
                        if p == 6:
                            act.wait_ge(pa_full, pos.at(PA_AT) + last)
                            ins = nc.scalar.activation(prob_t[:, :, :], pa[:, :, 0:KEYS], ACT.Copy)
                            ins.then_inc(pa_read, 1)
                        if p == 7:
                            act.wait_ge(pb_full, pos.at(PB_AT) + 2)
                            act.wait_ge(inv_ready, u + 1)
                            for e in range(2):
                                for t in range(T):
                                    n = 2 * e + t
                                    ins = nc.scalar.activation(y_dsa[:, t, bass.ds((u * 2 + e) * HD, HD)],
                                                               pb[:, 0, n * P:(n + 1) * P], ACT.Copy,
                                                               scale=inv_total[:, n:n + 1])
                            ins.then_inc(pb_read, 1)
                    if is_gt_stage(c) and p == 3:
                        j = c - 28
                        act.wait_ge(pa_full, pos.at(PA_AT) + 1)
                        copy_pa(m_hi[:, 4 * j:4 * j + 4, :]).then_inc(split_hi, 1)
                    if c in (29, 31) and 2 <= p <= 5:
                        act.wait_ge(pb_full, pos.at(PB_AT) + p - 1)
                        row = (gate1_row, gate2_row)[(c - 29) // 2]
                        ins = nc.scalar.activation(row[:, (p - 2) * W:(p - 1) * W], pb[:, 0, :], ACT.Copy)
                        ins.then_inc(pb_read, 1)
                    if c > C_FF and 1 <= group_slot(c) <= 4 and p == 3:
                        j = group_slot(c) - 1
                        act.wait_ge(pa_full, pos.at(PA_AT) + 1)
                        copy_pa(u_hi[:, 4 * j:4 * j + 4, :]).then_inc(split_hi, 1)

            act.wait_ge(x_landed, 16 * T)
            act.wait_ge(ones_ready, 1)
            sum_squares(0)
            normalise(0)
            for p in range(AHEAD):
                high(Pos(0), p)
            h_high(0, 0)
            h_high(0, 1)
            run_plan(act, chunk)
            act.wait_ge(res_steps, 2 * 4 + 2 * 16)
            sum_squares(2)

        @block.vector
        def _(dve):
            def low(pos, p):
                s = p % RING
                dve.wait_ge(hi_ready, PIECES * pos.n + (p + 1))
                n = width(pos)
                nc.vector.tensor_tensor(w_lo[:, s, :, 0:n], w_raw[:, s, :, 0:n], w_hi[:, s, :, 0:n].bitcast(F32),
                                        ALU.subtract).then_inc(lo_ready, 1)

            def mod_add(count, j):
                n, k = count, j % KT
                r = k % RING
                if j < MOD_FIRST * KT:
                    dve.wait_ge(mod_landed[r], 16 * ((n - r) // RING + 1))
                else:
                    dve.wait_ge(mod_late[r], n * (16 // RING) + (16 - (MOD_FIRST * KT + r) * (16 // RING)))
                s, b = m_raw[:, k % RING, :], m_sum[:, k % 2, :]
                if k < 2:
                    ins = nc.vector.tensor_scalar(b, s, c_act[:, k:k + 1], None, ALU.mult)
                else:
                    dve.wait_ge(mod_done, n - 1)
                    ins = nc.vector.scalar_tensor_tensor(b, s, c_act[:, k:k + 1], b, ALU.mult, ALU.add)
                ins.then_inc(mod_done, 1)

            def mod_take(m, ps, full_, free, use):
                dve.wait_ge(full_, use + 1)
                ins = nc.vector.tensor_tensor(mod_cols[:, bass.ds(m * MB, MB)], ps[:, 0, 0:MB],
                                              vec_cols[:, bass.ds(m * MB, MB)], ALU.add)
                ins.then_inc(free, 1)

            def inverse_root(of, to, n, count, step, start):
                mean, y, a = st[:, 30:30 + T], st[:, 32:32 + T], st[:, 34:34 + T]
                nc.vector.tensor_scalar(mean, of, 1.0 / n, EPS, ALU.mult, ALU.add).then_inc(step, 1)
                dve.wait_ge(root_ready, count)
                nc.vector.reciprocal(y, root).then_inc(step, 1)
                dve.wait_ge(step, start + 2)
                nc.vector.scalar_tensor_tensor(a, y, -0.5, mean, ALU.mult, ALU.mult).then_inc(step, 1)
                dve.wait_ge(step, start + 3)
                nc.vector.tensor_tensor(a, a, y, ALU.mult).then_inc(step, 1)
                dve.wait_ge(step, start + 4)
                nc.vector.scalar_tensor_tensor(to, a, 1.5, y, ALU.add, ALU.mult).then_inc(step, 1)

            def normalise(k):
                dve.wait_ge(x_ssq, T * (k + 1))
                inverse_root(ssq_x, rin_x, D, ROOT_X[k], norm_steps, ROOT_STEPS * k)
                dve.wait_ge(norm_steps, ROOT_STEPS * (k + 1))
                nc.vector.tensor_scalar(normed[:, 0, :], xs[:, 0, :], rin_x[:, 0:1], None,
                                        ALU.mult).then_inc(normed_ready, 1)

            def h_full(k, q):
                ps, at_, fulls, frees = (pa, PA_AT, pa_full, pa_read) if q % 2 == 0 else (pb, PB_AT, pb_full, pb_read)
                dve.wait_ge(fulls, at_[(0, C_FF)[k]] + q // 2 + 1)
                if q >= 2:
                    dve.wait_ge(h_lo_ready, 8 * k + q - 1)
                for a in range(2):
                    n = 2 * q + a
                    shift = mod_cols[:, 3 * KT * k + n:3 * KT * k + n + 1]
                    ins = nc.vector.tensor_scalar(full[:, q % 2, a * S:(a + 1) * S], ps[:, 0, a * S:(a + 1) * S],
                                                  h_scale[:, n:n + 1], shift, ALU.mult, ALU.add)
                ins.then_inc(frees, 1)

            def h_low(k, q):
                dve.wait_ge(h_hi_ready, 8 * k + q + 1)
                nc.vector.tensor_tensor(h_lo[:, 2 * q:2 * q + 2, :].rearrange("p a s -> p (a s)"), full[:, q % 2, :],
                                        h_hi[:, 2 * q:2 * q + 2, :].rearrange("p a s -> p (a s)").bitcast(F32),
                                        ALU.subtract).then_inc(h_lo_ready, 1)

            def h_start(k):
                sc = mod_cols[:, (3 * k + 1) * KT:(3 * k + 2) * KT]
                g = vec_cols[:, (N_MOD + k) * KT:(N_MOD + k + 1) * KT]
                nc.vector.scalar_tensor_tensor(h_scale[:, :], sc, 1.0, g, ALU.add, ALU.mult).then_inc(scale_ready, 1)
                dve.wait_ge(scale_ready, k + 1)
                if k:
                    dve.wait_ge(pa_read, PA_AT[30])
                    dve.wait_ge(res_steps, 2 * 4)
                for q in (0, 1):
                    h_full(k, q)
                for q in (0, 1):
                    h_low(k, q)

            def level_start(k):
                e = level[k % 2]
                if k >= 2:
                    dve.wait_ge(*((pa_full, PA_AT[8] + k // 2) if k % 2 == 0 else (pb_full, PB_AT[8] + 1 + k // 2)))
                if k < len(LEVELS):
                    s = LEVELS[k]
                    b4 = cum[:, :, :].rearrange("p a (n two s) -> p (a n) two s", two=2, s=s)
                    e4 = e[:, :, :].rearrange("p a (n two s) -> p (a n) two s", two=2, s=s)
                    mid = b4[:, :, 0, s - 1:s].to_broadcast([P, 8 * S // (2 * s), s])
                    nc.vector.tensor_tensor(e4[:, :, 0, :], mid, b4[:, :, 0, :], ALU.subtract)
                    ins = nc.vector.tensor_tensor(e4[:, :, 1, :], b4[:, :, 1, :], mid, ALU.subtract)
                else:
                    mid = cum[:, :, P - 1:P].to_broadcast([P, 8, P])
                    nc.vector.tensor_tensor(e[:, :, 0:P], mid, cum[:, :, 0:P], ALU.subtract)
                    ins = nc.vector.tensor_copy(e[:, :, P:S], cum[:, :, P:S])
                ins.then_inc(level_diff, 1)

            def level_scale(k):
                dve.wait_ge(level_exp, k + 1)
                s = (LEVELS + [P])[k]
                e4, k4, q4 = (y[:, :, :].rearrange("p a (n two s) -> p (a n) two s", two=2, s=s)
                              for y in (level[k % 2], kt, qt))
                nc.vector.tensor_tensor(e4[:, :, 0, :], e4[:, :, 0, :], k4[:, :, 0, :], ALU.mult)
                nc.vector.tensor_tensor(e4[:, :, 1, :], e4[:, :, 1, :], q4[:, :, 1, :], ALU.mult).then_inc(
                    level_ready, 1)

            def level_take(n, ps, frees, fulls, use, before):
                dve.wait_ge(fulls, use + 1)
                before()
                a = att[:, :, :, :].rearrange("p h t i -> p (h t) i")
                m = masks[:, n:n + 1, :].to_broadcast([P, H_GLA * T, P])
                ins = nc.vector.copy_predicated(a, m, ps[:, :, :].rearrange("p a (b i) -> p (a b) i", i=P))
                ins.then_inc(frees, 1)

            def chunk(pos):
                c = pos.first
                if c == 0:
                    h_start(0)
                mods = mod_ops(c)
                for p in range(PIECES):
                    if c > C_WO and c != C_FF and (c < C_FF or group_slot(c) in (0, 5, 6, 7)) and p == 0:
                        add_result(pos)
                    if c == C_FF and p == 0:
                        add_result(pos)
                        normalise(1)
                        h_start(1)
                    at_, q = later(pos, p)
                    if at_.first < CHUNKS:
                        low(at_, q)
                    if c in (0, C_FF) and p + 2 < 8:
                        h_full(int(c > 0), p + 2)
                        h_low(int(c > 0), p + 2)
                    if c == 1:
                        misc_side(p)
                    if c == 2 and p == 3:
                        dve.wait_ge(gate_l_ready, 1)
                        nc.vector.scalar_tensor_tensor(gate_x[:, :, :], gate_x[:, :, :], 0.0, gate_e[:, :, :],
                                                       ALU.min, ALU.subtract).then_inc(gate_chain, 1)
                    if c == 2 and p == 7:
                        dve.wait_ge(gate_chain, 3)
                        for b in range(8):
                            for t in range(T):
                                ins = nc.vector.tensor_tensor_scan(cum[:, b, t * P:(t + 1) * P], ones[:, :],
                                                                   gate_x[:, b, t * P:(t + 1) * P], 0.0,
                                                                   ALU.mult, ALU.add)
                        ins.then_inc(decay_ready, 1)
                    if c in (2, 3) and 3 <= p <= 6:
                        k = 4 * (c - 2) + p - 3
                        dve.wait_ge(pb_read, PB_AT[2] + k + 1)
                        for e in range(2):
                            for t, (a, b) in enumerate(((0, P), (P, KEYS))):
                                n = 4 * k + 2 * e + t
                                if n >= 2:
                                    dve.wait_ge(score_steps, n - 1)
                                nc.vector.scalar_tensor_tensor(
                                    score[:, a:b], relu[:, e, a:b], iw[:, t, 2 * k + e:2 * k + e + 1],
                                    score[:, a:b], ALU.mult, ALU.add).then_inc(score_steps, 1)
                    if c == 4:
                        topk_round(p)
                        if p == 7:
                            dve.wait_ge(topk_steps, 4 * (TOPK // 8))
                            nc.vector.tensor_scalar(mask[:, :], left[1][:, :], BETWEEN, NEG, ALU.is_gt,
                                                    ALU.mult).then_inc(topk_steps, 1)
                    if p < mods:
                        mod_add(pos.at(MOD_AT) + p, MOD_AT[c] + p)
                    if mods == 9 and p == 7:
                        mod_add(pos.at(MOD_AT) + 8, MOD_AT[c] + 8)
                    if mod_ends(c) and p == 7:
                        m = MOD_AT[c] // KT
                        mod_take(pos.i + m if pos.stride else m, pa, pa_full, pa_read,
                                 pos.at(PA_AT) + pa_uses(c) - 1)
                    if 8 <= c <= 11:
                        a, b = 2 * (c - 8), 2 * (c - 8) + 1
                        if p == 0:
                            if c == 8:
                                nc.vector.memset(att[:, :, :, :], 0.0).then_inc(att_zero, 1)
                                dve.wait_ge(pa_read, PA_AT[8])
                                dve.wait_ge(decay_ready, 1)
                            level_start(a)
                        if p == 1:
                            level_start(b)
                            if c == 8:
                                level_take(0, pb, pb_read, pb_full, PB_AT[8], lambda: dve.wait_ge(att_zero, 1))
                        if p == 2:
                            level_scale(a)
                        if p == 3:
                            level_scale(b)
                        if p == 4:
                            level_take(1 + a, pa, pa_read, pa_full, PA_AT[c],
                                       lambda: dve.wait_ge(pb_read, PB_AT[c] + int(c == 8)))
                        if p == 6:
                            use = PB_AT[c] + int(c == 8)
                            if c < 11:
                                level_take(1 + b, pb, pb_read, pb_full, use,
                                           lambda: dve.wait_ge(pa_read, PA_AT[c] + 1))
                            else:
                                dve.wait_ge(pb_full, use + 1)
                                ins = nc.vector.tensor_copy(att_far[:, :, :].rearrange("p h i -> p (h i)"), pb[:, 0, :])
                                ins.then_inc(pb_read, 1)
                    if 12 <= c <= 19:
                        dsa_side(pos, p)
                    if 20 <= c <= 27:
                        gate_side(pos, p)
                    if is_gt_stage(c):
                        merge_side(pos, p)
                    if c in (29, 31) and 1 <= p <= 4:
                        r = 2 * (c - 29) + p - 1
                        if r:
                            dve.wait_ge(pb_full, PB_AT[29] + r)
                        dve.wait_ge(pa_read, PA_AT[18 if c == 29 else 30])
                        for b in range(4):
                            n = (2 if c == 29 else 5) * KT + 4 * (p - 1) + b
                            ins = nc.vector.tensor_scalar(diag[:, b, :], ident[:, :], mod_cols[:, n:n + 1], None,
                                                          ALU.mult)
                        ins.then_inc(diag_ready, 1)
                    if c > C_FF and 1 <= group_slot(c) <= 4:
                        j = group_slot(c) - 1
                        if p == 1:
                            dve.wait_ge(z_full, pos.at(ZF_AT) + 1)
                            nc.vector.tensor_tensor(z[:, :, :], z[:, :, :], z[:, :, :], ALU.mult).then_inc(
                                square_ready, 1)
                        if p == 3:
                            split_low(pos, u_hi, u_lo, j)

            def split_low(pos, hi, lo, j):
                dve.wait_ge(split_hi, pos.at(SPLIT_AT) + 1)
                ins = nc.vector.tensor_tensor(
                    lo[:, 4 * j:4 * j + 4, :].rearrange("p a s -> p (a s)"),
                    pa[:, :, :].rearrange("p a w -> p (a w)"),
                    hi[:, 4 * j:4 * j + 4, :].rearrange("p a s -> p (a s)").bitcast(F32), ALU.subtract)
                ins.then_inc(pa_read, 1)

            def add_result(pos):
                prev = pos.n - 1
                c = pos.first - 1
                j = c - C_WO if c < C_FF else group_slot(c) - 4
                row = gate1_row if c < C_FF else gate2_row
                dve.wait_ge(pe_used, PIECES * prev + PIECES)
                if c == C_WO:
                    dve.wait_ge(x_again, 16 * T)
                    dve.wait_ge(pb_read, PB_AT[32])
                if c > C_WO:
                    dve.wait_ge(res_steps, pos.at(RES_AT) * 2)
                cols = slice(j * W, (j + 1) * W)
                for t in range(T):
                    ins = nc.vector.tensor_tensor(z[:, t, :], acc[:, c % 2, t, :], row[:, cols], ALU.mult)
                ins.then_inc(res_steps, 1)
                dve.wait_ge(res_steps, 2 * pos.at(RES_AT) + 1)
                ins = nc.vector.tensor_tensor(xs[:, :, cols], xs[:, :, cols], z[:, :, :], ALU.add)
                ins.then_inc(res_steps, 1)

            def misc_side(p):
                if p == 1:
                    dve.wait_ge(z_full, 1)
                    dve.wait_ge(normed_ready, 2)
                    nc.vector.tensor_copy(ik2[:, :, 0:D_IDX], z[:, :, LAT:LAT + D_IDX])
                    nc.vector.tensor_copy(ik2[:, :, D_IDX:2 * D_IDX], z[:, :, LAT:LAT + D_IDX])
                    nc.vector.tensor_scalar(iw[:, :, :], z[:, :, LAT + D_IDX:LAT + D_IDX + H_IDX],
                                            (H_IDX * D_IDX) ** -0.5, None, ALU.mult).then_inc(misc_ready, 1)
                    nc.vector.memset(score[:, :], 0.0).then_inc(score_zero, 1)
                    dve.wait_ge(kv_ssq, T)
                    inverse_root(ssq_kv, rin_kv, LAT, ROOT_KV, kv_chain, 0)
                    dve.wait_ge(kv_chain, ROOT_STEPS)
                    for t in range(T):
                        nc.vector.scalar_tensor_tensor(kvn[:, t, :], z[:, t, 0:LAT], rin_kv[:, t:t + 1], kv_g[:, :],
                                                       ALU.mult, ALU.mult).then_inc(kv_chain, 1)
                if p == 6:
                    dve.wait_ge(pa_full, PA_AT[1] + 2)
                    dve.wait_ge(pb_full, PB_AT[1] + 1)
                    for b in range(8):
                        ps = (pa, pb)[b // 4][:, b % 4 // 2, (b % 2) * S:(b % 2 + 1) * S]
                        ins = nc.vector.tensor_scalar(gate_x[:, b, :], ps, gate_cols[:, b:b + 1], None, ALU.add)
                        if b == 3:
                            ins.then_inc(pa_read, 1)
                    ins.then_inc(pb_read, 1)

            def topk_round(r):
                of, to = (score if r == 0 else left[(r + 1) % 2]), left[r % 2]
                if r == 0:
                    dve.wait_ge(score_masked, 2)
                else:
                    dve.wait_ge(topk_steps, 4 * r)
                for t, (a, b) in enumerate(((0, P), (P, KEYS))):
                    nc.vector.max(top8[:, t, :], of[:, a:b]).then_inc(topk_steps, 1)
                for t, (a, b) in enumerate(((0, P), (P, KEYS))):
                    dve.wait_ge(topk_steps, 4 * r + t + 1)
                    nc.vector.match_replace(to[:, a:b], top8[:, t, :], of[:, a:b], TAKEN).then_inc(topk_steps, 1)

            def dsa_side(pos, p):
                u = pos.n - 12
                base_ = u * DSA_STEPS
                if p == 2:
                    dve.wait_ge(pb_full, pos.at(PB_AT) + 1)
                    if pos.first == 12:
                        dve.wait_ge(bias_landed, 32)
                        dve.wait_ge(mask_ready, 2)
                    for e in range(2):
                        h = u * 2 + e
                        nc.vector.scalar_tensor_tensor(logit[:, e, 0:P], pb[:, e, 0:P], LAT ** -0.5,
                                                       one_head(bias, h, P, S), ALU.mult, ALU.add).then_inc(dsa_steps, 1)
                        ins = nc.vector.scalar_tensor_tensor(logit[:, e, P:KEYS], pb[:, e, P:KEYS], LAT ** -0.5,
                                                             one_head(bias, h, 0, S), ALU.mult, ALU.add)
                        ins.then_inc(pb_read if e else dsa_steps, 1)
                    dve.wait_ge(dsa_steps, base_ + 3)
                    dve.wait_ge(pb_read, pos.at(PB_AT) + 1)
                    nc.vector.tensor_tensor(logit[:, :, :], logit[:, :, :],
                                            mask[:, :].rearrange("p (a k) -> p a k", a=1).to_broadcast([P, 2, KEYS]),
                                            ALU.add).then_inc(dsa_steps, 1)
                    dve.wait_ge(dsa_steps, base_ + 4)
                    for t, (a, b) in enumerate(((0, P), (P, KEYS))):
                        nc.vector.tensor_reduce(neg_top[:, 2 * t:2 * t + 2], logit[:, :, a:b], AX_X, ALU.max,
                                                negate=True).then_inc(dsa_steps, 1)
                if p == 4 and pos.first <= 15:
                    g = pos.first - 12
                    dve.wait_ge(o_ssq, T * (g + 1))
                    inverse_root(ssq_o, rin_o, DV, ROOT_O + g, o_steps, ROOT_STEPS * g)
                    dve.wait_ge(o_steps, ROOT_STEPS * (g + 1))
                    for t in range(T):
                        ins = nc.vector.scalar_tensor_tensor(v[:, t, g * DV:(g + 1) * DV], pa[:, t, :],
                                                             rin_o[:, t:t + 1], gla_g[:, :], ALU.mult, ALU.mult)
                        if g == H_GLA - 1 and t == 0:
                            ins.then_inc(gate_steps, 1)
                    ins.then_inc(pa_read, 1)
                if p == 5:
                    dve.wait_ge(prob_ready, (u + 1) * 4)
                    nc.vector.reciprocal(inv_total, total).then_inc(inv_ready, 1)

            def one_head(t, h, a, b):
                return t[:, bass.ds(h, 1), a:b].rearrange("p a s -> p (a s)")

            def gate_side(pos, p):
                j = pos.i
                even = pos.first % 2 == 0
                done = pos.at(GATE_AT)
                if p == 0:
                    dve.wait_ge(z_full, pos.at(ZF_AT) + 1)
                    dve.wait_ge(pa_read, PA_AT[16])
                    if even:
                        ins = nc.vector.tensor_tensor(z[:, :, :], acc[:, (pos.first - 1) % 2, :, :], z[:, :, :],
                                                      ALU.mult)
                        ins.then_inc(gate_steps, 1)
                        dve.wait_ge(gate_steps, done + 1)
                    y = v[:, :, bass.ds(j * W, W)]
                    ins = nc.vector.tensor_tensor(y, y, z[:, :, :], ALU.mult)
                    ins.then_inc(gate_steps, 1)

            def merge_side(pos, p):
                j = pos.first - 28
                if p == 0:
                    dve.wait_ge(z_full, pos.at(ZF_AT) + 1)
                    if j == 0:
                        dve.wait_ge(pb_read, PB_AT[20])
                        dve.wait_ge(gate_steps, GATE_AT[28])
                    y, cols = y_dsa[:, :, j * W:(j + 1) * W], slice(j * W, (j + 1) * W)
                    nc.vector.tensor_tensor(y, y, z[:, :, :], ALU.mult).then_inc(merge_steps, 1)
                    dve.wait_ge(merge_steps, 2 * j + 1)
                    nc.vector.tensor_tensor(z[:, :, :], v[:, :, cols], y, ALU.add).then_inc(merge_steps, 1)
                if p == 3:
                    split_low(pos, m_hi, m_lo, j)

            nc.vector.memset(eps, EPS)
            nc.vector.memset(ones[:, :], 1.0).then_inc(ones_ready, 1)
            dve.wait_ge(act_setup, 1)
            nc.vector.tensor_scalar(c_tmp[:, 1, :], c_tmp[:, 0, :], 1.0, None, ALU.add).then_inc(dve_setup, 1)
            dve.wait_ge(dve_setup, 1)
            nc.vector.reciprocal(c_tmp[:, 2, :], c_tmp[:, 1, :]).then_inc(dve_setup, 1)
            dve.wait_ge(dve_setup, 2)
            nc.vector.tensor_tensor(c_act[:, :], c_act[:, :], c_tmp[:, 2, :], ALU.mult).then_inc(dve_setup, 1)
            dve.wait_ge(pa_full, 1)
            nc.vector.tensor_copy(vec_cols[:, :], pa[:, 0, 0:P])
            ins = nc.vector.tensor_copy(gate_cols[:, :], pa[:, 1, 0:8])
            ins.then_inc(pa_read, 1)
            dve.wait_ge(pb_full, 1)
            ins = nc.vector.tensor_copy(rows[:, :], pb[0:H_DSA, 0, 0:KEYS])
            ins.then_inc(pb_read, 1)
            normalise(0)
            dve.wait_ge(dve_setup, 3)
            dve.wait_ge(pa_read, 1)
            for m in range(MOD_FIRST):
                for k in range(KT):
                    mod_add(m * KT + k, k)
                mod_take(m, pb, pb_full, pb_read, 1 + m)
            dve.wait_ge(pb_read, 1 + MOD_FIRST)
            for p in range(AHEAD):
                low(Pos(0), p)
            run_plan(dve, chunk)
            add_result(Pos(CHUNKS))
            dve.wait_ge(x_ssq, T * 3)
            inverse_root(ssq_x, rin_x, D, ROOT_X[2], norm_steps, 2 * ROOT_STEPS)
            dve.wait_ge(norm_steps, 3 * ROOT_STEPS)
            dve.wait_ge(final_row_landed, 16)
            for t in range(T):
                nc.vector.scalar_tensor_tensor(normed[:, t, :], xs[:, t, :], rin_x[:, t:t + 1], final_row[:, :],
                                               ALU.mult, ALU.mult).then_inc(out_ready, 1)

        @block.tensor
        def _(pe):
            def transpose_h(k, q):
                ps, at_, fulls, frees = (pa, PA_AT, pa_full, pa_read) if q % 2 == 0 else (pb, PB_AT, pb_full, pb_read)
                pe.wait_ge(frees, at_[(0, C_FF)[k]] + q // 2)
                for a in range(2):
                    for t in range(T):
                        n = 2 * q + a
                        ins = nc.tensor.transpose(ps[:, 0, a * S + t * P:a * S + (t + 1) * P],
                                                  normed[:, t, n * P:(n + 1) * P], ident[:, :])
                ins.then_inc(fulls, 1)

            def sum_mod(count, ps, full_, free, use):
                pe.wait_ge(mod_done, count)
                pe.wait_ge(free, use)
                for b in range(MB):
                    for a in range(2):
                        ins = nc.tensor.matmul(ps[:, 0, b:b + 1], m_sum[:, a, b * P:(b + 1) * P], ones[:, 0:1],
                                               start=(a == 0), stop=(a == 1))
                ins.then_inc(full_, 1)

            def transpose_z(pos):
                pe.wait_ge(pa_read, pos.at(PA_AT))
                for b in range(4):
                    for t in range(T):
                        ins = nc.tensor.transpose(pa[:, b // 2, (b % 2) * S + t * P:(b % 2) * S + (t + 1) * P],
                                                  z[:, t, b * P:(b + 1) * P], ident[:, :])
                ins.then_inc(pa_full, 1)

            def level_product(k):
                ps, frees, fulls, use = ((pa, pa_read, pa_full, PA_AT[8 + k // 2]) if k % 2 == 0 else
                                         (pb, pb_read, pb_full, PB_AT[8 + k // 2] + int(k == 1)))
                pe.wait_ge(level_ready, k + 1)
                pe.wait_ge(frees, use)
                e = level[k % 2]
                for h in range(H_GLA):
                    for t in range(T):
                        far = k == len(LEVELS)
                        if far and t:
                            continue
                        n = h if far else h * T + t
                        to = ps[:, n // 4, (n % 4) * P:(n % 4 + 1) * P]
                        for a in range(2):
                            d = 2 * h + a
                            right = e[:, d, P:S] if far else e[:, d, t * P:(t + 1) * P]
                            ins = nc.tensor.matmul(to, e[:, d, t * P:(t + 1) * P], right, start=(a == 0), stop=(a == 1))
                ins.then_inc(fulls, 1)

            def diagonal_product():
                pe.wait_ge(pa_read, PA_AT[8])
                pe.wait_ge(pb_read, PB_AT[8])
                for n in range(H_GLA * T):
                    h, t = divmod(n, T)
                    for a in range(2):
                        d = 2 * h + a
                        ins = nc.tensor.matmul(pb[:, n // 4, (n % 4) * P:(n % 4 + 1) * P],
                                               kt[:, d, t * P:(t + 1) * P], qt[:, d, t * P:(t + 1) * P],
                                               start=(a == 0), stop=(a == 1))
                ins.then_inc(pb_full, 1)

            def sums_read(pos):
                c = pos.first - 1
                if 8 <= c <= 11:
                    pe.wait_ge(v_ready, c - 7)
                elif 20 <= c <= 27 and c % 2 == 0:
                    pe.wait_ge(gate_steps, pos.at(GATE_AT))
                elif C_WO < c <= C_FF or (c > C_FF and group_slot(c) not in (1, 2, 3, 4)):
                    pe.wait_ge(res_steps, pos.at(RES_AT) * 2)
                else:
                    pe.wait_ge(z_full, pos.at(ZF_AT))

            def side(pos, p):
                c = pos.first
                if c in (0, C_FF) and p + 2 < 8:
                    transpose_h(int(c > 0), p + 2)
                if c == 1 and p == 3:
                    pe.wait_ge(misc_ready, 1)
                    pe.wait_ge(kv_chain, ROOT_STEPS + T)
                    pe.wait_ge(pa_read, PA_AT[1])
                    for t in range(T):
                        cols = slice(t * P, (t + 1) * P)
                        for a in range(2):
                            nc.tensor.transpose(pa[:, 0, a * S + t * P:a * S + (t + 1) * P],
                                                kvn[:, t, a * P:(a + 1) * P], ident[:, :])
                        nc.tensor.transpose(pa[:, 1, cols], ik2[:, t, :], ident[:, :])
                        ins = nc.tensor.transpose(pa[0:RANK, 1, S + t * P:S + (t + 1) * P],
                                                  z[:, t, MISC - RANK:MISC], ident[:, :])
                    ins.then_inc(pa_full, 1)
                if c == 1 and p == 5:
                    pe.wait_ge(pa_read, PA_AT[1] + 1)
                    pe.wait_ge(pb_read, PB_AT[1])
                    for b in range(8):
                        ins = nc.tensor.matmul((pa, pb)[b // 4][:, b % 4 // 2, (b % 2) * S:(b % 2 + 1) * S],
                                               gate_up[:, b * P:(b + 1) * P], a_t[:, :], start=True, stop=True)
                        if b == 3:
                            ins.then_inc(pa_full, 1)
                    ins.then_inc(pb_full, 1)
                if 2 <= c <= 7 and p == 2:
                    pe.wait_ge(z_full, pos.at(ZF_AT) + 1)
                    transpose_z(pos)
                if c in (2, 3) and 3 <= p <= 6:
                    k = 4 * (c - 2) + p - 3
                    pe.wait_ge(pa_read, PA_AT[c] + 1)
                    pe.wait_ge(pb_read, PB_AT[2] + k)
                    for e in range(2):
                        rows_ = slice(e * D_IDX, (e + 1) * D_IDX)
                        nc.tensor.matmul(pb[:, e, 0:P], iqt[rows_, k, 0:P], ikt[rows_, 0:P], start=True, stop=True)
                        ins = nc.tensor.matmul(pb[:, e, P:KEYS], iqt[rows_, k, P:S], ikt[rows_, 0:S],
                                               start=True, stop=True)
                    ins.then_inc(pb_full, 1)
                if c in (5, 6) and p in (3, 5):
                    k = 2 * (c - 5) + (p - 3) // 2
                    pe.wait_ge(wuv_landed, 32)
                    pe.wait_ge(pb_read, PB_AT[5] + k)
                    for t in range(T):
                        for a in range(2):
                            ins = nc.tensor.matmul(pb[:, t, :], kvt[:, a, t * P:(t + 1) * P],
                                                   wuv[:, a, 4 * k:4 * k + 4, :].rearrange("p h d -> p (h d)"),
                                                   start=(a == 0), stop=(a == 1))
                    ins.then_inc(pb_full, 1)
                if mod_ends(c) and p == 7:
                    sum_mod(pos.at(MOD_AT) + 7, pa, pa_full, pa_read, pos.at(PA_AT) + pa_uses(c) - 1)
                if 8 <= c <= 11:
                    if c == 8 and p == 1:
                        diagonal_product()
                    if p == 4:
                        level_product(2 * (c - 8))
                    if p == 5:
                        level_product(2 * (c - 8) + 1)
                if 12 <= c <= 19:
                    dsa(pos, p)
                if is_gt_stage(c) and p == 2:
                    pe.wait_ge(merge_steps, 2 * (c - 28) + 2)
                    transpose_z(pos)
                if c in (29, 31) and 2 <= p <= 5:
                    r = 2 * (c - 29) + p - 2
                    pe.wait_ge(diag_ready, r + 1)
                    pe.wait_ge(pb_read, PB_AT[29] + r)
                    for b in range(4):
                        ins = nc.tensor.matmul(pb[:, 0, b * P:(b + 1) * P], ones[:, :], diag[:, b, :],
                                               start=True, stop=True)
                    ins.then_inc(pb_full, 1)
                if c > C_FF and 1 <= group_slot(c) <= 4 and p == 2:
                    pe.wait_ge(square_ready, pos.at(FF1_AT) + 1)
                    transpose_z(pos)

            def dsa(pos, p):
                c = pos.first
                u = pos.n - 12
                if p == 1:
                    pe.wait_ge(z_full, pos.at(ZF_AT) + 1)
                    transpose_z(pos)
                if p == 2:
                    pe.wait_ge(pa_read, pos.at(PA_AT) + 1)
                    pe.wait_ge(pb_read, pos.at(PB_AT))
                    for e in range(2):
                        for t, (a, b) in enumerate(((0, P), (P, KEYS))):
                            for m in range(2):
                                ins = nc.tensor.matmul(pb[:, e, a:b], q_lat[:, 2 * e + m, t * P:(t + 1) * P],
                                                       kvt[:, m, 0:b - a], start=(m == 0), stop=(m == 1))
                    ins.then_inc(pb_full, 1)
                if p == 3 and c <= 15:
                    g = c - 12
                    cols = slice(g * DV, (g + 1) * DV)
                    pe.wait_ge(v_ready, 4)
                    pe.wait_ge(pb_read, PB_AT[12])
                    pe.wait_ge(pa_read, PA_AT[c] + 1)
                    nc.tensor.matmul(pa[:, 0, :], att[:, g, 0, :], v[:, 0, cols], start=True, stop=True)
                    nc.tensor.matmul(pa[:, 1, :], att_far[:, g, :], v[:, 0, cols], start=True, stop=False)
                    nc.tensor.matmul(pa[:, 1, :], att[:, g, 1, :], v[:, 1, cols], start=False,
                                     stop=True).then_inc(pa_full, 1)
                if p == 6:
                    pe.wait_ge(prob_ready, (u + 1) * 4)
                    pe.wait_ge(pa_read, pos.at(PA_AT) + (2 if c <= 15 else 1))
                    for e in range(2):
                        for b in range(3):
                            ins = nc.tensor.transpose(pa[:, e, b * P:(b + 1) * P], logit[:, e, b * P:(b + 1) * P],
                                                      ident[:, :])
                    ins.then_inc(pa_full, 1)
                if p == 7:
                    pe.wait_ge(pa_read, pos.at(PA_AT) + (3 if c <= 15 else 2))
                    pe.wait_ge(pb_read, pos.at(PB_AT) + 1)
                    for e in range(2):
                        def value(t):
                            return vals[:, t, bass.ds((u * 2 + e) * HD, HD)]

                        n = 2 * e
                        nc.tensor.matmul(pb[:, 0, n * P:(n + 1) * P], prob_t[:, e, 0:P], value(0), start=True, stop=True)
                        nc.tensor.matmul(pb[:, 0, (n + 1) * P:(n + 2) * P], prob_t[:, e, P:2 * P], value(0),
                                         start=True, stop=False)
                        ins = nc.tensor.matmul(pb[:, 0, (n + 1) * P:(n + 2) * P], prob_t[:, e, 2 * P:KEYS], value(1),
                                               start=False, stop=True)
                    ins.then_inc(pb_full, 1)

            def chunk(pos):
                c = pos.first
                if C_WO <= c < C_FF:
                    hi, lo = m_hi, m_lo
                elif c >= C_FF and group_slot(c) >= 4:
                    hi, lo = u_hi, u_lo
                else:
                    hi, lo = h_hi, h_lo
                if c == 0:
                    transpose_h(0, 0)
                    transpose_h(0, 1)
                if c == C_FF:
                    pe.wait_ge(normed_ready, 4)
                    transpose_h(1, 0)
                    transpose_h(1, 1)
                for p in range(PIECES):
                    side(pos, p)
                    if p == 0 and c >= 2:
                        sums_read(pos)
                    pe.wait_ge(lo_ready, PIECES * pos.n + (p + 1))
                    if c in (0, C_FF):
                        pe.wait_ge(h_lo_ready, 8 * int(c > 0) + p + 1)
                    if C_WO <= c < C_FF and p % 2 == 0:
                        pe.wait_ge(pa_read, PA_AT[C_GD + 1 + p // 2] + 1)
                    if c >= C_FF and group_slot(c) == 4 and p % 2 == 0:
                        pe.wait_ge(pa_read, pos.at(PA_AT) + (p // 2 - 2))
                    n = width(pos)
                    s = p % RING
                    for a in range(PK):
                        k = p * PK + a
                        for t in range(T):
                            to = acc[:, c % 2, t, 0:n]
                            x_hi, x_lo = hi[:, k, t * P:(t + 1) * P], lo[:, k, t * P:(t + 1) * P]
                            nc.tensor.matmul(to, x_hi, w_hi[:, s, a, 0:n], start=(k == 0), stop=False)
                            nc.tensor.matmul(to, x_hi, w_lo[:, s, a, 0:n], start=False, stop=False)
                            ins = nc.tensor.matmul(to, x_lo, w_hi[:, s, a, 0:n], start=False, stop=(k == KT - 1))
                    ins.then_inc(pe_used, 1)

            pe.wait_ge(consts_landed, 16 * 11)
            nc.tensor.transpose(pa[:, 0, 0:P], vec_rows[:, :], ident[:, :])
            nc.tensor.transpose(pa[:, 1, 0:8], gate_rows[:, :], ident[0:8, 0:8]).then_inc(pa_full, 1)
            nc.tensor.matmul(pb[0:H_DSA, 0, 0:KEYS], table[:, :], onehot[:, :], start=True, stop=True).then_inc(pb_full, 1)
            pe.wait_ge(ones_ready, 1)
            for m in range(MOD_FIRST):
                sum_mod((m + 1) * KT, pb, pb_full, pb_read, 1 + m)
            pe.wait_ge(normed_ready, 2)
            run_plan(pe, chunk)


DSA_STEPS = 6
RES_AT = prefix(lambda c: int(C_WO < c <= C_FF or (c > C_FF and group_slot(c) in (0, 5, 6, 7)) ))
SPLIT_AT = prefix(lambda c: int(C_GD < c <= C_WO or (c > C_FF and 1 <= group_slot(c) <= 4)))
ROOT_STEPS = 5
ROOT_KV, ROOT_O, ROOT_X = 2, 3, (1, 3 + H_GLA, 4 + H_GLA)
ZF_AT = prefix(lambda c: int(1 <= c <= 7 or 12 <= c <= C_WO or (c > C_FF and 1 <= group_slot(c) <= 4)))
GATE_AT = prefix(lambda c: (2 - c % 2) if 20 <= c <= 27 else 0, 1)

_INS = ["x", "c", "w_mod", "b_mod", "norm1_g", "w_in", "w_gate_up", "b_gate", "gla_norm_g", "kv_norm_g",
        "w_uv", "w_out", "norm2_g", "w_ff1", "w_ff2", "rel_bias", "final_g"]
_OUTS = [((1, S, D), "float32")]


def kernel(**inputs):
    import numpy as _np
    import concourse.bacc as _bacc
    from concourse import mybir as _mybir
    from concourse.bass_utils import run_bass_kernel_spmd as _run

    nc = _bacc.Bacc("TRN2", target_bir_lowering=False, num_devices=1)
    arrays, args = {}, []
    for name in _INS:
        a = _np.ascontiguousarray(inputs[name])
        arrays[f"in_{name}_dram"] = a
        args.append(nc.dram_tensor(f"in_{name}_dram", a.shape, _mybir.dt.from_np(a.dtype), kind="ExternalInput").ap())
    for i, (shape, dtype) in enumerate(_OUTS):
        dt = _mybir.dt.from_np(_np.dtype(dtype))
        args.append(nc.dram_tensor(f"out_{i}_dram", shape, dt, kind="ExternalOutput").ap())
    build_layer(nc, *args)
    r = _run(nc, [arrays], core_ids=[0])
    got = tuple(r.results[0][f"out_{i}_dram"] for i in range(len(_OUTS)))
    return got[0]
```

```python
from contextlib import ExitStack

import numpy as np

import concourse.bass as bass
from concourse import mybir

F32 = mybir.dt.float32
F32R = mybir.dt.float32r
U8 = mybir.dt.uint8
ACT = mybir.ActivationFunctionType
ALU = mybir.AluOpType
AX_X = mybir.AxisListType.X

P = 128
D = 2048
S = 256
T = S // P
KT = D // P
W = 512
PIECES = 8
PK = KT // PIECES
RING = 4
AHEAD = RING - 1
H_GLA, DK, DV = 4, 256, 512
RANK = 16
H_DSA, LAT, HD = 16, 256, 128
H_IDX, D_IDX = 16, 64
TOPK = min(256, S // 4)
BUCKETS, MAX_DIST = 32, 128
N_MOD = 6
FF = 4 * D
EPS = 1e-6
MW = 512
MODS = N_MOD * D // MW
MOD_FIRST = 2 * D // MW
GROUPS = D // W
MB = MW // P
KEYS = P + S

SIZES = (H_GLA * DK, H_GLA * DK, H_GLA * DV, RANK, H_GLA * DV, H_DSA * LAT, LAT,
         H_IDX * D_IDX, D_IDX, H_IDX, D, D)
OFF = [sum(SIZES[:n]) for n in range(len(SIZES) + 1)]
(O_Q, O_K, O_V, O_A, O_R, O_QLAT, O_KV, O_IQ, O_IK, O_IW, O_GG, O_GD, N_IN) = OFF
MISC = LAT + D_IDX + H_IDX + RANK

FILL = -3.0e38
TAKEN = -3.4e38
BETWEEN = -3.2e38
NEG = -1.0e30

C_IQ, C_Q, C_K, C_V, C_QL, C_RG, C_GD, C_WO, C_FF = 1, 3, 5, 7, 11, 19, 27, 31, 35
CHUNKS = C_FF + 32
MOD_FROM = 2
JOINT = 0
MOD_ORDER = [n // 2 + (D // MW if n % 2 == 0 else 0) for n in range(MOD_FIRST)]
LEVELS = [1, 2, 4, 8, 16, 32, 64]

PLAN = [(2, 14, 1), (16, 2, 2), (20, 2, 4), (28, 8, 1), (36, 8, 3), (60, 7, 1)]


def group_slot(c):
    return (c - C_FF) % 8


def pa_uses(c):
    sums = int(mod_ends(c))
    if c == 0:
        return GROUPS
    if c == 2:
        return 3
    if 3 <= c <= 11:
        return 1 + sums
    if 12 <= c <= 15:
        return 3 + sums
    if 16 <= c <= 19:
        return 2 + sums
    if 20 <= c <= 27:
        return sums
    if is_gt_stage(c):
        return 1 + sums
    if C_WO < c < C_FF:
        return sums
    if c == C_FF:
        return GROUPS // 2
    if c > C_FF:
        return 1 if 1 <= group_slot(c) <= 4 else 0
    return 0


def pb_uses(c):
    if c == 0:
        return MOD_FIRST
    if c == C_FF:
        return GROUPS // 2
    if c == 2:
        return 1
    if c in (3, 4):
        return 4
    if c in (5, 6):
        return 2
    if c == 8:
        return 2
    if 9 <= c <= 11:
        return 1
    if 12 <= c <= 19:
        return 2
    if c in (30, 34):
        return 4
    return 0


def mod_ops(c):
    return KT // 2 if MOD_FROM <= c < MOD_FROM + 2 * (MODS - MOD_FIRST) else 0


def mod_slots(c):
    return (4, 5, 6, 6) if 8 <= c <= 11 else (0, 1, 2, 3)


def mod_ends(c):
    return mod_ops(c) > 0 and c % 2 == 1


def is_gt_stage(c):
    return C_GD + 1 <= c <= C_WO


def prefix(f, start=0):
    out = [start]
    for c in range(CHUNKS + 8):
        out.append(out[-1] + f(c))
    return out


SETUP_PA = 1
SETUP_PB = 1
PA_AT, PB_AT = prefix(pa_uses, SETUP_PA), prefix(pb_uses, SETUP_PB)
MOD_AT = prefix(lambda c: mod_ops(c) // PK, MOD_FIRST * PIECES)
FF1_AT = prefix(lambda c: int(c > C_FF and 1 <= group_slot(c) <= 4))


class Pos:

    def __init__(self, first, i=0, stride=0):
        self.first, self.i, self.stride = first, i, stride
        self.n = self.at(range(CHUNKS + 16))

    def at(self, table):
        per = table[self.first + self.stride] - table[self.first]
        return table[self.first] + self.i * per if per else table[self.first]


def run_plan(eng, chunk):
    for first, body, times in PLAN:
        if times == 1:
            for j in range(body):
                chunk(Pos(first + j))
        else:
            with eng.Fori(0, times) as i:
                for j in range(body):
                    chunk(Pos(first + j, i, body))


def buckets_of_distance():
    exact = BUCKETS // 2
    d = np.arange(S)
    far = np.log(np.maximum(d, 1) / exact) / np.log(MAX_DIST / exact) * (BUCKETS - exact)
    large = np.minimum(exact + np.floor(far + 1e-9).astype(int), BUCKETS - 1)
    return np.where(d < exact, d, large)


def shape_constants():
    ident = np.eye(P, dtype=np.float32)
    onehot = np.zeros((BUCKETS, KEYS), np.float32)
    bucket = buckets_of_distance()
    for j in range(KEYS):
        onehot[bucket[max(S - 1 - j, 0)], j] = 1
    j, i = np.arange(P)[:, None], np.arange(P)[None, :]
    masks = [i == j]
    for s in LEVELS:
        masks.append((j // (2 * s) == i // (2 * s)) & (j % (2 * s) < s) & (i % (2 * s) >= s))
    return ident, onehot, np.stack(masks, 1).astype(np.uint8)


def build_layer(nc, x, c, w_mod, b_mod, norm1_g, w_in, w_gate_up, b_gate, gla_norm_g, kv_norm_g,
                w_uv, w_out, norm2_g, w_ff1, w_ff2, rel_bias, final_g, out):
    ident_c, onehot_c, masks_c = shape_constants()
    ident_d = nc.inline_tensor(ident_c, "identity").ap()
    onehot_d = nc.inline_tensor(onehot_c, "bucket_onehot").ap()
    masks_d = nc.inline_tensor(masks_c.reshape(P, -1), "level_masks").ap()
    bias_rows_h = nc.dram_tensor("bias_rows", (H_DSA, P, KEYS), F32)
    bias_rows = bias_rows_h.ap()

    x_v = x.rearrange("b (t p) d -> p (b t) d", p=P)
    out_v = out.rearrange("b (t p) d -> p (b t) d", p=P)
    w_in_v = w_in.rearrange("l (k p) n -> p (l k) n", p=P)
    w_out_v = w_out.rearrange("l (k p) n -> p (l k) n", p=P)
    w_ff1_v = w_ff1.rearrange("l (k p) n -> p (l k) n", p=P)
    w_ff2_v = w_ff2.rearrange("l (k p) n -> p (l k) n", p=P)
    w_mod_v = w_mod.rearrange("l (p k) n -> p (l k) n", p=P)
    c_v = c.rearrange("b (p k) -> p (b k)", p=P)
    w_uv_v = w_uv.rearrange("l h (a p) d -> p a (l h) d", p=P)

    with ExitStack() as ctx:
        def sem(name):
            return ctx.enter_context(nc.semaphore(name))

        base = (nc.sbuf_base + 63) // 64 * 64
        KIB = 1024
        at = [base]
        used = []

        def place(name, shape, dt=F32, offset=None):
            size = mybir.dt.size(dt)
            for n in shape[1:]:
                size *= n
            if offset is None:
                offset = at[0]
                at[0] += (size + 31) // 32 * 32
            used.append(offset + size)
            return nc.alloc_sbuf_tensor_at(name, shape, dt, offset=offset)

        def region(kib):
            start = at[0]
            at[0] += kib * KIB
            return start

        h_hi = place("h_hi", [P, KT, S], F32R)
        h_lo = place("h_lo", [P, KT, S], F32R)
        w_raw = place("w_raw", [P, RING, PK, W])
        w_hi = place("w_hi", [P, RING, PK, W], F32R)
        w_lo = place("w_lo", [P, RING, PK, W], F32R)
        m_raw = place("m_raw", [P, RING, PK, MW])
        z = place("z", [P, T, W])
        full = place("full", [P, 4, S], F32, offset=at[0] - 4 * KIB)

        m_sum = place("m_sum", [P, 2, MW])
        r_att = region(6)
        m_sum_b = place("m_sum_b", [P, 2, MW], F32, r_att)
        ikt = place("ikt", [P, S], F32, r_att)
        a_t = place("a_t", [RANK, S], F32, r_att + KIB)
        att = place("att", [P, H_GLA, T, P], F32, r_att)
        att_far = place("att_far", [P, H_GLA, P], F32, r_att + 4 * KIB)

        r_act = region(32)
        m_hi = place("m_hi", [P, KT, S], F32R, r_act)
        m_lo = place("m_lo", [P, KT, S], F32R, r_act + 16 * KIB)
        u_hi = place("u_hi", [P, KT, S], F32R, r_act)
        u_lo = place("u_lo", [P, KT, S], F32R, r_act + 16 * KIB)
        vals = place("vals", [P, T, H_DSA * HD], F32, r_act)
        gate_up = place("gate_up", [RANK, H_GLA * DK], F32, r_act)
        onehot = place("onehot", [BUCKETS, KEYS], F32, r_act + 4 * KIB)
        table = place("table", [BUCKETS, H_DSA], F32, r_act + 6 * KIB)
        rows = place("rows", [H_DSA, KEYS], F32, r_act + 7 * KIB)
        kv_g = place("kv_g", [P, LAT], F32, r_act + 9 * KIB)
        vec_rows = place("vec_rows", [P, P], F32, r_act + 10 * KIB)
        gate_rows = place("gate_rows", [H_GLA * DK // P, P], F32, r_act + 11 * KIB)
        bias = place("bias", [P, H_DSA, S], F32, r_act + 16 * KIB)
        gate_x = place("gate_x", [P, 8, S], F32, r_act + 16 * KIB)
        gate_e = place("gate_e", [P, 8, S], F32, r_act + 24 * KIB)
        level = [place(f"level{n}", [P, 8, S], F32, r_act + (16 + 8 * n) * KIB) for n in (0, 1)]

        r_x = region(16)
        xs = place("xs", [P, T, D], F32, r_x)
        y_dsa = place("y_dsa", [P, T, D], F32, r_x)
        score = place("score", [P, KEYS], F32, r_x)
        left = [place(f"left{n}", [P, KEYS], F32, r_x + 1536 * (n + 1)) for n in (0, 1)]
        relu = place("relu", [P, 2, KEYS], F32, r_x + 1536 * 3)
        ik2 = place("ik2", [P, T, 2 * D_IDX], F32, r_x + 1536 * 5)
        kvn = place("kvn", [P, T, LAT], F32, r_x + 1536 * 5 + KIB)
        top8 = place("top8", [P, T, 8], F32, r_x + 1536 * 5 + 3 * KIB)

        r_v = region(16)
        normed = place("normed", [P, T, D], F32, r_v)
        wuv = place("wuv", [P, 2, H_DSA, HD], F32, r_v)
        v = place("v", [P, T, D], F32, r_v)

        r_g = region(24)
        qt = place("qt", [P, 8, S], F32, r_g)
        kt = place("kt", [P, 8, S], F32, r_g + 8 * KIB)
        cum = place("cum", [P, 8, S], F32, r_g + 16 * KIB)
        iqt = place("iqt", [P, 8, S], F32, r_g + 8 * KIB)
        q_lat = place("q_lat", [P, 4, S], F32, r_g)
        logit = place("logit", [P, 2, KEYS], F32, r_g + 4 * KIB)
        prob_t = place("prob_t", [P, 2, KEYS], F32, r_g + 7 * KIB)
        junk = place("junk", [P, T, W], F32, r_g + 10 * KIB)
        gate1_row = place("gate1_row", [P, D], F32, r_g)
        gate2_row = place("gate2_row", [P, D], F32, r_g + 8 * KIB)
        diag = place("diag", [P, 4, P], F32, r_g + 16 * KIB)
        final_row = place("final_row", [P, D], F32, r_g + 16 * KIB)

        ident = place("ident", [P, P])
        ones = place("ones", [P, P])
        masks = place("masks", [P, 1 + len(LEVELS), P], U8)
        gla_g = place("gla_g", [P, DV])
        kvt = place("kvt", [P, 2, S])
        mask = place("mask", [P, KEYS])
        vec_cols = place("vec_cols", [P, P])
        gate_cols = place("gate_cols", [P, 8])
        mod_cols = place("mod_cols", [P, N_MOD * KT])
        h_scale = place("h_scale", [P, KT])
        c_act = place("c_act", [P, KT])
        c_tmp = place("c_tmp", [P, 3, KT])
        iw = place("iw", [P, T, H_IDX])
        st = place("st", [P, 64])
        assert max(used + at) <= nc.sbuf_usable_end, (max(used + at), nc.sbuf_usable_end)
        ssq_x, rin_x = st[:, 0:T], st[:, 2:2 + T]
        ssq_kv, rin_kv = st[:, 4:4 + T], st[:, 6:6 + T]
        neg_top = st[:, 12:16]
        total, inv_total = st[:, 16:20], st[:, 20:24]
        ssq_o, rin_o = st[:, 24:24 + T], st[:, 26:26 + T]
        root, eps = st[:, 28:28 + T], st[:, 36:37]
        ssq_parts = st[:, 40:40 + T * GROUPS].rearrange("p (t j) -> p t j", t=T)

        acc = ctx.enter_context(nc.psum_tensor("acc", [P, 2, T, W], F32))
        pa = ctx.enter_context(nc.psum_tensor("pa", [P, 2, W], F32))
        pb = ctx.enter_context(nc.psum_tensor("pb", [P, 2, W], F32))

        raw_landed = [sem(f"raw_landed{n}") for n in range(RING)]
        hi_ready = sem("hi_ready")
        lo_ready = sem("lo_ready")
        pe_used = sem("pe_used")
        pa_full, pa_read = sem("pa_full"), sem("pa_read")
        pb_full, pb_read = sem("pb_full"), sem("pb_read")
        z_full = sem("z_full")
        mod_landed = [sem(f"mod_landed{n}") for n in range(RING)]
        mod_late = [sem(f"mod_late{n}") for n in range(RING)]
        mod_done = sem("mod_done")
        mod_merged = sem("mod_merged")
        x_landed, c_landed, consts_landed = sem("x_landed"), sem("c_landed"), sem("consts_landed")
        ones_ready = sem("ones_ready")
        act_setup, dve_setup = sem("act_setup"), sem("dve_setup")
        normed_ready = [sem(f"normed_ready{t}") for t in range(T)]
        h_full_ready = sem("h_full_ready")
        x_ssq, root_ready = sem("x_ssq"), sem("root_ready")
        scale_ready = sem("scale_ready")
        h_hi_ready, h_lo_ready = sem("h_hi_ready"), sem("h_lo_ready")
        rows_stored, bias_landed = sem("rows_stored"), sem("bias_landed")
        kv_ssq, misc_ready, kv_chain = sem("kv_ssq"), sem("misc_ready"), sem("kv_chain")
        gate_chain, gate_l_ready = sem("gate_chain"), sem("gate_l_ready")
        decay_ready = sem("decay_ready")
        score_zero, score_steps = sem("score_zero"), sem("score_steps")
        score_masked, topk_steps, mask_ready = sem("score_masked"), sem("topk_steps"), sem("mask_ready")
        wuv_landed = sem("wuv_landed")
        v_ready = sem("v_ready")
        level_diff, level_exp, level_ready = sem("level_diff"), sem("level_exp"), sem("level_ready")
        att_zero = sem("att_zero")
        dsa_steps, prob_ready, inv_ready = sem("dsa_steps"), sem("prob_ready"), sem("inv_ready")
        o_ssq, o_steps = sem("o_ssq"), sem("o_steps")
        gate_steps, merge_steps = sem("gate_steps"), sem("merge_steps")
        split_hi = sem("split_hi")
        diag_ready = sem("diag_ready")
        final_row_landed = sem("final_row_landed")
        x_again = sem("x_again")
        res_steps = sem("res_steps")
        norm_steps = sem("norm_steps")
        square_ready = sem("square_ready")
        out_ready, out_stored = sem("out_ready"), sem("out_stored")

        def raw_count(pos, p):
            if pos.first == JOINT:
                return (48 if p % RING < 2 else 16) * (p // RING + 1)
            return (192 if p % RING < 2 else 64) + 16 * (2 * (pos.n - 2) + p // RING + 1)

        def mod_of(pos):
            m = MOD_AT[pos.first] // PIECES
            return pos.i + m if pos.stride else m

        def piece_no(pos, p):
            return p if pos.first == JOINT else PIECES * pos.n + p

        def later(pos, p):
            if p + AHEAD < PIECES:
                return pos, p + AHEAD
            return Pos(pos.first + 1, pos.i, pos.stride), p + AHEAD - PIECES

        def width(pos, p=0):
            return MISC if pos.first == JOINT and p % RING < 2 else W

        def h_psum(k, g):
            if k == 0:
                return pa, pa_full, pa_read, PA_AT[0] + g
            if g % 2 == 0:
                return pa, pa_full, pa_read, PA_AT[C_FF] + g // 2
            return pb, pb_full, pb_read, PB_AT[C_FF] + g // 2

        block = ctx.enter_context(nc.Block())

        @block.sync
        def _(sp):
            sp.dma_start(c_act[:, :], c_v).then_inc(c_landed, 16)

            def load_first_mod(n):
                m = MOD_ORDER[n]
                for q in range(PIECES):
                    if n * PIECES + q >= RING:
                        sp.wait_ge(mod_done, (n * PIECES + q - RING + 1) * PK)
                    sp.dma_start(m_raw[:, q % RING, :, :],
                                 w_mod_v[:, q * PK:(q + 1) * PK, m * MW:(m + 1) * MW]).then_inc(
                                     mod_landed[q % RING], 16)

            def load(n, p, view, col, row=0):
                sp.wait_ge(lo_ready, PIECES * n + p - RING + 1)
                k = row + p * PK
                sp.dma_start(w_raw[:, p % RING, :, :], view[:, bass.ds(k, PK), bass.ds(col, W)]).then_inc(
                    raw_landed[p % RING], 16)

            for g in range(GROUPS):
                load_first_mod(2 * g)
                if g == 0:
                    for t in range(T):
                        sp.dma_start(xs[:, t, :], x_v[:, t, :]).then_inc(x_landed, 16)
                for s in range(RING):
                    if g:
                        sp.wait_ge(lo_ready, (g - 1) * RING + s + 1)
                    rows_ = slice((2 * g + s % 2) * PK, (2 * g + s % 2 + 1) * PK)
                    if s < 2:
                        for to, col, n in ((0, O_KV, LAT), (LAT, O_IK, D_IDX + H_IDX),
                                           (LAT + D_IDX + H_IDX, O_A, RANK)):
                            sp.dma_start(w_raw[:, s, :, to:to + n], w_in_v[:, rows_, col:col + n]).then_inc(
                                raw_landed[s], 16)
                    else:
                        sp.dma_start(w_raw[:, s, :, :], w_in_v[:, rows_, O_IQ:O_IQ + W]).then_inc(raw_landed[s], 16)
                load_first_mod(2 * g + 1)
            for first, count, col in ((C_IQ + 1, 1, O_IQ + W), (C_Q, 4, O_Q), (C_V, 4, O_V), (C_QL, 8, O_QLAT)):
                with sp.Fori(0, count) as i:
                    for p in range(PIECES):
                        load(i + first, p, w_in_v, i * W + col)
            with sp.Fori(0, H_GLA) as i:
                for p in range(PIECES):
                    load(i * 2 + C_RG, p, w_in_v, i * W + O_R)
                for p in range(PIECES):
                    load(i * 2 + (C_RG + 1), p, w_in_v, i * W + O_GG)
            with sp.Fori(0, D // W) as i:
                for p in range(PIECES):
                    load(i + C_GD, p, w_in_v, i * W + O_GD)
            with sp.Fori(0, D // W) as i:
                for p in range(PIECES):
                    load(i + C_WO, p, w_out_v, i * W)
            with sp.Fori(0, FF // D) as g:
                for j in range(D // W):
                    for p in range(PIECES):
                        load(g * 8 + (C_FF + j), p, w_ff1_v, g * D + j * W)
                for j in range(D // W):
                    for p in range(PIECES):
                        load(g * 8 + (C_FF + 4 + j), p, w_ff2_v, j * W, g * KT)
            for j in range(GROUPS):
                cols = slice(j * W, (j + 1) * W)
                sp.wait_ge(out_ready, j + 1)
                sp.dma_start(out_v[:, :, cols], normed[:, :, cols]).then_inc(out_stored, 16)
            sp.wait_ge(out_stored, 16 * GROUPS)
            sp.wait_ge(rows_stored, 16)

        @block.gpsimd
        def _(pool):
            pool.wait_ge(h_lo_ready, GROUPS)
            for a in range(2):
                pool.dma_start(wuv[:, a, :, :], w_uv_v[:, a, :, :]).then_inc(wuv_landed, 16)

            pool.dma_start(bias_rows, rows[:, :].rearrange("h (a j) -> h a j", a=1).to_broadcast(
                [H_DSA, P, KEYS])).then_inc(rows_stored, 16)

            def load_mod(n, q, col):
                pool.wait_ge(mod_done, n * PK + (1 - RING) * PK)
                pool.dma_start(m_raw[:, q % RING, :, :],
                               w_mod_v[:, q * PK:(q + 1) * PK, bass.ds(col, MW)]).then_inc(mod_late[q % RING], 16)

            def load_mods(start, stop):
                for n in range(start, stop):
                    load_mod(n, n % PIECES, n // PIECES * MW)

            def mod_piece(c):
                return MOD_FIRST * PIECES + (c - MOD_FROM) * PIECES // 2

            load_mods(mod_piece(MOD_FROM), mod_piece(6))
            pool.wait_ge(score_steps, 4 * H_IDX // 2)
            for t, (a, b) in enumerate(((0, P), (P, KEYS))):
                nc.gpsimd.affine_select(out=score[:, a:b], in_=score[:, a:b], compare_op=ALU.is_ge, fill=FILL,
                                        base=t * P, pattern=[[-1, b - a]], channel_multiplier=1).then_inc(
                                            score_masked, 1)
            load_mods(mod_piece(6), mod_piece(7))
            pool.wait_ge(topk_steps, 4 * (TOPK // 8) + 1)
            for t, (a, b) in enumerate(((0, P), (P, KEYS))):
                nc.gpsimd.affine_select(out=mask[:, a:b], in_=mask[:, a:b], compare_op=ALU.is_ge, fill=NEG,
                                        base=t * P, pattern=[[-1, b - a]], channel_multiplier=1).then_inc(
                                            mask_ready, 1)
            load_mods(mod_piece(7), mod_piece(8))
            with pool.Fori(0, 2) as i:
                for q in range(PIECES):
                    load_mod(i * PIECES + (mod_piece(8) + q), q, i * MW + mod_piece(8) // PIECES * MW)
            load_mods(mod_piece(12), mod_piece(13))
            pool.wait_ge(rows_stored, 16)
            pool.wait_ge(pa_full, PA_AT[12])
            pool.wait_ge(pb_full, PB_AT[12])
            for half in range(2):
                src = bass.AP(tensor=bias_rows_h, offset=P - 1 + half * 8 * P * KEYS,
                              ap=[[KEYS - 1, P], [P * KEYS, 8], [1, S]])
                pool.dma_start(bias[:, 8 * half:8 * half + 8, :], src).then_inc(bias_landed, 16)
            load_mods(mod_piece(13), mod_piece(14))
            with pool.Fori(0, (C_WO + 1 - 14) // 2) as i:
                for q in range(PIECES):
                    load_mod(i * PIECES + (mod_piece(14) + q), q, i * MW + mod_piece(14) // PIECES * MW)
            pool.wait_ge(merge_steps, 2 * (D // W))
            for t in range(T):
                pool.dma_start(xs[:, t, :], x_v[:, t, :]).then_inc(x_again, 16)
            load_mods(mod_piece(C_WO + 1), MODS * PIECES)
            pool.wait_ge(pb_full, PB_AT[35])
            pool.dma_start(final_row[:, :], final_g.rearrange("(a n) -> a n", a=1).to_broadcast([P, D])).then_inc(
                final_row_landed, 16)

        @block.scalar
        def _(act):
            def high(pos, p):
                s = p % RING
                act.wait_ge(raw_landed[s], raw_count(pos, p))
                if not (pos.first == JOINT and p < RING):
                    act.wait_ge(pe_used, piece_no(pos, p - RING + 1))
                n = width(pos, p)
                nc.scalar.activation(w_hi[:, s, :, 0:n], w_raw[:, s, :, 0:n], ACT.Copy).then_inc(hi_ready, 1)

            act.wait_ge(c_landed, 16)
            nc.scalar.activation(c_tmp[:, 0, :], c_act[:, :], ACT.Exp, scale=-1.0).then_inc(act_setup, 1)
            mod_rows, g_rows = N_MOD * KT, KT
            for to, of in (
                (ident[:, :], ident_d), (masks[:, :, :].rearrange("p a b -> p (a b)"), masks_d),
                (onehot[:, :], onehot_d), (table[:, :], rel_bias),
                (vec_rows[0:mod_rows, :], b_mod.rearrange("l (a p) -> (l a) p", p=P)),
                (vec_rows[mod_rows:mod_rows + g_rows, :], norm1_g.rearrange("l (a p) -> (l a) p", p=P)),
                (vec_rows[mod_rows + g_rows:P, :], norm2_g.rearrange("l (a p) -> (l a) p", p=P)),
                (gate_rows[:, :], b_gate.rearrange("l (a p) -> (l a) p", p=P)),
                (gate_up[:, :], w_gate_up.rearrange("l r n -> (l r) n")),
                (kv_g[:, :], kv_norm_g.to_broadcast([P, LAT])),
                (gla_g[:, :], gla_norm_g.to_broadcast([P, DV])),
            ):
                act.dma_start(to, of).then_inc(consts_landed, 16)

            def take_root(of, n, ready, count):
                act.wait_ge(ready, count)
                nc.scalar.activation(root, of, ACT.Sqrt, bias=eps, scale=1.0 / n).then_inc(root_ready, 1)

            def part_squares(j):
                cols = slice(j * W, (j + 1) * W)
                for t in range(T):
                    nc.scalar.activation(normed[:, t, cols], xs[:, t, cols], ACT.Square,
                                         accum_out=ssq_parts[:, t, j:j + 1]).then_inc(x_ssq, 1)

            def normalise(k):
                take_root(ssq_x, D, norm_steps, NORM_STEPS * k + 1)
                act.wait_ge(norm_steps, NORM_STEPS * (k + 1))
                for g in range(GROUPS):
                    cols = slice(g * W, (g + 1) * W)
                    nc.scalar.activation(normed[:, 1, cols], xs[:, 1, cols], ACT.Copy,
                                         scale=rin_x[:, 1:2]).then_inc(normed_ready[1], 1)
                    if k and g % 2:
                        h_high(k, g // 2)

            def h_high(k, g):
                ps, fulls, frees, use = h_psum(k, g)
                act.wait_ge(fulls, use + 1)
                act.wait_ge(scale_ready, k * GROUPS + g + 1)
                if k or g:
                    act.wait_ge(h_lo_ready, k * GROUPS + g)
                for b in range(4):
                    n = 4 * g + b
                    shift = mod_cols[:, 3 * KT * k + n:3 * KT * k + n + 1]
                    ins = nc.scalar.activation(full[:, b, :], ps[:, b // 2, (b % 2) * S:(b % 2 + 1) * S],
                                               ACT.Identity, bias=shift, scale=h_scale[:, n:n + 1])
                    ins.then_inc(frees if b == 3 else h_full_ready, 1)
                act.wait_ge(h_full_ready, 3 * (k * GROUPS + g + 1))
                act.wait_ge(frees, use + 1)
                nc.scalar.activation(h_hi[:, 4 * g:4 * g + 4, :].rearrange("p a s -> p (a s)"),
                                     full[:, :, :].rearrange("p a s -> p (a s)"), ACT.Copy).then_inc(h_hi_ready, 1)

            def take(pos, func, to=None):
                prev = pos.n - 1
                act.wait_ge(pe_used, PIECES * prev + PIECES)
                if pos.first == C_FF + 1:
                    act.wait_ge(h_lo_ready, 2 * GROUPS)
                if to is None:
                    to, done = z[:, :, :], z_full
                    if 20 <= pos.first <= 28:
                        act.wait_ge(gate_steps, pos.at(GATE_AT))
                    if pos.first > C_FF:
                        act.wait_ge(res_steps, pos.at(RES_AT) * 2)
                else:
                    done = v_ready
                a = acc[:, (pos.first - 1) % 2, :, :]
                return nc.scalar.activation(to, a, func), done

            def copy_pa(to, scale=1.0):
                return nc.scalar.activation(to.rearrange("p a s -> p (a s)"),
                                            pa[:, :, :].rearrange("p a w -> p (a w)"), ACT.Copy, scale=scale)

            def chunk(pos):
                c = pos.first
                for p in range(PIECES):
                    if p == 0 and (3 <= c <= 7 or 12 <= c <= 19 or is_gt_stage(c)
                                   or 20 <= c <= 27 or (c > C_FF and 1 <= group_slot(c) <= 4)):
                        func = (ACT.Sigmoid if 20 <= c <= 31 else ACT.Relu if c > C_FF else ACT.Copy)
                        ins, done = take(pos, func)
                        ins.then_inc(done, 1)
                    if p == 0 and 8 <= c <= 11:
                        ins, done = take(pos, ACT.Copy, v[:, :, (c - 8) * W:(c - 7) * W])
                        ins.then_inc(done, 1)
                    if p == 0 and c == C_FF:
                        part_squares_of(3, 1)
                        normalise(1)
                    at_, q = later(pos, p)
                    if at_.first < CHUNKS:
                        high(at_, q)
                    if c == C_FF and p in (1, 3):
                        h_high(1, 2 + p // 2)
                    if p == 2 and (C_WO + 1 <= c < C_FF or c > CHUNKS - 4):
                        part_squares_of(c - C_WO - 1 if c < C_FF else c - CHUNKS + 3, 1 + int(c > C_FF))
                    if p == 7 and c in (C_FF - 1, CHUNKS - 1):
                        nc.scalar.activation(st[:, 37:38], eps, ACT.Sqrt)
                    if c == 2:
                        if p == 0:
                            act.wait_ge(z_full, 1)
                            for t in range(T):
                                nc.scalar.activation(junk[:, t, 0:LAT], z[:, t, 0:LAT], ACT.Square,
                                                     accum_out=ssq_kv[:, t:t + 1]).then_inc(kv_ssq, 1)
                            take_root(ssq_kv, LAT, kv_ssq, T)
                        if p == 2:
                            act.wait_ge(pa_full, PA_AT[2] + 1)
                            nc.scalar.activation(kvt[:, :, :].rearrange("p a s -> p (a s)"), pa[:, 0, :], ACT.Copy)
                            nc.scalar.activation(ikt[:, :], pa[:, 1, 0:S], ACT.Copy)
                            nc.scalar.activation(a_t[:, :], pa[0:RANK, 1, S:2 * S], ACT.Copy).then_inc(pa_read, 1)
                        if p == 3:
                            act.wait_ge(kv_chain, ROOT_STEPS + T)
                            act.wait_ge(misc_ready, 1)
                            nc.scalar.activation(z[:, :, :], acc[:, 1, :, :], ACT.Copy).then_inc(z_full, 1)
                    if c == 2 and p == 6:
                        act.wait_ge(pb_read, PB_AT[2] + 1)
                        nc.scalar.activation(gate_e[:, :, :], gate_x[:, :, :], ACT.Abs).then_inc(gate_chain, 1)
                    if c == 2 and p == 7:
                        act.wait_ge(gate_chain, 1)
                        nc.scalar.activation(gate_e[:, :, :], gate_e[:, :, :], ACT.Exp,
                                             scale=-1.0).then_inc(gate_chain, 1)
                    if c == 3 and p == 1:
                        act.wait_ge(gate_chain, 2)
                        nc.scalar.activation(gate_e[:, :, :], gate_e[:, :, :], ACT.Ln,
                                             bias=1.0).then_inc(gate_l_ready, 1)
                    if 2 <= c <= 7 and p == (5 if c == 2 else 2):
                        act.wait_ge(pa_full, pos.at(PA_AT) + (3 if c == 2 else 1))
                        half = 4 * (c % 2)
                        to = (iqt, qt, kt)[(c - 2) // 2][:, half:half + 4, :]
                        if c == 6:
                            act.wait_ge(score_steps, 4 * H_IDX // 2)
                        ins = copy_pa(to, DK ** -0.5 if c in (4, 5) else 1.0)
                        ins.then_inc(pa_read, 1)
                    if c in (3, 4) and 3 <= p <= 6:
                        k = 4 * (c - 3) + p - 3
                        act.wait_ge(pb_full, PB_AT[3] + k + 1)
                        if k:
                            act.wait_ge(score_steps, 4 * k)
                        ins = nc.scalar.activation(relu[:, :, :], pb[:, :, 0:KEYS], ACT.Relu)
                        ins.then_inc(pb_read, 1)
                    if c in (5, 6) and p in (3, 5):
                        k = 2 * (c - 5) + (p - 3) // 2
                        act.wait_ge(pb_full, PB_AT[5] + k + 1)
                        act.wait_ge(rows_stored, 16)
                        ins = nc.scalar.activation(vals[:, :, k * W:(k + 1) * W], pb[:, :, :], ACT.Copy)
                        ins.then_inc(pb_read, 1)
                    if 8 <= c <= 11 and p in (1, 2):
                        k = 2 * (c - 8) + p - 1
                        act.wait_ge(level_diff, k + 1)
                        nc.scalar.activation(level[k % 2][:, :, :], level[k % 2][:, :, :], ACT.Exp,
                                             scale=1.0 / 16.0).then_inc(level_exp, 1)
                    if 12 <= c <= 19:
                        u = pos.n - 12
                        if p == 1:
                            act.wait_ge(pa_full, pos.at(PA_AT) + 1)
                            ins = copy_pa(q_lat[:, :, :])
                            ins.then_inc(pa_read, 1)
                        if p == 3 and c <= 15:
                            act.wait_ge(pa_full, pos.at(PA_AT) + 2)
                            for t in range(T):
                                nc.scalar.activation(junk[:, t, :], pa[:, t, :], ACT.Square,
                                                     accum_out=ssq_o[:, t:t + 1]).then_inc(o_ssq, 1)
                            take_root(ssq_o, DV, o_ssq, T * (c - 11))
                        if p == 4:
                            act.wait_ge(dsa_steps, u * DSA_STEPS + DSA_STEPS)
                            for e in range(2):
                                for t, (a, b) in enumerate(((0, P), (P, KEYS))):
                                    n = 2 * e + t
                                    nc.scalar.activation(logit[:, e, a:b], logit[:, e, a:b], ACT.Exp,
                                                         bias=neg_top[:, 2 * t + e:2 * t + e + 1],
                                                         accum_out=total[:, n:n + 1]).then_inc(prob_ready, 1)
                        last = 2 if c > 15 else 3
                        if p == 6:
                            act.wait_ge(pa_full, pos.at(PA_AT) + last)
                            ins = nc.scalar.activation(prob_t[:, :, :], pa[:, :, 0:KEYS], ACT.Copy)
                            ins.then_inc(pa_read, 1)
                        if p == 7:
                            act.wait_ge(pb_full, pos.at(PB_AT) + 2)
                            act.wait_ge(inv_ready, u + 1)
                            for e in range(2):
                                for t in range(T):
                                    n = 2 * e + t
                                    ins = nc.scalar.activation(y_dsa[:, t, bass.ds((u * 2 + e) * HD, HD)],
                                                               pb[:, 0, n * P:(n + 1) * P], ACT.Copy,
                                                               scale=inv_total[:, n:n + 1])
                            ins.then_inc(pb_read, 1)
                    if is_gt_stage(c) and p == 4:
                        j = c - 28
                        act.wait_ge(pa_full, pos.at(PA_AT) + 1)
                        copy_pa(m_hi[:, 4 * j:4 * j + 4, :]).then_inc(split_hi, 1)
                    if c in (30, 34) and 2 <= p <= 5:
                        act.wait_ge(pb_full, pos.at(PB_AT) + p - 1)
                        row = gate1_row if c == 30 else gate2_row
                        ins = nc.scalar.activation(row[:, (p - 2) * W:(p - 1) * W], pb[:, 0, :], ACT.Copy)
                        ins.then_inc(pb_read, 1)
                    if c > C_FF and 1 <= group_slot(c) <= 4 and p == 4:
                        j = group_slot(c) - 1
                        act.wait_ge(pa_full, pos.at(PA_AT) + 1)
                        copy_pa(u_hi[:, 4 * j:4 * j + 4, :]).then_inc(split_hi, 1)

            def part_squares_of(j, k):
                act.wait_ge(res_steps, 2 * (j + 1) + (2 * 16 - 2 * 4) * (k - 1) + (2 * 4 if k > 1 else 0))
                part_squares(j)

            act.wait_ge(x_landed, 16 * T)
            act.wait_ge(ones_ready, 1)
            for j in range(GROUPS):
                part_squares(j)
            for g in range(GROUPS):
                for s in range(RING):
                    high(Pos(JOINT), g * RING + s)
                if g == 0:
                    normalise(0)
                h_high(0, g)
            high(Pos(2), 0)
            high(Pos(2), 1)
            act.wait_ge(pe_used, 2 * PIECES - 2)
            act.wait_ge(h_lo_ready, GROUPS)
            nc.scalar.activation(z[:, :, 0:MISC], acc[:, 0, :, 0:MISC], ACT.Copy).then_inc(z_full, 1)
            high(Pos(2), 2)
            run_plan(act, chunk)
            part_squares_of(3, 2)
            take_root(ssq_x, D, norm_steps, NORM_STEPS * 2 + 1)

        @block.vector
        def _(dve):
            def low(pos, p):
                s = p % RING
                dve.wait_ge(hi_ready, piece_no(pos, p + 1))
                n = width(pos, p)
                nc.vector.tensor_tensor(w_lo[:, s, :, 0:n], w_raw[:, s, :, 0:n], w_hi[:, s, :, 0:n].bitcast(F32),
                                        ALU.subtract).then_inc(lo_ready, 1)

            def mod_add(count, j, sums=m_sum):
                q = j % PIECES
                r = q % RING
                if j < MOD_FIRST * PIECES:
                    dve.wait_ge(mod_landed[r], 16 * (j // RING + 1))
                else:
                    dve.wait_ge(mod_late[r], count * (16 // RING) + (16 - (MOD_FIRST * PIECES + r) * (16 // RING)))
                for a in range(PK):
                    k = q * PK + a
                    s, b = m_raw[:, r, a, :], sums[:, a, :]
                    if q == 0:
                        ins = nc.vector.tensor_scalar(b, s, c_act[:, k:k + 1], None, ALU.mult)
                    else:
                        dve.wait_ge(mod_done, count * PK + (a - 1))
                        ins = nc.vector.scalar_tensor_tensor(b, s, c_act[:, k:k + 1], b, ALU.mult, ALU.add)
                    ins.then_inc(mod_done, 1)

            def mod_merge(count, sums=m_sum):
                dve.wait_ge(mod_done, count)
                nc.vector.tensor_tensor(sums[:, 0, :], sums[:, 0, :], sums[:, 1, :], ALU.add).then_inc(mod_merged, 1)

            def mod_take(m, ps, full_, free, use):
                dve.wait_ge(full_, use + 1)
                ins = nc.vector.tensor_tensor(mod_cols[:, bass.ds(m * MB, MB)], ps[:, 0, 0:MB],
                                              vec_cols[:, bass.ds(m * MB, MB)], ALU.add)
                ins.then_inc(free, 1)

            def inverse_root(of, to, n, count, step, start):
                mean, y, a = st[:, 30:30 + T], st[:, 32:32 + T], st[:, 34:34 + T]
                nc.vector.tensor_scalar(mean, of, 1.0 / n, EPS, ALU.mult, ALU.add).then_inc(step, 1)
                dve.wait_ge(root_ready, count)
                nc.vector.reciprocal(y, root).then_inc(step, 1)
                dve.wait_ge(step, start + 2)
                nc.vector.scalar_tensor_tensor(a, y, -0.5, mean, ALU.mult, ALU.mult).then_inc(step, 1)
                dve.wait_ge(step, start + 3)
                nc.vector.tensor_tensor(a, a, y, ALU.mult).then_inc(step, 1)
                dve.wait_ge(step, start + 4)
                nc.vector.scalar_tensor_tensor(to, a, 1.5, y, ALU.add, ALU.mult).then_inc(step, 1)

            def norm_root(k):
                dve.wait_ge(x_ssq, T * GROUPS * (k + 1))
                nc.vector.tensor_reduce(ssq_x, ssq_parts, AX_X, ALU.add).then_inc(norm_steps, 1)
                dve.wait_ge(norm_steps, NORM_STEPS * k + 1)
                inverse_root(ssq_x, rin_x, D, ROOT_X[k], norm_steps, NORM_STEPS * k + 1)
                dve.wait_ge(norm_steps, NORM_STEPS * (k + 1))

            def normalise(k, g):
                cols = slice(g * W, (g + 1) * W)
                nc.vector.tensor_scalar(normed[:, 0, cols], xs[:, 0, cols], rin_x[:, 0:1], None,
                                        ALU.mult).then_inc(normed_ready[0], 1)

            def h_low(k, g):
                dve.wait_ge(h_hi_ready, k * GROUPS + g + 1)
                nc.vector.tensor_tensor(h_lo[:, 4 * g:4 * g + 4, :].rearrange("p a s -> p (a s)"),
                                        full[:, :, :].rearrange("p a s -> p (a s)"),
                                        h_hi[:, 4 * g:4 * g + 4, :].rearrange("p a s -> p (a s)").bitcast(F32),
                                        ALU.subtract).then_inc(h_lo_ready, 1)

            def h_scales(k, first, last):
                a, b = 4 * first, 4 * (last + 1)
                sc = mod_cols[:, (3 * k + 1) * KT + a:(3 * k + 1) * KT + b]
                g = vec_cols[:, (N_MOD + k) * KT + a:(N_MOD + k) * KT + b]
                return nc.vector.scalar_tensor_tensor(h_scale[:, a:b], sc, 1.0, g, ALU.add, ALU.mult)

            def level_start(k):
                e = level[k % 2]
                if k >= 2:
                    dve.wait_ge(*((pa_full, PA_AT[7 + k // 2] + 1) if k % 2 == 0 else
                                  (pb_full, PB_AT[8] + 1 + k // 2)))
                if k < len(LEVELS):
                    s = LEVELS[k]
                    b4 = cum[:, :, :].rearrange("p a (n two s) -> p (a n) two s", two=2, s=s)
                    e4 = e[:, :, :].rearrange("p a (n two s) -> p (a n) two s", two=2, s=s)
                    mid = b4[:, :, 0, s - 1:s].to_broadcast([P, 8 * S // (2 * s), s])
                    nc.vector.tensor_tensor(e4[:, :, 0, :], mid, b4[:, :, 0, :], ALU.subtract)
                    ins = nc.vector.tensor_tensor(e4[:, :, 1, :], b4[:, :, 1, :], mid, ALU.subtract)
                else:
                    mid = cum[:, :, P - 1:P].to_broadcast([P, 8, P])
                    nc.vector.tensor_tensor(e[:, :, 0:P], mid, cum[:, :, 0:P], ALU.subtract)
                    ins = nc.vector.tensor_copy(e[:, :, P:S], cum[:, :, P:S])
                ins.then_inc(level_diff, 1)

            def level_scale(k):
                dve.wait_ge(level_exp, k + 1)
                s = (LEVELS + [P])[k]
                e4, k4, q4 = (y[:, :, :].rearrange("p a (n two s) -> p (a n) two s", two=2, s=s)
                              for y in (level[k % 2], kt, qt))
                nc.vector.tensor_tensor(e4[:, :, 0, :], e4[:, :, 0, :], k4[:, :, 0, :], ALU.mult)
                nc.vector.tensor_tensor(e4[:, :, 1, :], e4[:, :, 1, :], q4[:, :, 1, :], ALU.mult).then_inc(
                    level_ready, 1)

            def level_take(n, ps, frees, fulls, use, before):
                dve.wait_ge(fulls, use + 1)
                before()
                a = att[:, :, :, :].rearrange("p h t i -> p (h t) i")
                m = masks[:, n:n + 1, :].to_broadcast([P, H_GLA * T, P])
                ins = nc.vector.copy_predicated(a, m, ps[:, :, :].rearrange("p a (b i) -> p (a b) i", i=P))
                ins.then_inc(frees, 1)

            def chunk(pos):
                c = pos.first
                for p in range(PIECES):
                    if c > C_WO and c != C_FF and (c < C_FF or group_slot(c) in (0, 5, 6, 7)) and p == 0:
                        add_result(pos)
                    if c == C_FF and p == 0:
                        add_result(pos)
                        dve.wait_ge(pa_read, PA_AT[C_FF])
                        dve.wait_ge(pb_read, PB_AT[C_FF])
                        h_scales(1, 0, GROUPS - 1).then_inc(scale_ready, GROUPS)
                        norm_root(1)
                        for g in range(GROUPS):
                            normalise(1, g)
                        h_low(1, 0)
                    at_, q = later(pos, p)
                    if at_.first < CHUNKS:
                        low(at_, q)
                    if c == C_FF and p in (0, 1, 3):
                        h_low(1, (p + 3) // 2)
                    if c == 2:
                        misc_side(p)
                    if c == 3 and p == 3:
                        dve.wait_ge(gate_l_ready, 1)
                        nc.vector.scalar_tensor_tensor(gate_x[:, :, :], gate_x[:, :, :], 0.0, gate_e[:, :, :],
                                                       ALU.min, ALU.subtract).then_inc(gate_chain, 1)
                    if c == 3 and p == 7:
                        dve.wait_ge(gate_chain, 3)
                        for b in range(8):
                            for t in range(T):
                                ins = nc.vector.tensor_tensor_scan(cum[:, b, t * P:(t + 1) * P], ones[:, :],
                                                                   gate_x[:, b, t * P:(t + 1) * P], 0.0,
                                                                   ALU.mult, ALU.add)
                        ins.then_inc(decay_ready, 1)
                    if c in (3, 4) and 3 <= p <= 6:
                        k = 4 * (c - 3) + p - 3
                        dve.wait_ge(pb_read, PB_AT[3] + k + 1)
                        for e in range(2):
                            for t, (a, b) in enumerate(((0, P), (P, KEYS))):
                                n = 4 * k + 2 * e + t
                                if n >= 2:
                                    dve.wait_ge(score_steps, n - 1)
                                nc.vector.scalar_tensor_tensor(
                                    score[:, a:b], relu[:, e, a:b], iw[:, t, 2 * k + e:2 * k + e + 1],
                                    score[:, a:b], ALU.mult, ALU.add).then_inc(score_steps, 1)
                    if c == 5:
                        topk_round(p)
                        if p == 7:
                            dve.wait_ge(topk_steps, 4 * (TOPK // 8))
                            nc.vector.tensor_scalar(mask[:, :], left[1][:, :], BETWEEN, NEG, ALU.is_gt,
                                                    ALU.mult).then_inc(topk_steps, 1)
                    for n in range(4):
                        if mod_ops(c) and mod_slots(c)[n] == p:
                            mod_add(pos.at(MOD_AT) + n, MOD_AT[c] + n)
                            if mod_ends(c) and n == 3:
                                mod_merge((pos.at(MOD_AT) + 4) * PK)
                    if mod_ends(c) and p == 7:
                        mod_take(mod_of(pos), pa, pa_full, pa_read,
                                 pos.at(PA_AT) + pa_uses(c) - 1)
                    if 8 <= c <= 11:
                        a, b = 2 * (c - 8), 2 * (c - 8) + 1
                        if p == 0:
                            if c == 8:
                                nc.vector.memset(att[:, :, :, :], 0.0).then_inc(att_zero, 1)
                                dve.wait_ge(pa_read, PA_AT[8])
                                dve.wait_ge(decay_ready, 1)
                            level_start(a)
                        if p == 1:
                            level_start(b)
                            if c == 8:
                                level_take(0, pb, pb_read, pb_full, PB_AT[8], lambda: dve.wait_ge(att_zero, 1))
                        if p == 2:
                            level_scale(a)
                        if p == 3:
                            level_scale(b)
                        if p == 6:
                            level_take(1 + a, pa, pa_read, pa_full, PA_AT[c],
                                       lambda: dve.wait_ge(pb_read, PB_AT[c] + int(c == 8)))
                        if p == 7:
                            use = PB_AT[c] + int(c == 8)
                            if c < 11:
                                level_take(1 + b, pb, pb_read, pb_full, use,
                                           lambda: dve.wait_ge(pa_read, PA_AT[c] + 1))
                            else:
                                dve.wait_ge(pb_full, use + 1)
                                ins = nc.vector.tensor_copy(att_far[:, :, :].rearrange("p h i -> p (h i)"), pb[:, 0, :])
                                ins.then_inc(pb_read, 1)
                    if 12 <= c <= 19:
                        dsa_side(pos, p)
                    if 20 <= c <= 27:
                        gate_side(pos, p)
                    if is_gt_stage(c):
                        merge_side(pos, p)
                    if c in (30, 34) and 1 <= p <= 4:
                        r = 4 * int(c == 34) + p - 1
                        if r:
                            dve.wait_ge(pb_full, PB_AT[30] + r)
                        dve.wait_ge(pa_read, PA_AT[12 if c == 30 else 34])
                        for b in range(4):
                            n = (2 if c == 30 else 5) * KT + 4 * (p - 1) + b
                            ins = nc.vector.tensor_scalar(diag[:, b, :], ident[:, :], mod_cols[:, n:n + 1], None,
                                                          ALU.mult)
                        ins.then_inc(diag_ready, 1)
                    if c > C_FF and 1 <= group_slot(c) <= 4:
                        j = group_slot(c) - 1
                        if p == 1:
                            dve.wait_ge(z_full, pos.at(ZF_AT) + 1)
                            nc.vector.tensor_tensor(z[:, :, :], z[:, :, :], z[:, :, :], ALU.mult).then_inc(
                                square_ready, 1)
                        if p == 4:
                            split_low(pos, u_hi, u_lo, j)

            def split_low(pos, hi, lo, j):
                dve.wait_ge(split_hi, pos.at(SPLIT_AT) + 1)
                ins = nc.vector.tensor_tensor(
                    lo[:, 4 * j:4 * j + 4, :].rearrange("p a s -> p (a s)"),
                    pa[:, :, :].rearrange("p a w -> p (a w)"),
                    hi[:, 4 * j:4 * j + 4, :].rearrange("p a s -> p (a s)").bitcast(F32), ALU.subtract)
                ins.then_inc(pa_read, 1)

            def add_result(pos):
                prev = pos.n - 1
                c = pos.first - 1
                j = c - C_WO if c < C_FF else group_slot(c) - 4
                row = gate1_row if c < C_FF else gate2_row
                dve.wait_ge(pe_used, PIECES * prev + PIECES)
                if c == C_WO:
                    dve.wait_ge(x_again, 16 * T)
                    dve.wait_ge(pb_read, PB_AT[32])
                if c > C_WO:
                    dve.wait_ge(res_steps, pos.at(RES_AT) * 2)
                cols = slice(j * W, (j + 1) * W)
                for t in range(T):
                    ins = nc.vector.tensor_tensor(z[:, t, :], acc[:, c % 2, t, :], row[:, cols], ALU.mult)
                ins.then_inc(res_steps, 1)
                dve.wait_ge(res_steps, 2 * pos.at(RES_AT) + 1)
                ins = nc.vector.tensor_tensor(xs[:, :, cols], xs[:, :, cols], z[:, :, :], ALU.add)
                ins.then_inc(res_steps, 1)

            def misc_side(p):
                if p == 0:
                    dve.wait_ge(z_full, 1)
                    dve.wait_ge(normed_ready[1], GROUPS)
                    nc.vector.tensor_copy(ik2[:, :, 0:D_IDX], z[:, :, LAT:LAT + D_IDX])
                    nc.vector.tensor_copy(ik2[:, :, D_IDX:2 * D_IDX], z[:, :, LAT:LAT + D_IDX])
                    nc.vector.tensor_scalar(iw[:, :, :], z[:, :, LAT + D_IDX:LAT + D_IDX + H_IDX],
                                            (H_IDX * D_IDX) ** -0.5, None, ALU.mult).then_inc(misc_ready, 1)
                    nc.vector.memset(score[:, :], 0.0).then_inc(score_zero, 1)
                    dve.wait_ge(kv_ssq, T)
                    inverse_root(ssq_kv, rin_kv, LAT, ROOT_KV, kv_chain, 0)
                    dve.wait_ge(kv_chain, ROOT_STEPS)
                    for t in range(T):
                        nc.vector.scalar_tensor_tensor(kvn[:, t, :], z[:, t, 0:LAT], rin_kv[:, t:t + 1], kv_g[:, :],
                                                       ALU.mult, ALU.mult).then_inc(kv_chain, 1)
                if p == 4:
                    dve.wait_ge(pa_full, PA_AT[2] + 2)
                    dve.wait_ge(pb_full, PB_AT[2] + 1)
                    for b in range(8):
                        ps = (pa, pb)[b // 4][:, b % 4 // 2, (b % 2) * S:(b % 2 + 1) * S]
                        ins = nc.vector.tensor_scalar(gate_x[:, b, :], ps, gate_cols[:, b:b + 1], None, ALU.add)
                        if b == 3:
                            ins.then_inc(pa_read, 1)
                    ins.then_inc(pb_read, 1)

            def topk_round(r):
                of, to = (score if r == 0 else left[(r + 1) % 2]), left[r % 2]
                if r == 0:
                    dve.wait_ge(score_masked, 2)
                else:
                    dve.wait_ge(topk_steps, 4 * r)
                for t, (a, b) in enumerate(((0, P), (P, KEYS))):
                    nc.vector.max(top8[:, t, :], of[:, a:b]).then_inc(topk_steps, 1)
                for t, (a, b) in enumerate(((0, P), (P, KEYS))):
                    dve.wait_ge(topk_steps, 4 * r + t + 1)
                    nc.vector.match_replace(to[:, a:b], top8[:, t, :], of[:, a:b], TAKEN).then_inc(topk_steps, 1)

            def dsa_side(pos, p):
                u = pos.n - 12
                base_ = u * DSA_STEPS
                if p == 2:
                    dve.wait_ge(pb_full, pos.at(PB_AT) + 1)
                    if pos.first == 12:
                        dve.wait_ge(bias_landed, 32)
                        dve.wait_ge(mask_ready, 2)
                    for e in range(2):
                        h = u * 2 + e
                        nc.vector.scalar_tensor_tensor(logit[:, e, 0:P], pb[:, e, 0:P], LAT ** -0.5,
                                                       one_head(bias, h, P, S), ALU.mult, ALU.add).then_inc(dsa_steps, 1)
                        ins = nc.vector.scalar_tensor_tensor(logit[:, e, P:KEYS], pb[:, e, P:KEYS], LAT ** -0.5,
                                                             one_head(bias, h, 0, S), ALU.mult, ALU.add)
                        ins.then_inc(pb_read if e else dsa_steps, 1)
                    dve.wait_ge(dsa_steps, base_ + 3)
                    dve.wait_ge(pb_read, pos.at(PB_AT) + 1)
                    nc.vector.tensor_tensor(logit[:, :, :], logit[:, :, :],
                                            mask[:, :].rearrange("p (a k) -> p a k", a=1).to_broadcast([P, 2, KEYS]),
                                            ALU.add).then_inc(dsa_steps, 1)
                    dve.wait_ge(dsa_steps, base_ + 4)
                    for t, (a, b) in enumerate(((0, P), (P, KEYS))):
                        nc.vector.tensor_reduce(neg_top[:, 2 * t:2 * t + 2], logit[:, :, a:b], AX_X, ALU.max,
                                                negate=True).then_inc(dsa_steps, 1)
                if p == 4 and pos.first <= 15:
                    g = pos.first - 12
                    dve.wait_ge(o_ssq, T * (g + 1))
                    inverse_root(ssq_o, rin_o, DV, ROOT_O + g, o_steps, ROOT_STEPS * g)
                    dve.wait_ge(o_steps, ROOT_STEPS * (g + 1))
                    for t in range(T):
                        ins = nc.vector.scalar_tensor_tensor(v[:, t, g * DV:(g + 1) * DV], pa[:, t, :],
                                                             rin_o[:, t:t + 1], gla_g[:, :], ALU.mult, ALU.mult)
                        if g == H_GLA - 1 and t == 0:
                            ins.then_inc(gate_steps, 1)
                    ins.then_inc(pa_read, 1)
                if p == 5:
                    dve.wait_ge(prob_ready, (u + 1) * 4)
                    nc.vector.reciprocal(inv_total, total).then_inc(inv_ready, 1)

            def one_head(t, h, a, b):
                return t[:, bass.ds(h, 1), a:b].rearrange("p a s -> p (a s)")

            def gate_side(pos, p):
                j = pos.i
                even = pos.first % 2 == 0
                done = pos.at(GATE_AT)
                if p == 0:
                    dve.wait_ge(z_full, pos.at(ZF_AT) + 1)
                    dve.wait_ge(pa_read, PA_AT[16])
                    if even:
                        ins = nc.vector.tensor_tensor(z[:, :, :], acc[:, (pos.first - 1) % 2, :, :], z[:, :, :],
                                                      ALU.mult)
                        ins.then_inc(gate_steps, 1)
                        dve.wait_ge(gate_steps, done + 1)
                    y = v[:, :, bass.ds(j * W, W)]
                    ins = nc.vector.tensor_tensor(y, y, z[:, :, :], ALU.mult)
                    ins.then_inc(gate_steps, 1)

            def merge_side(pos, p):
                j = pos.first - 28
                if p == 0:
                    dve.wait_ge(z_full, pos.at(ZF_AT) + 1)
                    if j == 0:
                        dve.wait_ge(pb_read, PB_AT[20])
                        dve.wait_ge(gate_steps, GATE_AT[28])
                    y, cols = y_dsa[:, :, j * W:(j + 1) * W], slice(j * W, (j + 1) * W)
                    nc.vector.tensor_tensor(y, y, z[:, :, :], ALU.mult).then_inc(merge_steps, 1)
                    dve.wait_ge(merge_steps, 2 * j + 1)
                    nc.vector.tensor_tensor(z[:, :, :], v[:, :, cols], y, ALU.add).then_inc(merge_steps, 1)
                if p == 4:
                    split_low(pos, m_hi, m_lo, j)

            nc.vector.memset(eps, EPS)
            nc.vector.memset(ones[:, :], 1.0).then_inc(ones_ready, 1)
            dve.wait_ge(act_setup, 1)
            nc.vector.tensor_scalar(c_tmp[:, 1, :], c_tmp[:, 0, :], 1.0, None, ALU.add).then_inc(dve_setup, 1)
            dve.wait_ge(dve_setup, 1)
            nc.vector.reciprocal(c_tmp[:, 2, :], c_tmp[:, 1, :]).then_inc(dve_setup, 1)
            dve.wait_ge(dve_setup, 2)
            nc.vector.tensor_tensor(c_act[:, :], c_act[:, :], c_tmp[:, 2, :], ALU.mult).then_inc(dve_setup, 1)
            dve.wait_ge(dve_setup, 3)

            def first_mods(n, start, stop):
                sums = (m_sum_b, m_sum)[n % 2]
                for q in range(start, stop):
                    mod_add(n * PIECES + q, n * PIECES + q, sums)
                if stop == PIECES:
                    mod_merge((n + 1) * KT, sums)

            first_mods(0, 0, PIECES)
            dve.wait_ge(pa_full, 1)
            nc.vector.tensor_copy(vec_cols[:, :], pa[:, 0, 0:P])
            ins = nc.vector.tensor_copy(gate_cols[:, :], pa[:, 1, 0:8])
            ins.then_inc(pa_read, 1)
            dve.wait_ge(pb_full, 1)
            ins = nc.vector.tensor_copy(rows[:, :], pb[0:H_DSA, 0, 0:KEYS])
            ins.then_inc(pb_read, 1)
            for g in range(GROUPS):
                if g:
                    first_mods(2 * g, 3, PIECES)
                for s in range(RING):
                    first_mods(2 * g + 1, 2 * s, 2 * s + 2)
                    if g == 0 and s == 1:
                        norm_root(0)
                        for j in range(GROUPS):
                            normalise(0, j)
                    low(Pos(JOINT), g * RING + s)
                    if s == 1:
                        dve.wait_ge(pa_read, 1)
                        mod_take(MOD_ORDER[2 * g], pb, pb_full, pb_read, PB_AT[0] + 2 * g)
                mod_take(MOD_ORDER[2 * g + 1], pb, pb_full, pb_read, PB_AT[0] + 2 * g + 1)
                dve.wait_ge(pb_read, PB_AT[0] + 2 * g + 2)
                h_scales(0, g, g).then_inc(scale_ready, 1)
                if g < GROUPS - 1:
                    first_mods(2 * g + 2, 0, 3)
                h_low(0, g)
            for p in range(AHEAD):
                low(Pos(2), p)
            run_plan(dve, chunk)
            add_result(Pos(CHUNKS))
            norm_root(2)
            dve.wait_ge(final_row_landed, 16)
            for j in range(GROUPS):
                cols = slice(j * W, (j + 1) * W)
                for t in range(T):
                    ins = nc.vector.scalar_tensor_tensor(normed[:, t, cols], xs[:, t, cols], rin_x[:, t:t + 1],
                                                         final_row[:, cols], ALU.mult, ALU.mult)
                ins.then_inc(out_ready, 1)

        @block.tensor
        def _(pe):
            def transpose_h(k, g):
                ps, fulls, frees, use = h_psum(k, g)
                pe.wait_ge(frees, use)
                for t in range(T):
                    pe.wait_ge(normed_ready[t], k * GROUPS + g + 1)
                for b in range(4):
                    for t in range(T):
                        n = 4 * g + b
                        ins = nc.tensor.transpose(ps[:, b // 2, (b % 2) * S + t * P:(b % 2) * S + (t + 1) * P],
                                                  normed[:, t, n * P:(n + 1) * P], ident[:, :])
                ins.then_inc(fulls, 1)

            def sum_mod(count, ps, full_, free, use, sums=m_sum):
                pe.wait_ge(mod_merged, count)
                pe.wait_ge(free, use)
                for b in range(MB):
                    ins = nc.tensor.matmul(ps[:, 0, b:b + 1], sums[:, 0, b * P:(b + 1) * P], ones[:, 0:1],
                                           start=True, stop=True)
                ins.then_inc(full_, 1)

            def transpose_z(pos, used=0):
                pe.wait_ge(pa_read, pos.at(PA_AT) + used)
                for b in range(4):
                    for t in range(T):
                        ins = nc.tensor.transpose(pa[:, b // 2, (b % 2) * S + t * P:(b % 2) * S + (t + 1) * P],
                                                  z[:, t, b * P:(b + 1) * P], ident[:, :])
                ins.then_inc(pa_full, 1)

            def level_product(k):
                ps, frees, fulls, use = ((pa, pa_read, pa_full, PA_AT[8 + k // 2]) if k % 2 == 0 else
                                         (pb, pb_read, pb_full, PB_AT[8 + k // 2] + int(k == 1)))
                pe.wait_ge(level_ready, k + 1)
                pe.wait_ge(frees, use)
                e = level[k % 2]
                for h in range(H_GLA):
                    for t in range(T):
                        far = k == len(LEVELS)
                        if far and t:
                            continue
                        n = h if far else h * T + t
                        to = ps[:, n // 4, (n % 4) * P:(n % 4 + 1) * P]
                        for a in range(2):
                            d = 2 * h + a
                            right = e[:, d, P:S] if far else e[:, d, t * P:(t + 1) * P]
                            ins = nc.tensor.matmul(to, e[:, d, t * P:(t + 1) * P], right, start=(a == 0), stop=(a == 1))
                ins.then_inc(fulls, 1)

            def diagonal_product():
                pe.wait_ge(pa_read, PA_AT[8])
                pe.wait_ge(pb_read, PB_AT[8])
                for n in range(H_GLA * T):
                    h, t = divmod(n, T)
                    for a in range(2):
                        d = 2 * h + a
                        ins = nc.tensor.matmul(pb[:, n // 4, (n % 4) * P:(n % 4 + 1) * P],
                                               kt[:, d, t * P:(t + 1) * P], qt[:, d, t * P:(t + 1) * P],
                                               start=(a == 0), stop=(a == 1))
                ins.then_inc(pb_full, 1)

            def sums_read(pos):
                c = pos.first - 1
                if 8 <= c <= 11:
                    pe.wait_ge(v_ready, c - 7)
                elif 20 <= c <= 27 and c % 2 == 0:
                    pe.wait_ge(gate_steps, pos.at(GATE_AT))
                elif C_WO < c <= C_FF or (c > C_FF and group_slot(c) not in (1, 2, 3, 4)):
                    pe.wait_ge(res_steps, pos.at(RES_AT) * 2)
                else:
                    pe.wait_ge(z_full, pos.at(ZF_AT))

            def side(pos, p):
                c = pos.first
                if c == C_FF and p in (1, 2):
                    transpose_h(1, p + 1)
                if c == 2 and p == 2:
                    pe.wait_ge(misc_ready, 1)
                    pe.wait_ge(kv_chain, ROOT_STEPS + T)
                    pe.wait_ge(pa_read, PA_AT[2])
                    for t in range(T):
                        cols = slice(t * P, (t + 1) * P)
                        for a in range(2):
                            nc.tensor.transpose(pa[:, 0, a * S + t * P:a * S + (t + 1) * P],
                                                kvn[:, t, a * P:(a + 1) * P], ident[:, :])
                        nc.tensor.transpose(pa[:, 1, cols], ik2[:, t, :], ident[:, :])
                        ins = nc.tensor.transpose(pa[0:RANK, 1, S + t * P:S + (t + 1) * P],
                                                  z[:, t, MISC - RANK:MISC], ident[:, :])
                    ins.then_inc(pa_full, 1)
                if c == 2 and p == 4:
                    pe.wait_ge(pa_read, PA_AT[2] + 1)
                    pe.wait_ge(pb_read, PB_AT[2])
                    for b in range(8):
                        ins = nc.tensor.matmul((pa, pb)[b // 4][:, b % 4 // 2, (b % 2) * S:(b % 2 + 1) * S],
                                               gate_up[:, b * P:(b + 1) * P], a_t[:, :], start=True, stop=True)
                        if b == 3:
                            ins.then_inc(pa_full, 1)
                    ins.then_inc(pb_full, 1)
                if 2 <= c <= 7 and p == (5 if c == 2 else 2):
                    pe.wait_ge(z_full, pos.at(ZF_AT) + 1)
                    transpose_z(pos, 2 if c == 2 else 0)
                if c in (3, 4) and 3 <= p <= 6:
                    k = 4 * (c - 3) + p - 3
                    pe.wait_ge(pa_read, PA_AT[c])
                    pe.wait_ge(pb_read, PB_AT[3] + k)
                    for e in range(2):
                        rows_ = slice(e * D_IDX, (e + 1) * D_IDX)
                        nc.tensor.matmul(pb[:, e, 0:P], iqt[rows_, k, 0:P], ikt[rows_, 0:P], start=True, stop=True)
                        ins = nc.tensor.matmul(pb[:, e, P:KEYS], iqt[rows_, k, P:S], ikt[rows_, 0:S],
                                               start=True, stop=True)
                    ins.then_inc(pb_full, 1)
                if c in (5, 6) and p in (3, 5):
                    k = 2 * (c - 5) + (p - 3) // 2
                    pe.wait_ge(wuv_landed, 32)
                    pe.wait_ge(pb_read, PB_AT[5] + k)
                    for t in range(T):
                        for a in range(2):
                            ins = nc.tensor.matmul(pb[:, t, :], kvt[:, a, t * P:(t + 1) * P],
                                                   wuv[:, a, 4 * k:4 * k + 4, :].rearrange("p h d -> p (h d)"),
                                                   start=(a == 0), stop=(a == 1))
                    ins.then_inc(pb_full, 1)
                if mod_ends(c) and p == 7:
                    sum_mod(mod_of(pos) + 1, pa, pa_full, pa_read, pos.at(PA_AT) + pa_uses(c) - 1)
                if 8 <= c <= 11:
                    if c == 8 and p == 1:
                        diagonal_product()
                    if p == 5:
                        level_product(2 * (c - 8))
                    if p == 6:
                        level_product(2 * (c - 8) + 1)
                if 12 <= c <= 19:
                    dsa(pos, p)
                if is_gt_stage(c) and p == 3:
                    pe.wait_ge(merge_steps, 2 * (c - 28) + 2)
                    transpose_z(pos)
                if c in (30, 34) and 2 <= p <= 5:
                    r = 4 * int(c == 34) + p - 2
                    pe.wait_ge(diag_ready, r + 1)
                    pe.wait_ge(pb_read, PB_AT[30] + r)
                    for b in range(4):
                        ins = nc.tensor.matmul(pb[:, 0, b * P:(b + 1) * P], ones[:, :], diag[:, b, :],
                                               start=True, stop=True)
                    ins.then_inc(pb_full, 1)
                if c > C_FF and 1 <= group_slot(c) <= 4 and p == 3:
                    pe.wait_ge(square_ready, pos.at(FF1_AT) + 1)
                    transpose_z(pos)

            def dsa(pos, p):
                c = pos.first
                u = pos.n - 12
                if p == 1:
                    pe.wait_ge(z_full, pos.at(ZF_AT) + 1)
                    transpose_z(pos)
                if p == 2:
                    pe.wait_ge(pa_read, pos.at(PA_AT) + 1)
                    pe.wait_ge(pb_read, pos.at(PB_AT))
                    for e in range(2):
                        for t, (a, b) in enumerate(((0, P), (P, KEYS))):
                            for m in range(2):
                                ins = nc.tensor.matmul(pb[:, e, a:b], q_lat[:, 2 * e + m, t * P:(t + 1) * P],
                                                       kvt[:, m, 0:b - a], start=(m == 0), stop=(m == 1))
                    ins.then_inc(pb_full, 1)
                if p == 3 and c <= 15:
                    g = c - 12
                    cols = slice(g * DV, (g + 1) * DV)
                    pe.wait_ge(v_ready, 4)
                    pe.wait_ge(pb_read, PB_AT[12])
                    pe.wait_ge(pa_read, PA_AT[c] + 1)
                    nc.tensor.matmul(pa[:, 0, :], att[:, g, 0, :], v[:, 0, cols], start=True, stop=True)
                    nc.tensor.matmul(pa[:, 1, :], att_far[:, g, :], v[:, 0, cols], start=True, stop=False)
                    nc.tensor.matmul(pa[:, 1, :], att[:, g, 1, :], v[:, 1, cols], start=False,
                                     stop=True).then_inc(pa_full, 1)
                if p == 6:
                    pe.wait_ge(prob_ready, (u + 1) * 4)
                    pe.wait_ge(pa_read, pos.at(PA_AT) + (2 if c <= 15 else 1))
                    for e in range(2):
                        for b in range(3):
                            ins = nc.tensor.transpose(pa[:, e, b * P:(b + 1) * P], logit[:, e, b * P:(b + 1) * P],
                                                      ident[:, :])
                    ins.then_inc(pa_full, 1)
                if p == 7:
                    pe.wait_ge(pa_read, pos.at(PA_AT) + (3 if c <= 15 else 2))
                    pe.wait_ge(pb_read, pos.at(PB_AT) + 1)
                    for e in range(2):
                        def value(t):
                            return vals[:, t, bass.ds((u * 2 + e) * HD, HD)]

                        n = 2 * e
                        nc.tensor.matmul(pb[:, 0, n * P:(n + 1) * P], prob_t[:, e, 0:P], value(0), start=True, stop=True)
                        nc.tensor.matmul(pb[:, 0, (n + 1) * P:(n + 2) * P], prob_t[:, e, P:2 * P], value(0),
                                         start=True, stop=False)
                        ins = nc.tensor.matmul(pb[:, 0, (n + 1) * P:(n + 2) * P], prob_t[:, e, 2 * P:KEYS], value(1),
                                               start=False, stop=True)
                    ins.then_inc(pb_full, 1)

            def chunk(pos):
                c = pos.first
                if C_WO <= c < C_FF:
                    hi, lo = m_hi, m_lo
                elif c >= C_FF and group_slot(c) >= 4:
                    hi, lo = u_hi, u_lo
                else:
                    hi, lo = h_hi, h_lo
                if c == C_FF:
                    transpose_h(1, 0)
                    transpose_h(1, 1)
                for p in range(PIECES):
                    side(pos, p)
                    if p == 0:
                        sums_read(pos)
                    pe.wait_ge(lo_ready, PIECES * pos.n + (p + 1))
                    if c == C_FF:
                        pe.wait_ge(h_lo_ready, GROUPS + p // 2 + 1)
                    if C_WO <= c < C_FF and p % 2 == 0:
                        pe.wait_ge(pa_read, PA_AT[C_GD + 1 + p // 2] + 1)
                    if c >= C_FF and group_slot(c) == 4 and p % 2 == 0:
                        pe.wait_ge(pa_read, pos.at(PA_AT) + (p // 2 - 2))
                    products(c, p, p % RING, W, hi, lo)

            def products(c, p, s, n, hi, lo):
                for a in range(PK):
                    k = p * PK + a
                    for t in range(T):
                        to = acc[:, c % 2, t, 0:n]
                        x_hi, x_lo = hi[:, k, t * P:(t + 1) * P], lo[:, k, t * P:(t + 1) * P]
                        nc.tensor.matmul(to, x_hi, w_hi[:, s, a, 0:n], start=(k == 0), stop=False)
                        nc.tensor.matmul(to, x_hi, w_lo[:, s, a, 0:n], start=False, stop=False)
                        ins = nc.tensor.matmul(to, x_lo, w_hi[:, s, a, 0:n], start=False, stop=(k == KT - 1))
                ins.then_inc(pe_used, 1)

            pe.wait_ge(consts_landed, 16 * 11)
            nc.tensor.transpose(pa[:, 0, 0:P], vec_rows[:, :], ident[:, :])
            nc.tensor.transpose(pa[:, 1, 0:8], gate_rows[:, :], ident[0:8, 0:8]).then_inc(pa_full, 1)
            nc.tensor.matmul(pb[0:H_DSA, 0, 0:KEYS], table[:, :], onehot[:, :], start=True, stop=True).then_inc(pb_full, 1)
            pe.wait_ge(ones_ready, 1)
            for g in range(GROUPS):
                transpose_h(0, g)
                for n in (2 * g, 2 * g + 1):
                    sum_mod(n + 1, pb, pb_full, pb_read, PB_AT[0] + n, (m_sum_b, m_sum)[n % 2])
                for s in range(RING):
                    pe.wait_ge(lo_ready, g * RING + s + 1)
                    pe.wait_ge(h_lo_ready, g + 1)
                    products(s // 2, 2 * g + s % 2, s, width(Pos(JOINT), s), h_hi, h_lo)
            run_plan(pe, chunk)


DSA_STEPS = 6
RES_AT = prefix(lambda c: int(C_WO < c <= C_FF or (c > C_FF and group_slot(c) in (0, 5, 6, 7)) ))
SPLIT_AT = prefix(lambda c: int(C_GD < c <= C_WO or (c > C_FF and 1 <= group_slot(c) <= 4)))
ROOT_STEPS = 5
NORM_STEPS = ROOT_STEPS + 1
ROOT_KV, ROOT_O, ROOT_X = 2, 3, (1, 3 + H_GLA, 4 + H_GLA)
ZF_AT = prefix(lambda c: int(c == 0 or 2 <= c <= 7 or 12 <= c <= C_WO or (c > C_FF and 1 <= group_slot(c) <= 4)))
GATE_AT = prefix(lambda c: (2 - c % 2) if 20 <= c <= 27 else 0, 1)

_INS = ["x", "c", "w_mod", "b_mod", "norm1_g", "w_in", "w_gate_up", "b_gate", "gla_norm_g", "kv_norm_g",
        "w_uv", "w_out", "norm2_g", "w_ff1", "w_ff2", "rel_bias", "final_g"]
_OUTS = [((1, S, D), "float32")]


def kernel(**inputs):
    import numpy as _np
    import concourse.bacc as _bacc
    from concourse import mybir as _mybir
    from concourse.bass_utils import run_bass_kernel_spmd as _run

    nc = _bacc.Bacc("TRN2", target_bir_lowering=False, num_devices=1)
    arrays, args = {}, []
    for name in _INS:
        a = _np.ascontiguousarray(inputs[name])
        arrays[f"in_{name}_dram"] = a
        args.append(nc.dram_tensor(f"in_{name}_dram", a.shape, _mybir.dt.from_np(a.dtype), kind="ExternalInput").ap())
    for i, (shape, dtype) in enumerate(_OUTS):
        dt = _mybir.dt.from_np(_np.dtype(dtype))
        args.append(nc.dram_tensor(f"out_{i}_dram", shape, dt, kind="ExternalOutput").ap())
    build_layer(nc, *args)
    r = _run(nc, [arrays], core_ids=[0])
    got = tuple(r.results[0][f"out_{i}_dram"] for i in range(len(_OUTS)))
    return got[0]
```

```python
from contextlib import ExitStack

import numpy as np

import concourse.bass as bass
from concourse import mybir

F32 = mybir.dt.float32
F32R = mybir.dt.float32r
U8 = mybir.dt.uint8
ACT = mybir.ActivationFunctionType
ALU = mybir.AluOpType
AX_X = mybir.AxisListType.X

P = 128
D = 2048
S = 256
T = S // P
KT = D // P
W = 512
PIECES = 8
PK = KT // PIECES
RING = 4
FIRST_RING = 6
AHEAD = RING - 1
H_GLA, DK, DV = 4, 256, 512
RANK = 16
H_DSA, LAT, HD = 16, 256, 128
H_IDX, D_IDX = 16, 64
TOPK = min(256, S // 4)
BUCKETS, MAX_DIST = 32, 128
N_MOD = 6
FF = 4 * D
EPS = 1e-6
MW = 512
MODS = N_MOD * D // MW
MOD_FIRST = 2 * D // MW
GROUPS = D // W
MB = MW // P
KEYS = P + S

SIZES = (H_GLA * DK, H_GLA * DK, H_GLA * DV, RANK, H_GLA * DV, H_DSA * LAT, LAT,
         H_IDX * D_IDX, D_IDX, H_IDX, D, D)
OFF = [sum(SIZES[:n]) for n in range(len(SIZES) + 1)]
(O_Q, O_K, O_V, O_A, O_R, O_QLAT, O_KV, O_IQ, O_IK, O_IW, O_GG, O_GD, N_IN) = OFF
MISC = LAT + D_IDX + H_IDX + RANK

FILL = -3.0e38
TAKEN = -3.4e38
BETWEEN = -3.2e38
NEG = -1.0e30

C_IQ, C_Q, C_K, C_V, C_QL, C_RG, C_GD, C_WO, C_FF = 1, 3, 5, 7, 11, 19, 27, 31, 35
CHUNKS = C_FF + 32
MOD_FROM = 2
JOINT = 0
MOD_ORDER = [n // 2 + (D // MW if n % 2 == 0 else 0) for n in range(MOD_FIRST)]
GATE_BLOCKS = 2 * D // MW
GATES_FROM = MODS - GATE_BLOCKS


def mod_at(n):
    return n + D // MW if n < GATES_FROM + GATE_BLOCKS // 2 else n - GATES_FROM + 2 * D // MW - GATE_BLOCKS // 2


def gate_slot(n):
    return (n - GATES_FROM - 1) % GATE_BLOCKS


LEVELS = [1, 2, 4, 8, 16, 32, 64]

PLAN = [(2, 18, 1), (20, 2, 4), (28, 8, 1), (36, 8, 3), (60, 7, 1)]


def group_slot(c):
    return (c - C_FF) % 8


def pa_uses(c):
    sums = int(mod_ends(c))
    if c == 0:
        return GROUPS
    if c == 2:
        return 3
    if 3 <= c <= 11:
        return 1 + sums
    if 12 <= c <= 15:
        return 3 + sums
    if 16 <= c <= 19:
        return 2 + sums
    if 20 <= c <= 27:
        return sums
    if is_gt_stage(c):
        return 1 + sums
    if C_WO < c < C_FF:
        return sums
    if c == C_FF:
        return GROUPS // 2
    if c > C_FF:
        return 1 if 1 <= group_slot(c) <= 4 else 0
    return 0


def pb_uses(c):
    if c == 0:
        return MOD_FIRST
    if c == C_FF:
        return GROUPS // 2
    if c == 2:
        return 1
    if c in (3, 4):
        return 4
    if c in (5, 6):
        return 2
    if c == 8:
        return 2
    if 9 <= c <= 11:
        return 1
    if 12 <= c <= 19:
        return 2
    return 0


def mod_ops(c):
    return KT // 2 if MOD_FROM <= c < MOD_FROM + 2 * (MODS - MOD_FIRST) else 0


GPSIMD_PIECE = 3


def by_gpsimd(j):
    return j % PIECES == GPSIMD_PIECE


def mod_slots(c):
    return (4, 5, 5, 6) if 8 <= c <= 11 else (0, 1, 2, 3)


def mod_ends(c):
    return mod_ops(c) > 0 and c % 2 == 1


def is_gt_stage(c):
    return C_GD + 1 <= c <= C_WO


def prefix(f, start=0):
    out = [start]
    for c in range(CHUNKS + 8):
        out.append(out[-1] + f(c))
    return out


SETUP_PA = 1
SETUP_PB = 1
PA_AT, PB_AT = prefix(pa_uses, SETUP_PA), prefix(pb_uses, SETUP_PB)
DVE_ROWS = [sum(PK for i in range(j) if not by_gpsimd(i)) for j in range(MOD_FIRST * PIECES + 1)]
POOL_PIECES = [sum(by_gpsimd(i) for i in range(j)) for j in range(MOD_FIRST * PIECES + 1)]
POOL_ROWS = POOL_PIECES[-1] * PK


def pool_steps(j):
    return 3 * POOL_PIECES[j]


MOD_AT = prefix(lambda c: mod_ops(c) // PK, MOD_FIRST * PIECES)
FF1_AT = prefix(lambda c: int(c > C_FF and 1 <= group_slot(c) <= 4))


class Pos:

    def __init__(self, first, i=0, stride=0):
        self.first, self.i, self.stride = first, i, stride
        self.n = self.at(range(CHUNKS + 16))

    def at(self, table):
        per = table[self.first + self.stride] - table[self.first]
        return table[self.first] + self.i * per if per else table[self.first]


def run_plan(eng, chunk):
    for first, body, times in PLAN:
        if times == 1:
            for j in range(body):
                chunk(Pos(first + j))
        else:
            with eng.Fori(0, times) as i:
                for j in range(body):
                    chunk(Pos(first + j, i, body))


def buckets_of_distance():
    exact = BUCKETS // 2
    d = np.arange(S)
    far = np.log(np.maximum(d, 1) / exact) / np.log(MAX_DIST / exact) * (BUCKETS - exact)
    large = np.minimum(exact + np.floor(far + 1e-9).astype(int), BUCKETS - 1)
    return np.where(d < exact, d, large)


def shape_constants():
    ident = np.eye(P, dtype=np.float32)
    onehot = np.zeros((BUCKETS, KEYS), np.float32)
    bucket = buckets_of_distance()
    for j in range(KEYS):
        onehot[bucket[max(S - 1 - j, 0)], j] = 1
    j, i = np.arange(P)[:, None], np.arange(P)[None, :]
    masks = [i == j]
    for s in LEVELS:
        m = (j // (2 * s) == i // (2 * s)) & (j % (2 * s) < s)
        m = m[:, np.arange(P) % (2 * s) >= s]
        masks.append(np.concatenate([m, m], 1))
    return ident, onehot, np.stack(masks, 1).astype(np.uint8)


def build_layer(nc, x, c, w_mod, b_mod, norm1_g, w_in, w_gate_up, b_gate, gla_norm_g, kv_norm_g,
                w_uv, w_out, norm2_g, w_ff1, w_ff2, rel_bias, final_g, out):
    ident_c, onehot_c, masks_c = shape_constants()
    ident_d = nc.inline_tensor(ident_c, "identity").ap()
    onehot_d = nc.inline_tensor(onehot_c, "bucket_onehot").ap()
    masks_d = nc.inline_tensor(masks_c.reshape(P, -1), "level_masks").ap()
    bias_rows_h = nc.dram_tensor("bias_rows", (H_DSA, P, KEYS), F32)
    bias_rows = bias_rows_h.ap()

    x_v = x.rearrange("b (t p) d -> p (b t) d", p=P)
    out_v = out.rearrange("b (t p) d -> p (b t) d", p=P)
    w_in_v = w_in.rearrange("l (k p) n -> p (l k) n", p=P)
    w_out_v = w_out.rearrange("l (k p) n -> p (l k) n", p=P)
    w_ff1_v = w_ff1.rearrange("l (k p) n -> p (l k) n", p=P)
    w_ff2_v = w_ff2.rearrange("l (k p) n -> p (l k) n", p=P)
    w_mod_v = w_mod.rearrange("l (p k) n -> p (l k) n", p=P)
    c_v = c.rearrange("b (p k) -> p (b k)", p=P)
    w_uv_v = w_uv.rearrange("l h (a p) d -> p a (l h) d", p=P)

    with ExitStack() as ctx:
        def sem(name):
            return ctx.enter_context(nc.semaphore(name))

        base = (nc.sbuf_base + 63) // 64 * 64
        KIB = 1024
        at = [base]
        used = []

        def place(name, shape, dt=F32, offset=None):
            size = mybir.dt.size(dt)
            for n in shape[1:]:
                size *= n
            if offset is None:
                offset = at[0]
                at[0] += (size + 31) // 32 * 32
            used.append(offset + size)
            return nc.alloc_sbuf_tensor_at(name, shape, dt, offset=offset)

        def region(kib):
            start = at[0]
            at[0] += kib * KIB
            return start

        h_hi = place("h_hi", [P, KT, S], F32R)
        h_lo = place("h_lo", [P, KT, S], F32R)
        w_raw = place("w_raw", [P, RING, PK, W])
        w_hi = place("w_hi", [P, RING, PK, W], F32R)
        w_lo = place("w_lo", [P, RING, PK, W], F32R)
        m_raw = place("m_raw", [P, RING, PK, MW])
        z = place("z", [P, T, W])
        full = place("full", [P, 4, S], F32, offset=at[0] - 4 * KIB)

        m_sum = place("m_sum", [P, 2, MW])
        r_att = region(6)
        m_sum_b = place("m_sum_b", [P, 2, MW], F32, r_att)
        ikt = place("ikt", [P, S], F32, r_att)
        a_t = place("a_t", [RANK, S], F32, r_att + KIB)
        att = place("att", [P, H_GLA, T, P], F32, r_att)
        att_far = place("att_far", [P, H_GLA, P], F32, r_att + 4 * KIB)

        r_act = region(32)
        m_hi = place("m_hi", [P, KT, S], F32R, r_act)
        m_lo = place("m_lo", [P, KT, S], F32R, r_act + 16 * KIB)
        u_hi = place("u_hi", [P, KT, S], F32R, r_act)
        u_lo = place("u_lo", [P, KT, S], F32R, r_act + 16 * KIB)
        vals = place("vals", [P, T, H_DSA * HD], F32, r_act)
        gate_up = place("gate_up", [RANK, H_GLA * DK], F32, r_act)
        onehot = place("onehot", [BUCKETS, KEYS], F32, r_act + 4 * KIB)
        table = place("table", [BUCKETS, H_DSA], F32, r_act + 6 * KIB)
        rows = place("rows", [H_DSA, KEYS], F32, r_act + 7 * KIB)
        m_sum_c = place("m_sum_c", [P, 2, MW], F32, r_act + 12 * KIB)
        m_product = place("m_product", [P, MW], F32, r_act + 16 * KIB)
        kv_g = place("kv_g", [P, LAT], F32, r_act + 9 * KIB)
        vec_rows = place("vec_rows", [P, P], F32, r_act + 10 * KIB)
        gate_rows = place("gate_rows", [H_GLA * DK // P, P], F32, r_act + 11 * KIB)
        bias = place("bias", [P, H_DSA, S], F32, r_act + 16 * KIB)
        gate_x = place("gate_x", [P, 8, S], F32, r_act + 16 * KIB)
        gate_e = place("gate_e", [P, 8, S], F32, r_act + 24 * KIB)
        level = [place(f"level{n}", [P, 8, S], F32, r_act + (16 + 8 * n) * KIB) for n in (0, 1)]

        r_x = region(16)
        xs = place("xs", [P, T, D], F32, r_x)
        y_dsa = place("y_dsa", [P, T, D], F32, r_x)
        score = place("score", [P, KEYS], F32, r_x)
        left = [place(f"left{n}", [P, KEYS], F32, r_x + 1536 * (n + 1)) for n in (0, 1)]
        relu = place("relu", [P, 2, KEYS], F32, r_x + 1536 * 3)
        ik2 = place("ik2", [P, T, 2 * D_IDX], F32, r_x + 1536 * 5)
        kvn = place("kvn", [P, T, LAT], F32, r_x + 1536 * 5 + KIB)
        top8 = place("top8", [P, T, 8], F32, r_x + 1536 * 5 + 3 * KIB)

        r_v = region(16)
        normed = place("normed", [P, T, D], F32, r_v)
        wuv = place("wuv", [P, 2, H_DSA, HD], F32, r_v)
        v = place("v", [P, T, D], F32, r_v)

        r_g = region(24)
        m_first = place("m_first", [P, FIRST_RING, PK, MW], F32, r_g)
        qt = place("qt", [P, 8, S], F32, r_g)
        kt = place("kt", [P, 8, S], F32, r_g + 8 * KIB)
        cum = place("cum", [P, 8, S], F32, r_g + 16 * KIB)
        iqt = place("iqt", [P, 8, S], F32, r_g + 8 * KIB)
        q_lat = place("q_lat", [P, 4, S], F32, r_g)
        logit = place("logit", [P, 2, KEYS], F32, r_g + 4 * KIB)
        prob_t = place("prob_t", [P, 2, KEYS], F32, r_g + 7 * KIB)
        junk = place("junk", [P, T, W], F32, r_g + 10 * KIB)
        gates = place("gates", [P, GATE_BLOCKS, MW], F32, r_g + 8 * KIB)
        final_row = place("final_row", [P, D], F32, r_g)

        ident = place("ident", [P, P])
        ones = place("ones", [P, P])
        masks = place("masks", [P, 1 + len(LEVELS), P], U8)
        gla_g = place("gla_g", [P, DV])
        kvt = place("kvt", [P, 2, S])
        mask = place("mask", [P, KEYS])
        vec_cols = place("vec_cols", [P, P])
        gate_cols = place("gate_cols", [P, 8])
        mod_cols = place("mod_cols", [P, N_MOD * KT])
        h_scale = place("h_scale", [P, KT])
        c_act = place("c_act", [P, KT])
        c_tmp = place("c_tmp", [P, 3, KT])
        iw = place("iw", [P, T, H_IDX])
        st = place("st", [P, 64])
        assert max(used + at) <= nc.sbuf_usable_end, (max(used + at), nc.sbuf_usable_end)
        ssq_x, rin_x = st[:, 0:T], st[:, 2:2 + T]
        ssq_kv, rin_kv = st[:, 4:4 + T], st[:, 6:6 + T]
        neg_top = st[:, 12:16]
        total, inv_total = st[:, 16:20], st[:, 20:24]
        ssq_o, rin_o = st[:, 24:24 + T], st[:, 26:26 + T]
        root, eps = st[:, 28:28 + T], st[:, 36:37]
        ssq_parts = st[:, 40:40 + T * GROUPS].rearrange("p (t j) -> p t j", t=T)

        acc = ctx.enter_context(nc.psum_tensor("acc", [P, 2, T, W], F32))
        pa = ctx.enter_context(nc.psum_tensor("pa", [P, 2, W], F32))
        pb = ctx.enter_context(nc.psum_tensor("pb", [P, 2, W], F32))

        raw_landed = [sem(f"raw_landed{n}") for n in range(RING)]
        hi_ready = sem("hi_ready")
        lo_ready = sem("lo_ready")
        pe_used = sem("pe_used")
        pa_full, pa_read = sem("pa_full"), sem("pa_read")
        pb_full, pb_read = sem("pb_full"), sem("pb_read")
        z_full = sem("z_full")
        mod_landed = [sem(f"mod_landed{n}") for n in range(FIRST_RING)]
        mod_late = [sem(f"mod_late{n}") for n in range(RING)]
        mod_done = sem("mod_done")
        mod_by_pool = sem("mod_by_pool")
        mod_pool_added = sem("mod_pool_added")
        mod_merged = sem("mod_merged")
        x_landed, c_landed, consts_landed = sem("x_landed"), sem("c_landed"), sem("consts_landed")
        ones_ready = sem("ones_ready")
        act_setup, dve_setup = sem("act_setup"), sem("dve_setup")
        normed_ready = [sem(f"normed_ready{t}") for t in range(T)]
        h_full_ready = sem("h_full_ready")
        x_ssq, root_ready = sem("x_ssq"), sem("root_ready")
        scale_ready = sem("scale_ready")
        h_hi_ready, h_lo_ready = sem("h_hi_ready"), sem("h_lo_ready")
        rows_stored, bias_landed = sem("rows_stored"), sem("bias_landed")
        kv_ssq, misc_ready, kv_chain = sem("kv_ssq"), sem("misc_ready"), sem("kv_chain")
        gate_chain, gate_l_ready = sem("gate_chain"), sem("gate_l_ready")
        decay_ready = sem("decay_ready")
        score_zero, score_steps = sem("score_zero"), sem("score_steps")
        score_masked, topk_steps, mask_ready = sem("score_masked"), sem("topk_steps"), sem("mask_ready")
        wuv_landed = sem("wuv_landed")
        v_ready = sem("v_ready")
        level_diff, level_exp, level_ready = sem("level_diff"), sem("level_exp"), sem("level_ready")
        att_zero = sem("att_zero")
        dsa_steps, prob_ready, inv_ready = sem("dsa_steps"), sem("prob_ready"), sem("inv_ready")
        o_ssq, o_steps = sem("o_ssq"), sem("o_steps")
        gate_steps, merge_steps = sem("gate_steps"), sem("merge_steps")
        split_hi = sem("split_hi")
        gate_bias_landed = sem("gate_bias_landed")
        final_row_landed = sem("final_row_landed")
        x_again = sem("x_again")
        res_steps = sem("res_steps")
        norm_steps = sem("norm_steps")
        square_ready = sem("square_ready")
        out_ready, out_stored = sem("out_ready"), sem("out_stored")

        def raw_count(pos, p):
            if pos.first == JOINT:
                return (48 if p % RING < 2 else 16) * (p // RING + 1)
            return (192 if p % RING < 2 else 64) + 16 * (2 * (pos.n - 2) + p // RING + 1)

        def mod_of(pos):
            m = MOD_AT[pos.first] // PIECES
            return pos.i + m if pos.stride else m

        def halves(x, s):
            return x.rearrange("p (n two s) -> p n two s", two=2, s=s)

        def piece_no(pos, p):
            return p if pos.first == JOINT else PIECES * pos.n + p

        def later(pos, p):
            if p + AHEAD < PIECES:
                return pos, p + AHEAD
            return Pos(pos.first + 1, pos.i, pos.stride), p + AHEAD - PIECES

        def width(pos, p=0):
            return MISC if pos.first == JOINT and p % RING < 2 else W

        def h_psum(k, g):
            if k == 0:
                return pa, pa_full, pa_read, PA_AT[0] + g
            if g % 2 == 0:
                return pa, pa_full, pa_read, PA_AT[C_FF] + g // 2
            return pb, pb_full, pb_read, PB_AT[C_FF] + g // 2

        block = ctx.enter_context(nc.Block())

        @block.sync
        def _(sp):
            sp.dma_start(c_act[:, :], c_v).then_inc(c_landed, 16)

            def load_first_mod(n):
                m = MOD_ORDER[n]
                for q in range(PIECES):
                    piece = n * PIECES + q
                    if piece >= FIRST_RING:
                        before = piece - FIRST_RING
                        if by_gpsimd(before):
                            sp.wait_ge(mod_by_pool, pool_steps(before + 1))
                        else:
                            sp.wait_ge(mod_done, DVE_ROWS[before + 1])
                    sp.dma_start(m_first[:, piece % FIRST_RING, :, :],
                                 w_mod_v[:, q * PK:(q + 1) * PK, m * MW:(m + 1) * MW]).then_inc(
                                     mod_landed[piece % FIRST_RING], 16)

            def load(n, p, view, col, row=0):
                sp.wait_ge(lo_ready, PIECES * n + p - RING + 1)
                k = row + p * PK
                sp.dma_start(w_raw[:, p % RING, :, :], view[:, bass.ds(k, PK), bass.ds(col, W)]).then_inc(
                    raw_landed[p % RING], 16)

            for g in range(GROUPS):
                load_first_mod(2 * g)
                if g == 0:
                    for t in range(T):
                        sp.dma_start(xs[:, t, :], x_v[:, t, :]).then_inc(x_landed, 16)
                for s in range(RING):
                    if g:
                        sp.wait_ge(lo_ready, (g - 1) * RING + s + 1)
                    rows_ = slice((2 * g + s % 2) * PK, (2 * g + s % 2 + 1) * PK)
                    if s < 2:
                        for to, col, n in ((0, O_KV, LAT), (LAT, O_IK, D_IDX + H_IDX),
                                           (LAT + D_IDX + H_IDX, O_A, RANK)):
                            sp.dma_start(w_raw[:, s, :, to:to + n], w_in_v[:, rows_, col:col + n]).then_inc(
                                raw_landed[s], 16)
                    else:
                        sp.dma_start(w_raw[:, s, :, :], w_in_v[:, rows_, O_IQ:O_IQ + W]).then_inc(raw_landed[s], 16)
                load_first_mod(2 * g + 1)
            for first, count, col in ((C_IQ + 1, 1, O_IQ + W), (C_Q, 4, O_Q), (C_V, 4, O_V), (C_QL, 8, O_QLAT)):
                with sp.Fori(0, count) as i:
                    for p in range(PIECES):
                        load(i + first, p, w_in_v, i * W + col)
            with sp.Fori(0, H_GLA) as i:
                for p in range(PIECES):
                    load(i * 2 + C_RG, p, w_in_v, i * W + O_R)
                for p in range(PIECES):
                    load(i * 2 + (C_RG + 1), p, w_in_v, i * W + O_GG)
            with sp.Fori(0, D // W) as i:
                for p in range(PIECES):
                    load(i + C_GD, p, w_in_v, i * W + O_GD)
            with sp.Fori(0, D // W) as i:
                for p in range(PIECES):
                    load(i + C_WO, p, w_out_v, i * W)
            with sp.Fori(0, FF // D) as g:
                for j in range(D // W):
                    for p in range(PIECES):
                        load(g * 8 + (C_FF + j), p, w_ff1_v, g * D + j * W)
                for j in range(D // W):
                    for p in range(PIECES):
                        load(g * 8 + (C_FF + 4 + j), p, w_ff2_v, j * W, g * KT)
            for j in range(GROUPS):
                cols = slice(j * W, (j + 1) * W)
                sp.wait_ge(out_ready, j + 1)
                sp.dma_start(out_v[:, :, cols], normed[:, :, cols]).then_inc(out_stored, 16)
            sp.wait_ge(out_stored, 16 * GROUPS)
            sp.wait_ge(rows_stored, 16)

        @block.gpsimd
        def _(pool):
            pool.wait_ge(dve_setup, 3)
            for j in range(MOD_FIRST * PIECES):
                if not by_gpsimd(j):
                    continue
                n, q = divmod(j, PIECES)
                pool.wait_ge(mod_landed[j % FIRST_RING], 16 * (j // FIRST_RING + 1))
                if n >= 2:
                    pool.wait_ge(mod_pool_added, n - 1)
                done = pool_steps(j)
                if done:
                    pool.wait_ge(mod_by_pool, done)
                for a in range(PK):
                    k = q * PK + a
                    raw, to = m_first[:, j % FIRST_RING, a, :], m_sum_c[:, n % 2, :]
                    nc.gpsimd.tensor_scalar(m_product[:, :] if a else to, raw, c_act[:, k:k + 1], None,
                                            ALU.mult).then_inc(mod_by_pool, 1)
                pool.wait_ge(mod_by_pool, done + PK)
                nc.gpsimd.tensor_tensor(to, to, m_product[:, :], ALU.add).then_inc(mod_by_pool, 1)

            def load_mod(n, q, col):
                pool.wait_ge(mod_done, n * PK - ((RING - 1) * PK + POOL_ROWS))
                pool.dma_start(m_raw[:, q % RING, :, :],
                               w_mod_v[:, q * PK:(q + 1) * PK, bass.ds(col, MW)]).then_inc(mod_late[q % RING], 16)

            def load_mods(start, stop):
                for n in range(start, stop):
                    load_mod(n, n % PIECES, mod_at(n // PIECES) * MW)

            def load_gate_bias(at_, m):
                pool.dma_start(gates[:, bass.ds(at_, 1), :], b_mod[:, bass.ds(m * MW, MW)].rearrange(
                    "l (a n) -> l a n", a=1).to_broadcast([P, 1, MW])).then_inc(gate_bias_landed, 16)

            def load_mods_loop(first, last, gates_too=False):
                with pool.Fori(0, last - first + 1) as i:
                    for q in range(PIECES):
                        if gates_too and q == PIECES // 2:
                            pool.wait_ge(pb_read, PB_AT[20])
                            load_gate_bias(i + gate_slot(first), i + mod_at(first))
                        load_mod(i * PIECES + (first * PIECES + q), q, i * MW + mod_at(first) * MW)

            def mod_piece(c):
                return MOD_FIRST * PIECES + (c - MOD_FROM) * PIECES // 2

            pool.wait_ge(h_lo_ready, 2 * GROUPS)
            load_mods(mod_piece(MOD_FROM), mod_piece(4))
            pool.wait_ge(pa_full, PA_AT[1])
            for a in range(2):
                pool.dma_start(wuv[:, a, :, :], w_uv_v[:, a, :, :]).then_inc(wuv_landed, 16)

            pool.dma_start(bias_rows, rows[:, :].rearrange("h (a j) -> h a j", a=1).to_broadcast(
                [H_DSA, P, KEYS])).then_inc(rows_stored, 16)

            load_mods(mod_piece(4), mod_piece(6))
            pool.wait_ge(score_steps, 4 * H_IDX // 2)
            for t, (a, b) in enumerate(((0, P), (P, KEYS))):
                nc.gpsimd.affine_select(out=score[:, a:b], in_=score[:, a:b], compare_op=ALU.is_ge, fill=FILL,
                                        base=t * P, pattern=[[-1, b - a]], channel_multiplier=1).then_inc(
                                            score_masked, 1)
            load_mods(mod_piece(6), mod_piece(7))
            pool.wait_ge(topk_steps, 4 * (TOPK // 8) + 1)
            for t, (a, b) in enumerate(((0, P), (P, KEYS))):
                nc.gpsimd.affine_select(out=mask[:, a:b], in_=mask[:, a:b], compare_op=ALU.is_ge, fill=NEG,
                                        base=t * P, pattern=[[-1, b - a]], channel_multiplier=1).then_inc(
                                            mask_ready, 1)
            load_mods(mod_piece(7), mod_piece(8))
            load_mods_loop(mod_piece(8) // PIECES, mod_piece(10) // PIECES)
            load_mods(mod_piece(12), mod_piece(13))
            pool.wait_ge(rows_stored, 16)
            pool.wait_ge(pa_full, PA_AT[12])
            pool.wait_ge(pb_full, PB_AT[12])
            for half in range(2):
                src = bass.AP(tensor=bias_rows_h, offset=P - 1 + half * 8 * P * KEYS,
                              ap=[[KEYS - 1, P], [P * KEYS, 8], [1, S]])
                pool.dma_start(bias[:, 8 * half:8 * half + 8, :], src).then_inc(bias_landed, 16)
            load_mods(mod_piece(13), mod_piece(14))
            load_mods_loop(mod_piece(14) // PIECES, GATES_FROM - 1)
            load_gate_bias(gate_slot(GATES_FROM), mod_at(GATES_FROM))
            load_mods(GATES_FROM * PIECES, (GATES_FROM + 1) * PIECES)
            load_mods_loop(GATES_FROM + 1, GATES_FROM + GATE_BLOCKS // 2 - 1, gates_too=True)
            load_mods_loop(GATES_FROM + GATE_BLOCKS // 2, MODS - 2, gates_too=True)
            pool.wait_ge(merge_steps, 2 * (D // W))
            for t in range(T):
                pool.dma_start(xs[:, t, :], x_v[:, t, :]).then_inc(x_again, 16)
            load_gate_bias(gate_slot(MODS - 1), mod_at(MODS - 1))
            load_mods(mod_piece(C_WO + 1), MODS * PIECES)
            pool.dma_start(final_row[:, :], final_g.rearrange("(a n) -> a n", a=1).to_broadcast([P, D])).then_inc(
                final_row_landed, 16)

        @block.scalar
        def _(act):
            def high(pos, p):
                s = p % RING
                act.wait_ge(raw_landed[s], raw_count(pos, p))
                if not (pos.first == JOINT and p < RING):
                    act.wait_ge(pe_used, piece_no(pos, p - RING + 1))
                n = width(pos, p)
                nc.scalar.activation(w_hi[:, s, :, 0:n], w_raw[:, s, :, 0:n], ACT.Copy).then_inc(hi_ready, 1)

            act.wait_ge(c_landed, 16)
            nc.scalar.activation(c_tmp[:, 0, :], c_act[:, :], ACT.Exp, scale=-1.0).then_inc(act_setup, 1)
            mod_rows, g_rows = N_MOD * KT, KT
            for to, of in (
                (ident[:, :], ident_d), (masks[:, :, :].rearrange("p a b -> p (a b)"), masks_d),
                (onehot[:, :], onehot_d), (table[:, :], rel_bias),
                (vec_rows[0:mod_rows, :], b_mod.rearrange("l (a p) -> (l a) p", p=P)),
                (vec_rows[mod_rows:mod_rows + g_rows, :], norm1_g.rearrange("l (a p) -> (l a) p", p=P)),
                (vec_rows[mod_rows + g_rows:P, :], norm2_g.rearrange("l (a p) -> (l a) p", p=P)),
                (gate_rows[:, :], b_gate.rearrange("l (a p) -> (l a) p", p=P)),
                (gate_up[:, :], w_gate_up.rearrange("l r n -> (l r) n")),
                (kv_g[:, :], kv_norm_g.to_broadcast([P, LAT])),
                (gla_g[:, :], gla_norm_g.to_broadcast([P, DV])),
            ):
                act.dma_start(to, of).then_inc(consts_landed, 16)

            def take_root(of, n, ready, count):
                act.wait_ge(ready, count)
                nc.scalar.activation(root, of, ACT.Sqrt, bias=eps, scale=1.0 / n).then_inc(root_ready, 1)

            def part_squares(j, added=0):
                cols = slice(j * W, (j + 1) * W)
                for t in range(T):
                    if added:
                        act.wait_ge(res_steps, added + t - 1)
                    nc.scalar.activation(normed[:, t, cols], xs[:, t, cols], ACT.Square,
                                         accum_out=ssq_parts[:, t, j:j + 1]).then_inc(x_ssq, 1)

            def normalise(k):
                take_root(ssq_x, D, norm_steps, NORM_STEPS * k + 1)
                act.wait_ge(norm_steps, NORM_STEPS * (k + 1))
                for g in range(GROUPS):
                    cols = slice(g * W, (g + 1) * W)
                    nc.scalar.activation(normed[:, 1, cols], xs[:, 1, cols], ACT.Copy,
                                         scale=rin_x[:, 1:2]).then_inc(normed_ready[1], 1)
                    if k and g % 2:
                        h_high(k, g // 2)

            def h_high(k, g):
                ps, fulls, frees, use = h_psum(k, g)
                act.wait_ge(fulls, use + 1)
                act.wait_ge(scale_ready, k * GROUPS + g + 1)
                if k or g:
                    act.wait_ge(h_lo_ready, 2 * (k * GROUPS + g))
                for half in range(2):
                    for b in (2 * half, 2 * half + 1):
                        n = 4 * g + b
                        shift = mod_cols[:, 3 * KT * k + n:3 * KT * k + n + 1]
                        ins = nc.scalar.activation(full[:, b, :], ps[:, b // 2, (b % 2) * S:(b % 2 + 1) * S],
                                                   ACT.Identity, bias=shift, scale=h_scale[:, n:n + 1])
                        ins.then_inc(frees if b == 3 else h_full_ready, 1)
                    act.wait_ge(h_full_ready, 3 * (k * GROUPS + g) + 2 + half)
                    if half:
                        act.wait_ge(frees, use + 1)
                    t = slice(2 * half, 2 * half + 2)
                    nc.scalar.activation(h_hi[:, 4 * g + t.start:4 * g + t.stop, :].rearrange("p a s -> p (a s)"),
                                         full[:, t, :].rearrange("p a s -> p (a s)"), ACT.Copy).then_inc(h_hi_ready, 1)

            def take(pos, func, to=None):
                prev = pos.n - 1
                act.wait_ge(pe_used, PIECES * prev + PIECES)
                if pos.first == C_FF + 1:
                    act.wait_ge(h_lo_ready, 4 * GROUPS)
                if to is None:
                    to, done = z[:, :, :], z_full
                    if 20 <= pos.first <= 28:
                        act.wait_ge(gate_steps, pos.at(GATE_AT))
                    if pos.first > C_FF:
                        act.wait_ge(res_steps, pos.at(RES_AT) * 4)
                else:
                    done = v_ready
                a = acc[:, (pos.first - 1) % 2, :, :]
                return nc.scalar.activation(to, a, func), done

            def copy_pa(to, scale=1.0):
                return nc.scalar.activation(to.rearrange("p a s -> p (a s)"),
                                            pa[:, :, :].rearrange("p a w -> p (a w)"), ACT.Copy, scale=scale)

            def chunk(pos):
                c = pos.first
                for p in range(PIECES):
                    if p == 0 and (3 <= c <= 7 or 12 <= c <= 19 or is_gt_stage(c)
                                   or 20 <= c <= 27 or (c > C_FF and 1 <= group_slot(c) <= 4)):
                        func = (ACT.Sigmoid if 20 <= c <= 31 else ACT.Relu if c > C_FF else ACT.Copy)
                        ins, done = take(pos, func)
                        ins.then_inc(done, 1)
                    if p == 0 and 8 <= c <= 11:
                        ins, done = take(pos, ACT.Copy, v[:, :, (c - 8) * W:(c - 7) * W])
                        ins.then_inc(done, 1)
                    if p == 0 and c == C_FF:
                        part_squares_of(3, 1)
                        normalise(1)
                    at_, q = later(pos, p)
                    if at_.first < CHUNKS:
                        high(at_, q)
                    if c == C_FF and p in (1, 3):
                        h_high(1, 2 + p // 2)
                    if p == 2 and (C_WO + 1 <= c < C_FF or c > CHUNKS - 4):
                        part_squares_of(c - C_WO - 1 if c < C_FF else c - CHUNKS + 3, 1 + int(c > C_FF))
                    if p == 7 and c in (C_FF - 1, CHUNKS - 1):
                        nc.scalar.activation(st[:, 37:38], eps, ACT.Sqrt)
                    if c == 2:
                        if p == 0:
                            act.wait_ge(z_full, 1)
                            for t in range(T):
                                nc.scalar.activation(junk[:, t, 0:LAT], z[:, t, 0:LAT], ACT.Square,
                                                     accum_out=ssq_kv[:, t:t + 1]).then_inc(kv_ssq, 1)
                            take_root(ssq_kv, LAT, kv_ssq, T)
                        if p == 4:
                            act.wait_ge(pa_full, PA_AT[2] + 1)
                            nc.scalar.activation(kvt[:, :, :].rearrange("p a s -> p (a s)"), pa[:, 0, :], ACT.Copy)
                            nc.scalar.activation(ikt[:, :], pa[:, 1, 0:S], ACT.Copy)
                            nc.scalar.activation(a_t[:, :], pa[0:RANK, 1, S:2 * S], ACT.Copy).then_inc(pa_read, 1)
                        if p == 5:
                            act.wait_ge(kv_chain, ROOT_STEPS + T)
                            act.wait_ge(misc_ready, 1)
                            nc.scalar.activation(z[:, :, :], acc[:, 1, :, :], ACT.Copy).then_inc(z_full, 1)
                    if c == 3 and p == 7:
                        act.wait_ge(pb_read, PB_AT[2] + 1)
                        nc.scalar.activation(gate_e[:, :, :], gate_x[:, :, :], ACT.Abs).then_inc(gate_chain, 1)
                    if c == 5 and p == 1:
                        act.wait_ge(gate_chain, 1)
                        nc.scalar.activation(gate_e[:, :, :], gate_e[:, :, :], ACT.Exp,
                                             scale=-1.0).then_inc(gate_chain, 1)
                    if c == 5 and p == 4:
                        act.wait_ge(gate_chain, 2)
                        nc.scalar.activation(gate_e[:, :, :], gate_e[:, :, :], ACT.Ln,
                                             bias=1.0).then_inc(gate_l_ready, 1)
                    if 2 <= c <= 7 and p == (7 if c == 2 else 2):
                        act.wait_ge(pa_full, pos.at(PA_AT) + (3 if c == 2 else 1))
                        half = 4 * (c % 2)
                        to = (iqt, qt, kt)[(c - 2) // 2][:, half:half + 4, :]
                        if c == 6:
                            act.wait_ge(score_steps, 4 * H_IDX // 2)
                        ins = copy_pa(to, DK ** -0.5 if c in (4, 5) else 1.0)
                        ins.then_inc(pa_read, 1)
                    if c in (3, 4) and 3 <= p <= 6:
                        k = 4 * (c - 3) + p - 3
                        act.wait_ge(pb_full, PB_AT[3] + k + 1)
                        if k:
                            act.wait_ge(score_steps, 4 * k)
                        ins = nc.scalar.activation(relu[:, :, :], pb[:, :, 0:KEYS], ACT.Relu)
                        ins.then_inc(pb_read, 1)
                    if c in (5, 6) and p in (3, 5):
                        k = 2 * (c - 5) + (p - 3) // 2
                        act.wait_ge(pb_full, PB_AT[5] + k + 1)
                        act.wait_ge(rows_stored, 16)
                        ins = nc.scalar.activation(vals[:, :, k * W:(k + 1) * W], pb[:, :, :], ACT.Copy)
                        ins.then_inc(pb_read, 1)
                    if 8 <= c <= 11 and p in (1, 2):
                        k = 2 * (c - 8) + p - 1
                        act.wait_ge(level_diff, k + 1)
                        nc.scalar.activation(level[k % 2][:, :, :], level[k % 2][:, :, :], ACT.Exp,
                                             scale=1.0 / 16.0).then_inc(level_exp, 1)
                    if 12 <= c <= 19:
                        u = pos.n - 12
                        if p == 1:
                            act.wait_ge(pa_full, pos.at(PA_AT) + 1)
                            ins = copy_pa(q_lat[:, :, :])
                            ins.then_inc(pa_read, 1)
                        if p == 3 and c <= 15:
                            act.wait_ge(pa_full, pos.at(PA_AT) + 2)
                            for t in range(T):
                                nc.scalar.activation(junk[:, t, :], pa[:, t, :], ACT.Square,
                                                     accum_out=ssq_o[:, t:t + 1]).then_inc(o_ssq, 1)
                            take_root(ssq_o, DV, o_ssq, T * (c - 11))
                        if p == 4:
                            act.wait_ge(dsa_steps, u * DSA_STEPS + DSA_STEPS)
                            for e in range(2):
                                for t, (a, b) in enumerate(((0, P), (P, KEYS))):
                                    n = 2 * e + t
                                    nc.scalar.activation(logit[:, e, a:b], logit[:, e, a:b], ACT.Exp,
                                                         bias=neg_top[:, 2 * t + e:2 * t + e + 1],
                                                         accum_out=total[:, n:n + 1]).then_inc(prob_ready, 1)
                        last = 2 if c > 15 else 3
                        if p == 6:
                            act.wait_ge(pa_full, pos.at(PA_AT) + last)
                            ins = nc.scalar.activation(prob_t[:, :, :], pa[:, :, 0:KEYS], ACT.Copy)
                            ins.then_inc(pa_read, 1)
                        if p == 7:
                            act.wait_ge(pb_full, pos.at(PB_AT) + 2)
                            act.wait_ge(inv_ready, u + 1)
                            for e in range(2):
                                for t in range(T):
                                    n = 2 * e + t
                                    ins = nc.scalar.activation(y_dsa[:, t, bass.ds((u * 2 + e) * HD, HD)],
                                                               pb[:, 0, n * P:(n + 1) * P], ACT.Copy,
                                                               scale=inv_total[:, n:n + 1])
                            ins.then_inc(pb_read, 1)
                    if is_gt_stage(c) and p == 4:
                        j = c - 28
                        act.wait_ge(pa_full, pos.at(PA_AT) + 1)
                        copy_pa(m_hi[:, 4 * j:4 * j + 4, :]).then_inc(split_hi, 1)
                    if c > C_FF and 1 <= group_slot(c) <= 4 and p == 4:
                        j = group_slot(c) - 1
                        act.wait_ge(pa_full, pos.at(PA_AT) + 1)
                        copy_pa(u_hi[:, 4 * j:4 * j + 4, :]).then_inc(split_hi, 1)

            def part_squares_of(j, k):
                part_squares(j, 4 * (j + 1 + (GROUPS * GROUPS if k > 1 else 0)))

            act.wait_ge(x_landed, 16 * T)
            act.wait_ge(ones_ready, 1)
            for j in range(GROUPS):
                part_squares(j)
            for g in range(GROUPS):
                for s in range(RING):
                    high(Pos(JOINT), g * RING + s)
                if g == 0:
                    normalise(0)
                h_high(0, g)
            high(Pos(2), 0)
            high(Pos(2), 1)
            act.wait_ge(pe_used, 2 * PIECES - 2)
            act.wait_ge(h_lo_ready, 2 * GROUPS)
            nc.scalar.activation(z[:, :, 0:MISC], acc[:, 0, :, 0:MISC], ACT.Copy).then_inc(z_full, 1)
            high(Pos(2), 2)
            run_plan(act, chunk)
            part_squares_of(3, 2)
            take_root(ssq_x, D, norm_steps, NORM_STEPS * 2 + 1)

        @block.vector
        def _(dve):
            def low(pos, p):
                s = p % RING
                dve.wait_ge(hi_ready, piece_no(pos, p + 1))
                n = width(pos, p)
                nc.vector.tensor_tensor(w_lo[:, s, :, 0:n], w_raw[:, s, :, 0:n], w_hi[:, s, :, 0:n].bitcast(F32),
                                        ALU.subtract).then_inc(lo_ready, 1)

            def mod_add(count, j, sums=m_sum):
                q = j % PIECES
                r = q % RING
                raw, before = m_raw[:, r, :, :], count * PK - POOL_ROWS
                if j < MOD_FIRST * PIECES:
                    raw, before = m_first[:, j % FIRST_RING, :, :], DVE_ROWS[j]
                    dve.wait_ge(mod_landed[j % FIRST_RING], 16 * (j // FIRST_RING + 1))
                else:
                    dve.wait_ge(mod_late[r], count * (16 // RING) + (16 - (MOD_FIRST * PIECES + r) * (16 // RING)))
                for a in range(PK):
                    k = q * PK + a
                    s, b = raw[:, a, :], sums[:, a, :]
                    if q == 0:
                        ins = nc.vector.tensor_scalar(b, s, c_act[:, k:k + 1], None, ALU.mult)
                    else:
                        dve.wait_ge(mod_done, before + (a - 1))
                        if j < MOD_FIRST * PIECES and q == 7 and a == 0:
                            dve.wait_ge(mod_pool_added, j // PIECES + 1)
                        ins = nc.vector.scalar_tensor_tensor(b, s, c_act[:, k:k + 1], b, ALU.mult, ALU.add)
                    ins.then_inc(mod_done, 1)

            def mod_merge(count):
                dve.wait_ge(mod_done, count)
                nc.vector.tensor_tensor(m_sum[:, 0, :], m_sum[:, 0, :], m_sum[:, 1, :], ALU.add).then_inc(mod_merged, 1)

            def mod_take(m, ps, full_, free, use):
                dve.wait_ge(full_, use + 1)
                ins = nc.vector.tensor_tensor(mod_cols[:, bass.ds(m * MB, MB)], ps[:, 0, 0:MB],
                                              vec_cols[:, bass.ds(m * MB, MB)], ALU.add)
                ins.then_inc(free, 1)

            def gate_take(n, at_, use):
                row = gates[:, bass.ds(at_, 1), :].rearrange("p a n -> p (a n)")
                dve.wait_ge(pa_full, use + 1)
                dve.wait_ge(gate_bias_landed, n * 16 - 16 * (GATES_FROM - 1))
                nc.vector.tensor_tensor(row, pa[:, 0, :], row, ALU.add).then_inc(pa_read, 1)

            def inverse_root(of, to, n, count, step, start):
                mean, y, a = st[:, 30:30 + T], st[:, 32:32 + T], st[:, 34:34 + T]
                nc.vector.tensor_scalar(mean, of, 1.0 / n, EPS, ALU.mult, ALU.add).then_inc(step, 1)
                dve.wait_ge(root_ready, count)
                nc.vector.reciprocal(y, root).then_inc(step, 1)
                dve.wait_ge(step, start + 2)
                nc.vector.scalar_tensor_tensor(a, y, -0.5, mean, ALU.mult, ALU.mult).then_inc(step, 1)
                dve.wait_ge(step, start + 3)
                nc.vector.tensor_tensor(a, a, y, ALU.mult).then_inc(step, 1)
                dve.wait_ge(step, start + 4)
                nc.vector.scalar_tensor_tensor(to, a, 1.5, y, ALU.add, ALU.mult).then_inc(step, 1)

            def norm_root(k):
                dve.wait_ge(x_ssq, T * GROUPS * (k + 1))
                nc.vector.tensor_reduce(ssq_x, ssq_parts, AX_X, ALU.add).then_inc(norm_steps, 1)
                dve.wait_ge(norm_steps, NORM_STEPS * k + 1)
                inverse_root(ssq_x, rin_x, D, ROOT_X[k], norm_steps, NORM_STEPS * k + 1)
                dve.wait_ge(norm_steps, NORM_STEPS * (k + 1))

            def normalise(k, g):
                cols = slice(g * W, (g + 1) * W)
                nc.vector.tensor_scalar(normed[:, 0, cols], xs[:, 0, cols], rin_x[:, 0:1], None,
                                        ALU.mult).then_inc(normed_ready[0], 1)

            def h_low(k, g):
                for half in range(2):
                    dve.wait_ge(h_hi_ready, 2 * (k * GROUPS + g) + half + 1)
                    t, u = 2 * half, 4 * g + 2 * half
                    nc.vector.tensor_tensor(h_lo[:, u:u + 2, :].rearrange("p a s -> p (a s)"),
                                            full[:, t:t + 2, :].rearrange("p a s -> p (a s)"),
                                            h_hi[:, u:u + 2, :].rearrange("p a s -> p (a s)").bitcast(F32),
                                            ALU.subtract).then_inc(h_lo_ready, 1)

            def h_scales(k, first, last):
                a, b = 4 * first, 4 * (last + 1)
                sc = mod_cols[:, (3 * k + 1) * KT + a:(3 * k + 1) * KT + b]
                g = vec_cols[:, (N_MOD + k) * KT + a:(N_MOD + k) * KT + b]
                return nc.vector.scalar_tensor_tensor(h_scale[:, a:b], sc, 1.0, g, ALU.add, ALU.mult)

            def level_start(k):
                e = level[k % 2]
                if k >= 2:
                    dve.wait_ge(*((pa_full, PA_AT[7 + k // 2] + 1) if k % 2 == 0 else
                                  (pb_full, PB_AT[8] + 1 + k // 2)))
                if k < len(LEVELS):
                    s = LEVELS[k]
                    b4 = cum[:, :, :].rearrange("p a (n two s) -> p (a n) two s", two=2, s=s)
                    e4 = e[:, :, :].rearrange("p a (n two s) -> p (a n) two s", two=2, s=s)
                    mid = b4[:, :, 0, s - 1:s].to_broadcast([P, 8 * S // (2 * s), s])
                    nc.vector.tensor_tensor(e4[:, :, 0, :], mid, b4[:, :, 0, :], ALU.subtract)
                    ins = nc.vector.tensor_tensor(e4[:, :, 1, :], b4[:, :, 1, :], mid, ALU.subtract)
                else:
                    mid = cum[:, :, P - 1:P].to_broadcast([P, 8, P])
                    nc.vector.tensor_tensor(e[:, :, 0:P], mid, cum[:, :, 0:P], ALU.subtract)
                    ins = nc.vector.tensor_copy(e[:, :, P:S], cum[:, :, P:S])
                ins.then_inc(level_diff, 1)

            def level_scale(k):
                dve.wait_ge(level_exp, k + 1)
                s = (LEVELS + [P])[k]
                e4, k4, q4 = (y[:, :, :].rearrange("p a (n two s) -> p (a n) two s", two=2, s=s)
                              for y in (level[k % 2], kt, qt))
                nc.vector.tensor_tensor(e4[:, :, 0, :], e4[:, :, 0, :], k4[:, :, 0, :], ALU.mult)
                nc.vector.tensor_tensor(e4[:, :, 1, :], e4[:, :, 1, :], q4[:, :, 1, :], ALU.mult).then_inc(
                    level_ready, 1)

            def level_take(n, ps, frees, fulls, use, before):
                dve.wait_ge(fulls, use + 1)
                before()
                a = att[:, :, :, :].rearrange("p h t i -> p (h t) i")
                if n == 0:
                    m = masks[:, 0:1, :].to_broadcast([P, H_GLA * T, P])
                    of = ps[:, :, :].rearrange("p a (b i) -> p (a b) i", i=P)
                else:
                    s = LEVELS[n - 1]
                    a = a.rearrange("p b (n two s) -> p (b n) two s", two=2, s=s)[:, :, 1, :]
                    blocks = P // (2 * s)
                    m = (masks[:, n, 0:P // 2].rearrange("p (b n s) -> p b n s", b=1, s=s)
                         .to_broadcast([P, H_GLA * T, blocks, s]))
                    of = ps[:, 0, :].rearrange("p (b n s) -> p b n s", n=blocks, s=s)
                    a = a.rearrange("p (b n) s -> p b n s", n=blocks)
                ins = nc.vector.copy_predicated(a, m, of)
                ins.then_inc(frees, 1)

            def chunk(pos):
                c = pos.first
                for p in range(PIECES):
                    if c > C_WO and c != C_FF and (c < C_FF or group_slot(c) in (0, 5, 6, 7)) and p == 0:
                        add_result(pos)
                    if c == C_FF and p == 0:
                        add_result(pos)
                        dve.wait_ge(pa_read, PA_AT[C_FF])
                        h_scales(1, 0, GROUPS - 1).then_inc(scale_ready, GROUPS)
                        norm_root(1)
                        for g in range(GROUPS):
                            normalise(1, g)
                        h_low(1, 0)
                    at_, q = later(pos, p)
                    if at_.first < CHUNKS:
                        low(at_, q)
                    if c == C_FF and p in (0, 1, 3):
                        h_low(1, (p + 3) // 2)
                    if c == 2:
                        misc_side(p)
                    if c == 6 and p == 5:
                        dve.wait_ge(gate_l_ready, 1)
                        nc.vector.scalar_tensor_tensor(gate_x[:, :, :], gate_x[:, :, :], 0.0, gate_e[:, :, :],
                                                       ALU.min, ALU.subtract).then_inc(gate_chain, 1)
                    if c == 6 and p == 6:
                        dve.wait_ge(gate_chain, 3)
                        for b in range(8):
                            for t in range(T):
                                ins = nc.vector.tensor_tensor_scan(cum[:, b, t * P:(t + 1) * P], ones[:, :],
                                                                   gate_x[:, b, t * P:(t + 1) * P], 0.0,
                                                                   ALU.mult, ALU.add)
                        ins.then_inc(decay_ready, 1)
                    if c in (3, 4) and 3 <= p <= 6:
                        k = 4 * (c - 3) + p - 3
                        dve.wait_ge(pb_read, PB_AT[3] + k + 1)
                        for e in range(2):
                            for t, (a, b) in enumerate(((0, P), (P, KEYS))):
                                n = 4 * k + 2 * e + t
                                if n >= 2:
                                    dve.wait_ge(score_steps, n - 1)
                                nc.vector.scalar_tensor_tensor(
                                    score[:, a:b], relu[:, e, a:b], iw[:, t, 2 * k + e:2 * k + e + 1],
                                    score[:, a:b], ALU.mult, ALU.add).then_inc(score_steps, 1)
                    if c == 5:
                        topk_round(p)
                        if p == 7:
                            dve.wait_ge(topk_steps, 4 * (TOPK // 8))
                            nc.vector.tensor_scalar(mask[:, :], left[1][:, :], BETWEEN, NEG, ALU.is_gt,
                                                    ALU.mult).then_inc(topk_steps, 1)
                    for n in range(4):
                        if mod_ops(c) and mod_slots(c)[n] == p:
                            mod_add(pos.at(MOD_AT) + n, MOD_AT[c] + n)
                            if mod_ends(c) and n == 3:
                                mod_merge(pos.at(MOD_AT) * PK + (4 * PK - POOL_ROWS))
                    if mod_ends(c) and p == 7:
                        use = pos.at(PA_AT) + pa_uses(c) - 1
                        if MOD_AT[c] // PIECES < GATES_FROM:
                            mod_take(mod_at(MOD_AT[c] // PIECES), pa, pa_full, pa_read, use)
                        else:
                            gate_take(mod_of(pos), pos.i + gate_slot(MOD_AT[c] // PIECES), use)
                    if 8 <= c <= 11:
                        a, b = 2 * (c - 8), 2 * (c - 8) + 1
                        if p == 0:
                            if c == 8:
                                nc.vector.memset(att[:, :, :, :], 0.0).then_inc(att_zero, 1)
                                dve.wait_ge(pa_read, PA_AT[8])
                                dve.wait_ge(decay_ready, 1)
                            level_start(a)
                        if p == 1:
                            level_start(b)
                            if c == 8:
                                level_take(0, pb, pb_read, pb_full, PB_AT[8], lambda: dve.wait_ge(att_zero, 1))
                        if p == 2:
                            level_scale(a)
                        if p == 3:
                            level_scale(b)
                        if p == 6:
                            level_take(1 + a, pa, pa_read, pa_full, PA_AT[c],
                                       lambda: dve.wait_ge(pb_read, PB_AT[c] + int(c == 8)))
                        if p == 7:
                            use = PB_AT[c] + int(c == 8)
                            if c < 11:
                                level_take(1 + b, pb, pb_read, pb_full, use,
                                           lambda: dve.wait_ge(pa_read, PA_AT[c] + 1))
                            else:
                                dve.wait_ge(pb_full, use + 1)
                                ins = nc.vector.tensor_copy(att_far[:, :, :].rearrange("p h i -> p (h i)"), pb[:, 0, :])
                                ins.then_inc(pb_read, 1)
                    if 12 <= c <= 19:
                        dsa_side(pos, p)
                    if 20 <= c <= 27:
                        gate_side(pos, p)
                    if is_gt_stage(c):
                        merge_side(pos, p)
                    if c > C_FF and 1 <= group_slot(c) <= 4:
                        j = group_slot(c) - 1
                        if p == 1:
                            dve.wait_ge(z_full, pos.at(ZF_AT) + 1)
                            nc.vector.tensor_tensor(z[:, :, :], z[:, :, :], z[:, :, :], ALU.mult).then_inc(
                                square_ready, 1)
                        if p == 4:
                            split_low(pos, u_hi, u_lo, j)

            def split_low(pos, hi, lo, j):
                dve.wait_ge(split_hi, pos.at(SPLIT_AT) + 1)
                ins = nc.vector.tensor_tensor(
                    lo[:, 4 * j:4 * j + 4, :].rearrange("p a s -> p (a s)"),
                    pa[:, :, :].rearrange("p a w -> p (a w)"),
                    hi[:, 4 * j:4 * j + 4, :].rearrange("p a s -> p (a s)").bitcast(F32), ALU.subtract)
                ins.then_inc(pa_read, 1)

            def add_result(pos):
                prev = pos.n - 1
                c = pos.first - 1
                j = c - C_WO if c < C_FF else group_slot(c) - 4
                row = gates[:, gate_slot(GATES_FROM + j + (GATE_BLOCKS // 2 if c < C_FF else 0)), :]
                dve.wait_ge(pe_used, PIECES * prev + PIECES)
                if c == C_WO:
                    dve.wait_ge(x_again, 16 * T)
                if c < C_FF:
                    dve.wait_ge(pa_read, PA_AT[28 + 2 * j])
                if c > C_WO:
                    dve.wait_ge(res_steps, pos.at(RES_AT) * 4)
                cols = slice(j * W, (j + 1) * W)
                for t in range(T):
                    nc.vector.tensor_tensor(z[:, t, :], acc[:, c % 2, t, :], row, ALU.mult).then_inc(res_steps, 1)
                for t in range(T):
                    dve.wait_ge(res_steps, 4 * pos.at(RES_AT) + t + 1)
                    nc.vector.tensor_tensor(xs[:, t, cols], xs[:, t, cols], z[:, t, :], ALU.add).then_inc(res_steps, 1)

            def misc_side(p):
                if p == 0:
                    dve.wait_ge(z_full, 1)
                    dve.wait_ge(normed_ready[1], GROUPS)
                    nc.vector.tensor_copy(ik2[:, :, 0:D_IDX], z[:, :, LAT:LAT + D_IDX])
                    nc.vector.tensor_copy(ik2[:, :, D_IDX:2 * D_IDX], z[:, :, LAT:LAT + D_IDX])
                    nc.vector.tensor_scalar(iw[:, :, :], z[:, :, LAT + D_IDX:LAT + D_IDX + H_IDX],
                                            (H_IDX * D_IDX) ** -0.5, None, ALU.mult).then_inc(misc_ready, 1)
                    nc.vector.memset(score[:, :], 0.0).then_inc(score_zero, 1)
                    dve.wait_ge(kv_ssq, T)
                    inverse_root(ssq_kv, rin_kv, LAT, ROOT_KV, kv_chain, 0)
                    dve.wait_ge(kv_chain, ROOT_STEPS)
                    for t in range(T):
                        nc.vector.scalar_tensor_tensor(kvn[:, t, :], z[:, t, 0:LAT], rin_kv[:, t:t + 1], kv_g[:, :],
                                                       ALU.mult, ALU.mult).then_inc(kv_chain, 1)
                if p == 6:
                    dve.wait_ge(pa_full, PA_AT[2] + 2)
                    dve.wait_ge(pb_full, PB_AT[2] + 1)
                    for b in range(8):
                        ps = (pa, pb)[b // 4][:, b % 4 // 2, (b % 2) * S:(b % 2 + 1) * S]
                        ins = nc.vector.tensor_scalar(gate_x[:, b, :], ps, gate_cols[:, b:b + 1], None, ALU.add)
                        if b == 3:
                            ins.then_inc(pa_read, 1)
                    ins.then_inc(pb_read, 1)

            def topk_round(r):
                of, to = (score if r == 0 else left[(r + 1) % 2]), left[r % 2]
                if r == 0:
                    dve.wait_ge(score_masked, 2)
                else:
                    dve.wait_ge(topk_steps, 4 * r)
                for t, (a, b) in enumerate(((0, P), (P, KEYS))):
                    nc.vector.max(top8[:, t, :], of[:, a:b]).then_inc(topk_steps, 1)
                for t, (a, b) in enumerate(((0, P), (P, KEYS))):
                    dve.wait_ge(topk_steps, 4 * r + t + 1)
                    nc.vector.match_replace(to[:, a:b], top8[:, t, :], of[:, a:b], TAKEN).then_inc(topk_steps, 1)

            def dsa_side(pos, p):
                u = pos.n - 12
                base_ = u * DSA_STEPS
                if p == 2:
                    dve.wait_ge(pb_full, pos.at(PB_AT) + 1)
                    if pos.first == 12:
                        dve.wait_ge(bias_landed, 32)
                        dve.wait_ge(mask_ready, 2)
                    for e in range(2):
                        h = u * 2 + e
                        nc.vector.scalar_tensor_tensor(logit[:, e, 0:P], pb[:, e, 0:P], LAT ** -0.5,
                                                       one_head(bias, h, P, S), ALU.mult, ALU.add).then_inc(dsa_steps, 1)
                        ins = nc.vector.scalar_tensor_tensor(logit[:, e, P:KEYS], pb[:, e, P:KEYS], LAT ** -0.5,
                                                             one_head(bias, h, 0, S), ALU.mult, ALU.add)
                        ins.then_inc(pb_read if e else dsa_steps, 1)
                    dve.wait_ge(dsa_steps, base_ + 3)
                    dve.wait_ge(pb_read, pos.at(PB_AT) + 1)
                    nc.vector.tensor_tensor(logit[:, :, :], logit[:, :, :],
                                            mask[:, :].rearrange("p (a k) -> p a k", a=1).to_broadcast([P, 2, KEYS]),
                                            ALU.add).then_inc(dsa_steps, 1)
                    dve.wait_ge(dsa_steps, base_ + 4)
                    for t, (a, b) in enumerate(((0, P), (P, KEYS))):
                        nc.vector.tensor_reduce(neg_top[:, 2 * t:2 * t + 2], logit[:, :, a:b], AX_X, ALU.max,
                                                negate=True).then_inc(dsa_steps, 1)
                if p == 4 and pos.first <= 15:
                    g = pos.first - 12
                    dve.wait_ge(o_ssq, T * (g + 1))
                    inverse_root(ssq_o, rin_o, DV, ROOT_O + g, o_steps, ROOT_STEPS * g)
                    dve.wait_ge(o_steps, ROOT_STEPS * (g + 1))
                    for t in range(T):
                        ins = nc.vector.scalar_tensor_tensor(v[:, t, g * DV:(g + 1) * DV], pa[:, t, :],
                                                             rin_o[:, t:t + 1], gla_g[:, :], ALU.mult, ALU.mult)
                        if g == H_GLA - 1 and t == 0:
                            ins.then_inc(gate_steps, 1)
                    ins.then_inc(pa_read, 1)
                if p == 5:
                    dve.wait_ge(prob_ready, (u + 1) * 4)
                    nc.vector.reciprocal(inv_total, total).then_inc(inv_ready, 1)

            def one_head(t, h, a, b):
                return t[:, bass.ds(h, 1), a:b].rearrange("p a s -> p (a s)")

            def gate_side(pos, p):
                j = pos.i
                even = pos.first % 2 == 0
                done = pos.at(GATE_AT)
                if p == 0:
                    dve.wait_ge(z_full, pos.at(ZF_AT) + 1)
                    dve.wait_ge(pa_read, PA_AT[16])
                    if even:
                        ins = nc.vector.tensor_tensor(z[:, :, :], acc[:, (pos.first - 1) % 2, :, :], z[:, :, :],
                                                      ALU.mult)
                        ins.then_inc(gate_steps, 1)
                        dve.wait_ge(gate_steps, done + 1)
                    y = v[:, :, bass.ds(j * W, W)]
                    ins = nc.vector.tensor_tensor(y, y, z[:, :, :], ALU.mult)
                    ins.then_inc(gate_steps, 1)

            def merge_side(pos, p):
                j = pos.first - 28
                if p == 0:
                    dve.wait_ge(z_full, pos.at(ZF_AT) + 1)
                    if j == 0:
                        dve.wait_ge(pb_read, PB_AT[20])
                        dve.wait_ge(gate_steps, GATE_AT[28])
                    y, cols = y_dsa[:, :, j * W:(j + 1) * W], slice(j * W, (j + 1) * W)
                    nc.vector.tensor_tensor(y, y, z[:, :, :], ALU.mult).then_inc(merge_steps, 1)
                    dve.wait_ge(merge_steps, 2 * j + 1)
                    nc.vector.tensor_tensor(z[:, :, :], v[:, :, cols], y, ALU.add).then_inc(merge_steps, 1)
                if p == 4:
                    split_low(pos, m_hi, m_lo, j)

            nc.vector.memset(eps, EPS)
            nc.vector.memset(ones[:, :], 1.0).then_inc(ones_ready, 1)
            dve.wait_ge(act_setup, 1)
            nc.vector.tensor_scalar(c_tmp[:, 1, :], c_tmp[:, 0, :], 1.0, None, ALU.add).then_inc(dve_setup, 1)
            dve.wait_ge(dve_setup, 1)
            nc.vector.reciprocal(c_tmp[:, 2, :], c_tmp[:, 1, :]).then_inc(dve_setup, 1)
            dve.wait_ge(dve_setup, 2)
            nc.vector.tensor_tensor(c_act[:, :], c_act[:, :], c_tmp[:, 2, :], ALU.mult).then_inc(dve_setup, 1)
            dve.wait_ge(dve_setup, 3)

            def first_mods(n, start, stop):
                sums = (m_sum_b, m_sum)[n % 2]
                for q in range(start, stop):
                    if not by_gpsimd(n * PIECES + q):
                        mod_add(n * PIECES + q, n * PIECES + q, sums)
                    if q == 6:
                        dve.wait_ge(mod_by_pool, pool_steps((n + 1) * PIECES))
                        dve.wait_ge(mod_done, DVE_ROWS[n * PIECES + q + 1] - 1)
                        nc.vector.tensor_tensor(sums[:, 0, :], sums[:, 0, :], m_sum_c[:, n % 2, :], ALU.add).then_inc(
                            mod_pool_added, 1)
                if stop == PIECES:
                    dve.wait_ge(mod_done, DVE_ROWS[(n + 1) * PIECES])
                    nc.vector.tensor_tensor(sums[:, 0, :], sums[:, 0, :], sums[:, 1, :], ALU.add).then_inc(mod_merged, 1)

            first_mods(0, 0, PIECES)
            dve.wait_ge(pa_full, 1)
            nc.vector.tensor_copy(vec_cols[:, :], pa[:, 0, 0:P])
            ins = nc.vector.tensor_copy(gate_cols[:, :], pa[:, 1, 0:8])
            ins.then_inc(pa_read, 1)
            dve.wait_ge(pb_full, 1)
            ins = nc.vector.tensor_copy(rows[:, :], pb[0:H_DSA, 0, 0:KEYS])
            ins.then_inc(pb_read, 1)
            for g in range(GROUPS):
                if g:
                    first_mods(2 * g, 3, PIECES)
                for s in range(RING):
                    if s == RING - 1:
                        low(Pos(JOINT), g * RING + s)
                    first_mods(2 * g + 1, 2 * s, 2 * s + 2)
                    if g == 0 and s == 1:
                        norm_root(0)
                        for j in range(GROUPS):
                            normalise(0, j)
                    if s < RING - 1:
                        low(Pos(JOINT), g * RING + s)
                    if s == 1:
                        dve.wait_ge(pa_read, 1)
                        mod_take(MOD_ORDER[2 * g], pb, pb_full, pb_read, PB_AT[0] + 2 * g)
                mod_take(MOD_ORDER[2 * g + 1], pb, pb_full, pb_read, PB_AT[0] + 2 * g + 1)
                dve.wait_ge(pb_read, PB_AT[0] + 2 * g + 2)
                h_scales(0, g, g).then_inc(scale_ready, 1)
                if g < GROUPS - 1:
                    first_mods(2 * g + 2, 0, 3)
                h_low(0, g)
            for p in range(AHEAD):
                low(Pos(2), p)
            run_plan(dve, chunk)
            add_result(Pos(CHUNKS))
            norm_root(2)
            dve.wait_ge(final_row_landed, 16)
            for j in range(GROUPS):
                cols = slice(j * W, (j + 1) * W)
                for t in range(T):
                    ins = nc.vector.scalar_tensor_tensor(normed[:, t, cols], xs[:, t, cols], rin_x[:, t:t + 1],
                                                         final_row[:, cols], ALU.mult, ALU.mult)
                ins.then_inc(out_ready, 1)

        @block.tensor
        def _(pe):
            def transpose_h(k, g):
                ps, fulls, frees, use = h_psum(k, g)
                pe.wait_ge(frees, use)
                for t in range(T):
                    pe.wait_ge(normed_ready[t], k * GROUPS + g + 1)
                for b in range(4):
                    for t in range(T):
                        n = 4 * g + b
                        ins = nc.tensor.transpose(ps[:, b // 2, (b % 2) * S + t * P:(b % 2) * S + (t + 1) * P],
                                                  normed[:, t, n * P:(n + 1) * P], ident[:, :])
                ins.then_inc(fulls, 1)

            def first_mod(n):
                pe.wait_ge(mod_merged, n + 1)
                pe.wait_ge(pb_read, PB_AT[0] + n)
                sums = (m_sum_b, m_sum)[n % 2]
                for b in range(MB):
                    ins = nc.tensor.matmul(pb[:, 0, b:b + 1], sums[:, 0, b * P:(b + 1) * P], ones[:, 0:1],
                                           start=True, stop=True)
                ins.then_inc(pb_full, 1)

            def sum_mod(count, use):
                pe.wait_ge(mod_merged, count)
                pe.wait_ge(pa_read, use)
                for b in range(MB):
                    ins = nc.tensor.matmul(pa[:, 0, b:b + 1], m_sum[:, 0, b * P:(b + 1) * P], ones[:, 0:1],
                                           start=True, stop=True)
                ins.then_inc(pa_full, 1)

            def transpose_z(pos, used=0):
                pe.wait_ge(pa_read, pos.at(PA_AT) + used)
                for b in range(4):
                    for t in range(T):
                        ins = nc.tensor.transpose(pa[:, b // 2, (b % 2) * S + t * P:(b % 2) * S + (t + 1) * P],
                                                  z[:, t, b * P:(b + 1) * P], ident[:, :])
                ins.then_inc(pa_full, 1)

            def level_product(k):
                ps, frees, fulls, use = ((pa, pa_read, pa_full, PA_AT[8 + k // 2]) if k % 2 == 0 else
                                         (pb, pb_read, pb_full, PB_AT[8 + k // 2] + int(k == 1)))
                pe.wait_ge(level_ready, k + 1)
                pe.wait_ge(frees, use)
                e = level[k % 2]
                far = k == len(LEVELS)
                for h in range(H_GLA):
                    for t in range(1 if far else T):
                        n, size = (h, P) if far else (h * T + t, P // 2)
                        to = ps[:, 0, n * size:(n + 1) * size]
                        for a in range(2):
                            d = 2 * h + a
                            if far:
                                right = e[:, d, P:S]
                            else:
                                right = halves(e[:, d, t * P:(t + 1) * P], LEVELS[k])[:, :, 1, :]
                                to = to if a else to.rearrange("p (n s) -> p n s", s=LEVELS[k])
                            ins = nc.tensor.matmul(to, e[:, d, t * P:(t + 1) * P], right, start=(a == 0), stop=(a == 1))
                ins.then_inc(fulls, 1)

            def diagonal_product():
                pe.wait_ge(pa_read, PA_AT[8])
                pe.wait_ge(pb_read, PB_AT[8])
                for n in range(H_GLA * T):
                    h, t = divmod(n, T)
                    for a in range(2):
                        d = 2 * h + a
                        ins = nc.tensor.matmul(pb[:, n // 4, (n % 4) * P:(n % 4 + 1) * P],
                                               kt[:, d, t * P:(t + 1) * P], qt[:, d, t * P:(t + 1) * P],
                                               start=(a == 0), stop=(a == 1))
                ins.then_inc(pb_full, 1)

            def sums_read(pos):
                c = pos.first - 1
                if 8 <= c <= 11:
                    pe.wait_ge(v_ready, c - 7)
                elif 20 <= c <= 27 and c % 2 == 0:
                    pe.wait_ge(gate_steps, pos.at(GATE_AT))
                elif C_WO < c <= C_FF or (c > C_FF and group_slot(c) not in (1, 2, 3, 4)):
                    pe.wait_ge(res_steps, pos.at(RES_AT) * 4)
                else:
                    pe.wait_ge(z_full, pos.at(ZF_AT))

            def side(pos, p):
                c = pos.first
                if c == C_FF and p in (1, 2):
                    transpose_h(1, p + 1)
                if c == 2 and p == 4:
                    pe.wait_ge(misc_ready, 1)
                    pe.wait_ge(kv_chain, ROOT_STEPS + T)
                    pe.wait_ge(pa_read, PA_AT[2])
                    for t in range(T):
                        cols = slice(t * P, (t + 1) * P)
                        for a in range(2):
                            nc.tensor.transpose(pa[:, 0, a * S + t * P:a * S + (t + 1) * P],
                                                kvn[:, t, a * P:(a + 1) * P], ident[:, :])
                        nc.tensor.transpose(pa[:, 1, cols], ik2[:, t, :], ident[:, :])
                        ins = nc.tensor.transpose(pa[0:RANK, 1, S + t * P:S + (t + 1) * P],
                                                  z[:, t, MISC - RANK:MISC], ident[:, :])
                    ins.then_inc(pa_full, 1)
                if c == 2 and p == 6:
                    pe.wait_ge(pa_read, PA_AT[2] + 1)
                    pe.wait_ge(pb_read, PB_AT[2])
                    for b in range(8):
                        ins = nc.tensor.matmul((pa, pb)[b // 4][:, b % 4 // 2, (b % 2) * S:(b % 2 + 1) * S],
                                               gate_up[:, b * P:(b + 1) * P], a_t[:, :], start=True, stop=True)
                        if b == 3:
                            ins.then_inc(pa_full, 1)
                    ins.then_inc(pb_full, 1)
                if 2 <= c <= 7 and p == (7 if c == 2 else 2):
                    pe.wait_ge(z_full, pos.at(ZF_AT) + 1)
                    transpose_z(pos, 2 if c == 2 else 0)
                if c in (3, 4) and 3 <= p <= 6:
                    k = 4 * (c - 3) + p - 3
                    pe.wait_ge(pa_read, PA_AT[c])
                    pe.wait_ge(pb_read, PB_AT[3] + k)
                    for e in range(2):
                        rows_ = slice(e * D_IDX, (e + 1) * D_IDX)
                        nc.tensor.matmul(pb[:, e, 0:P], iqt[rows_, k, 0:P], ikt[rows_, 0:P], start=True, stop=True)
                        ins = nc.tensor.matmul(pb[:, e, P:KEYS], iqt[rows_, k, P:S], ikt[rows_, 0:S],
                                               start=True, stop=True)
                    ins.then_inc(pb_full, 1)
                if c in (5, 6) and p in (3, 5):
                    k = 2 * (c - 5) + (p - 3) // 2
                    pe.wait_ge(wuv_landed, 32)
                    pe.wait_ge(pb_read, PB_AT[5] + k)
                    for t in range(T):
                        for a in range(2):
                            ins = nc.tensor.matmul(pb[:, t, :], kvt[:, a, t * P:(t + 1) * P],
                                                   wuv[:, a, 4 * k:4 * k + 4, :].rearrange("p h d -> p (h d)"),
                                                   start=(a == 0), stop=(a == 1))
                    ins.then_inc(pb_full, 1)
                if mod_ends(c) and p == 7 and MOD_AT[c] // PIECES >= GATES_FROM:
                    pe.wait_ge(mod_merged, mod_of(pos) + 1)
                    pe.wait_ge(pa_read, pos.at(PA_AT) + pa_uses(c) - 1)
                    nc.tensor.matmul(pa[:, 0, :], ones[:, :], m_sum[:, 0, :], start=True, stop=True).then_inc(pa_full, 1)
                elif mod_ends(c) and p == 7:
                    sum_mod(mod_of(pos) + 1, pos.at(PA_AT) + pa_uses(c) - 1)
                if 8 <= c <= 11:
                    if c == 8 and p == 1:
                        diagonal_product()
                    if p == 5:
                        level_product(2 * (c - 8))
                    if p == 6:
                        level_product(2 * (c - 8) + 1)
                if 12 <= c <= 19:
                    dsa(pos, p)
                if is_gt_stage(c) and p == 3:
                    pe.wait_ge(merge_steps, 2 * (c - 28) + 2)
                    transpose_z(pos)
                if c > C_FF and 1 <= group_slot(c) <= 4 and p == 3:
                    pe.wait_ge(square_ready, pos.at(FF1_AT) + 1)
                    transpose_z(pos)

            def dsa(pos, p):
                c = pos.first
                u = pos.n - 12
                if p == 1:
                    pe.wait_ge(z_full, pos.at(ZF_AT) + 1)
                    transpose_z(pos)
                if p == 2:
                    pe.wait_ge(pa_read, pos.at(PA_AT) + 1)
                    pe.wait_ge(pb_read, pos.at(PB_AT))
                    for e in range(2):
                        for t, (a, b) in enumerate(((0, P), (P, KEYS))):
                            for m in range(2):
                                ins = nc.tensor.matmul(pb[:, e, a:b], q_lat[:, 2 * e + m, t * P:(t + 1) * P],
                                                       kvt[:, m, 0:b - a], start=(m == 0), stop=(m == 1))
                    ins.then_inc(pb_full, 1)
                if p == 3 and c <= 15:
                    g = c - 12
                    cols = slice(g * DV, (g + 1) * DV)
                    pe.wait_ge(v_ready, 4)
                    pe.wait_ge(pb_read, PB_AT[12])
                    pe.wait_ge(pa_read, PA_AT[c] + 1)
                    nc.tensor.matmul(pa[:, 0, :], att[:, g, 0, :], v[:, 0, cols], start=True, stop=True)
                    nc.tensor.matmul(pa[:, 1, :], att_far[:, g, :], v[:, 0, cols], start=True, stop=False)
                    nc.tensor.matmul(pa[:, 1, :], att[:, g, 1, :], v[:, 1, cols], start=False,
                                     stop=True).then_inc(pa_full, 1)
                if p == 6:
                    pe.wait_ge(prob_ready, (u + 1) * 4)
                    pe.wait_ge(pa_read, pos.at(PA_AT) + (2 if c <= 15 else 1))
                    for e in range(2):
                        for b in range(3):
                            ins = nc.tensor.transpose(pa[:, e, b * P:(b + 1) * P], logit[:, e, b * P:(b + 1) * P],
                                                      ident[:, :])
                    ins.then_inc(pa_full, 1)
                if p == 7:
                    pe.wait_ge(pa_read, pos.at(PA_AT) + (3 if c <= 15 else 2))
                    pe.wait_ge(pb_read, pos.at(PB_AT) + 1)
                    for e in range(2):
                        def value(t):
                            return vals[:, t, bass.ds((u * 2 + e) * HD, HD)]

                        n = 2 * e
                        nc.tensor.matmul(pb[:, 0, n * P:(n + 1) * P], prob_t[:, e, 0:P], value(0), start=True, stop=True)
                        nc.tensor.matmul(pb[:, 0, (n + 1) * P:(n + 2) * P], prob_t[:, e, P:2 * P], value(0),
                                         start=True, stop=False)
                        ins = nc.tensor.matmul(pb[:, 0, (n + 1) * P:(n + 2) * P], prob_t[:, e, 2 * P:KEYS], value(1),
                                               start=False, stop=True)
                    ins.then_inc(pb_full, 1)

            def chunk(pos):
                c = pos.first
                if C_WO <= c < C_FF:
                    hi, lo = m_hi, m_lo
                elif c >= C_FF and group_slot(c) >= 4:
                    hi, lo = u_hi, u_lo
                else:
                    hi, lo = h_hi, h_lo
                if c == C_FF:
                    transpose_h(1, 0)
                    transpose_h(1, 1)
                for p in range(PIECES):
                    side(pos, p)
                    if p == 0:
                        sums_read(pos)
                    pe.wait_ge(lo_ready, PIECES * pos.n + (p + 1))
                    if c == C_FF:
                        pe.wait_ge(h_lo_ready, 2 * GROUPS + p + 1)
                    if C_WO <= c < C_FF and p % 2 == 0:
                        pe.wait_ge(pa_read, PA_AT[C_GD + 1 + p // 2] + 1)
                    if c >= C_FF and group_slot(c) == 4 and p % 2 == 0:
                        pe.wait_ge(pa_read, pos.at(PA_AT) + (p // 2 - 2))
                    products(c, p, p % RING, W, hi, lo)

            def products(c, p, s, n, hi, lo):
                for a in range(PK):
                    k = p * PK + a
                    for t in range(T):
                        to = acc[:, c % 2, t, 0:n]
                        x_hi, x_lo = hi[:, k, t * P:(t + 1) * P], lo[:, k, t * P:(t + 1) * P]
                        nc.tensor.matmul(to, x_hi, w_hi[:, s, a, 0:n], start=(k == 0), stop=False)
                        nc.tensor.matmul(to, x_hi, w_lo[:, s, a, 0:n], start=False, stop=False)
                        ins = nc.tensor.matmul(to, x_lo, w_hi[:, s, a, 0:n], start=False, stop=(k == KT - 1))
                ins.then_inc(pe_used, 1)

            pe.wait_ge(consts_landed, 16 * 11)
            nc.tensor.transpose(pa[:, 0, 0:P], vec_rows[:, :], ident[:, :])
            nc.tensor.transpose(pa[:, 1, 0:8], gate_rows[:, :], ident[0:8, 0:8]).then_inc(pa_full, 1)
            nc.tensor.matmul(pb[0:H_DSA, 0, 0:KEYS], table[:, :], onehot[:, :], start=True, stop=True).then_inc(pb_full, 1)
            pe.wait_ge(ones_ready, 1)
            for g in range(GROUPS):
                if g:
                    transpose_h(0, g)
                first_mod(2 * g)
                if g == 0:
                    transpose_h(0, g)
                first_mod(2 * g + 1)
                for s in range(RING):
                    pe.wait_ge(lo_ready, g * RING + s + 1)
                    pe.wait_ge(h_lo_ready, 2 * g + s % 2 + 1)
                    products(s // 2, 2 * g + s % 2, s, width(Pos(JOINT), s), h_hi, h_lo)
            run_plan(pe, chunk)


DSA_STEPS = 6
RES_AT = prefix(lambda c: int(C_WO < c <= C_FF or (c > C_FF and group_slot(c) in (0, 5, 6, 7)) ))
SPLIT_AT = prefix(lambda c: int(C_GD < c <= C_WO or (c > C_FF and 1 <= group_slot(c) <= 4)))
ROOT_STEPS = 5
NORM_STEPS = ROOT_STEPS + 1
ROOT_KV, ROOT_O, ROOT_X = 2, 3, (1, 3 + H_GLA, 4 + H_GLA)
ZF_AT = prefix(lambda c: int(c == 0 or 2 <= c <= 7 or 12 <= c <= C_WO or (c > C_FF and 1 <= group_slot(c) <= 4)))
GATE_AT = prefix(lambda c: (2 - c % 2) if 20 <= c <= 27 else 0, 1)

_INS = ["x", "c", "w_mod", "b_mod", "norm1_g", "w_in", "w_gate_up", "b_gate", "gla_norm_g", "kv_norm_g",
        "w_uv", "w_out", "norm2_g", "w_ff1", "w_ff2", "rel_bias", "final_g"]
_OUTS = [((1, S, D), "float32")]


def kernel(**inputs):
    import numpy as _np
    import concourse.bacc as _bacc
    from concourse import mybir as _mybir
    from concourse.bass_utils import run_bass_kernel_spmd as _run

    nc = _bacc.Bacc("TRN2", target_bir_lowering=False, num_devices=1)
    arrays, args = {}, []
    for name in _INS:
        a = _np.ascontiguousarray(inputs[name])
        arrays[f"in_{name}_dram"] = a
        args.append(nc.dram_tensor(f"in_{name}_dram", a.shape, _mybir.dt.from_np(a.dtype), kind="ExternalInput").ap())
    for i, (shape, dtype) in enumerate(_OUTS):
        dt = _mybir.dt.from_np(_np.dtype(dtype))
        args.append(nc.dram_tensor(f"out_{i}_dram", shape, dt, kind="ExternalOutput").ap())
    build_layer(nc, *args)
    r = _run(nc, [arrays], core_ids=[0])
    got = tuple(r.results[0][f"out_{i}_dram"] for i in range(len(_OUTS)))
    return got[0]
```
